# Optimizing a Trainium2 kernel written in Bass

```python
import math
import jax, jax.numpy as jnp
from jax import lax
import numpy as np

D_MODEL = 2048
BATCH = 1
SEQ = 512
DEPTH = 1
DEC_BATCH = 8
DEC_SEQ = 8
PAST_LEN = 4096
PAGE_SIZE = 128

CONV_DIM = D_MODEL
CONV_WIDTH = 3
GLA_HEADS = 4
GLA_DK_TOT = D_MODEL // 2
GLA_DV_TOT = D_MODEL
GLA_DK = GLA_DK_TOT // GLA_HEADS
GLA_DV = GLA_DV_TOT // GLA_HEADS
GLA_RANK = 16
GLA_TAU = 16.0
GLA_CHUNK = 64
NORM_EPS = 1e-6
SPLITS = (D_MODEL, D_MODEL, CONV_DIM, CONV_DIM, CONV_DIM, CONV_DIM,
          GLA_DK_TOT, GLA_DK_TOT, GLA_DV_TOT, GLA_DV_TOT, GLA_RANK)
IN_WIDTH = 2 * D_MODEL + 4 * CONV_DIM + 2 * GLA_DK_TOT + 2 * GLA_DV_TOT + GLA_RANK

kernel_name = "hybrid_shortconv_gla_step"

def rmsnorm(x, g):
    x32 = x.astype(jnp.float32)
    y = x32 * lax.rsqrt(jnp.mean(x32 * x32, axis=-1, keepdims=True) + NORM_EPS)
    return (y * g.astype(jnp.float32)).astype(x.dtype)

def gla_chunked(q, k, v, log_a, s0):
    B, L, H, K = q.shape
    V = v.shape[-1]
    c = math.gcd(L, GLA_CHUNK)
    n = L // c

    def blocks(t):
        return jnp.moveaxis(t.astype(jnp.float32).reshape(B, n, c, H, t.shape[-1]), 1, 0)

    mask = jnp.tril(jnp.ones((c, c), dtype=bool))[None, :, :, None, None]

    def step(S, inp):
        qc, kc, vc, ac = inp
        b = jnp.cumsum(ac, axis=1)
        diff = b[:, :, None] - b[:, None, :]
        decay = jnp.exp(jnp.where(mask, diff, -jnp.inf))
        scores = jnp.sum(qc[:, :, None] * kc[:, None, :] * decay, axis=-1)
        o_intra = jnp.einsum('btsh,bshv->bthv', scores, vc)
        o_inter = jnp.einsum('bthk,bhkv->bthv', qc * jnp.exp(b), S)
        b_last = b[:, -1]
        k_dec = kc * jnp.exp(b_last[:, None] - b)
        S_new = jnp.exp(b_last)[..., None] * S + jnp.einsum('bshk,bshv->bhkv', k_dec, vc)
        return S_new, o_intra + o_inter

    S_fin, o = lax.scan(step, s0.astype(jnp.float32), (blocks(q), blocks(k), blocks(v), blocks(log_a)))
    o = jnp.moveaxis(o, 0, 1).reshape(B, L, H, V)
    return o, S_fin

def mixer_layer(x, conv_buf, gla_state, norm_g, w_in, conv_w, w_alpha2, b_alpha,
                gla_norm_g, w_branch_a, w_branch_b, w_out):
    B, L, _ = x.shape
    h = rmsnorm(x, norm_g)
    proj = jnp.einsum('bld,dp->blp', h, w_in)
    idx = np.cumsum(SPLITS)[:-1].tolist()
    ga, gb, cB, cC, cx, cg, q, k, v, gg, lr = jnp.split(proj, idx, axis=-1)

    u = cC * cx
    u_pad = jnp.concatenate([conv_buf.astype(u.dtype), u], axis=1)
    conv = u_pad[:, 0:L] * conv_w[0]
    for j in range(1, CONV_WIDTH):
        conv = conv + u_pad[:, j:j + L] * conv_w[j]
    za = cB * conv * jax.nn.silu(cg)
    branch_a = jnp.einsum('blc,cd->bld', za, w_branch_a)
    new_buf = u_pad[:, L:]

    qh = q.reshape(B, L, GLA_HEADS, GLA_DK) * (GLA_DK ** -0.5)
    kh = k.reshape(B, L, GLA_HEADS, GLA_DK)
    vh = v.reshape(B, L, GLA_HEADS, GLA_DV)
    a_logit = (jnp.einsum('blr,rk->blk', lr, w_alpha2) + b_alpha).astype(jnp.float32)
    log_a = (jax.nn.log_sigmoid(a_logit) / GLA_TAU).reshape(B, L, GLA_HEADS, GLA_DK)
    o, S_new = gla_chunked(qh, kh, vh, log_a, gla_state)
    o = rmsnorm(o, gla_norm_g).astype(x.dtype)
    zb = o.reshape(B, L, GLA_DV_TOT) * jax.nn.silu(gg)
    branch_b = jnp.einsum('blv,vd->bld', zb, w_branch_b)

    merged = jax.nn.sigmoid(ga) * branch_a + jax.nn.sigmoid(gb) * branch_b
    x = x + jnp.einsum('bld,de->ble', merged, w_out)
    return x, new_buf, S_new

def setup_inputs(seed: int = 0) -> dict:
    key = jax.random.key(seed)
    ks = jax.random.split(key, 16)
    f32 = jnp.float32
    x_prompt = jax.random.normal(ks[0], (BATCH, SEQ, D_MODEL), f32)
    x_sample = jax.random.normal(ks[1], (DEC_BATCH, DEC_SEQ, D_MODEL), f32)
    state_conv = jax.random.normal(ks[2], (DEPTH, DEC_BATCH, CONV_WIDTH - 1, CONV_DIM), f32)
    state_gla = 0.5 * jax.random.normal(ks[3], (DEPTH, DEC_BATCH, GLA_HEADS, GLA_DK, GLA_DV), f32)
    norm_g = 1.0 + 0.02 * jax.random.normal(ks[4], (DEPTH, D_MODEL), f32)
    w_in = jax.random.normal(ks[5], (DEPTH, D_MODEL, IN_WIDTH), f32) * D_MODEL ** -0.5
    conv_w = jax.random.normal(ks[6], (DEPTH, CONV_WIDTH, CONV_DIM), f32) * CONV_WIDTH ** -0.5
    w_alpha2 = jax.random.normal(ks[7], (DEPTH, GLA_RANK, GLA_DK_TOT), f32) * GLA_RANK ** -0.5
    b_alpha = 0.01 * jax.random.normal(ks[8], (DEPTH, GLA_DK_TOT), f32)
    gla_norm_g = 1.0 + 0.02 * jax.random.normal(ks[9], (DEPTH, GLA_DV), f32)
    w_branch_a = jax.random.normal(ks[10], (DEPTH, CONV_DIM, D_MODEL), f32) * CONV_DIM ** -0.5
    w_branch_b = jax.random.normal(ks[11], (DEPTH, GLA_DV_TOT, D_MODEL), f32) * GLA_DV_TOT ** -0.5
    w_out = jax.random.normal(ks[12], (DEPTH, D_MODEL, D_MODEL), f32) * D_MODEL ** -0.5
    final_norm_g = 1.0 + 0.02 * jax.random.normal(ks[13], (D_MODEL,), f32)
    return {"x_prompt": x_prompt, "x_sample": x_sample, "state_conv": state_conv,
            "state_gla": state_gla, "norm_g": norm_g, "w_in": w_in, "conv_w": conv_w,
            "w_alpha2": w_alpha2, "b_alpha": b_alpha, "gla_norm_g": gla_norm_g,
            "w_branch_a": w_branch_a, "w_branch_b": w_branch_b, "w_out": w_out,
            "final_norm_g": final_norm_g}

def reference(x_prompt, x_sample, state_conv, state_gla, norm_g, w_in, conv_w, w_alpha2,
              b_alpha, gla_norm_g, w_branch_a, w_branch_b, w_out, final_norm_g):
    xp = x_prompt
    xs = x_sample
    Bp = x_prompt.shape[0]
    conv_p, gla_p, conv_s, gla_s = [], [], [], []
    for l in range(DEPTH):
        params = (norm_g[l], w_in[l], conv_w[l], w_alpha2[l], b_alpha[l], gla_norm_g[l],
                  w_branch_a[l], w_branch_b[l], w_out[l])
        buf0 = jnp.zeros((Bp, CONV_WIDTH - 1, CONV_DIM), xp.dtype)
        s0 = jnp.zeros((Bp, GLA_HEADS, GLA_DK, GLA_DV), jnp.float32)
        xp, bp, sp = mixer_layer(xp, buf0, s0, *params)
        xs, bs, ss = mixer_layer(xs, state_conv[l], state_gla[l], *params)
        conv_p.append(bp)
        gla_p.append(sp)
        conv_s.append(bs)
        gla_s.append(ss)
    y_prompt = rmsnorm(xp, final_norm_g)
    y_sample = rmsnorm(xs, final_norm_g)
    return (y_prompt, y_sample, jnp.stack(conv_p), jnp.stack(gla_p), jnp.stack(conv_s), jnp.stack(gla_s))


_drawn_inputs = setup_inputs


def setup_inputs(seed=0):
    import zlib

    import numpy as np

    out = dict(_drawn_inputs(seed))
    spreads = {}
    factors = {'b_alpha': 8.0, 'gla_norm_g': 8.0, 'final_norm_g': 2.773}
    for name, (base, spread) in spreads.items():
        noise = np.random.default_rng([zlib.crc32(name.encode()), seed]).standard_normal(out[name].shape)
        drawn = base * np.exp(spread * noise) if base else spread * noise
        out[name] = __import__('jax').numpy.asarray(drawn.astype(out[name].dtype))
    for name, factor in factors.items():
        out[name] = (out[name] * factor).astype(out[name].dtype)
    return out
```

```python
from contextlib import ExitStack

import concourse.bass as bass
from concourse import mybir

ALU = mybir.AluOpType
ACT = mybir.ActivationFunctionType
AX_X = mybir.AxisListType.X
F32 = mybir.dt.float32
F32R = mybir.dt.float32r
U8 = mybir.dt.uint8

P = 128
EPS = 1e-6
TAU = 16.0

LEVELS = [64, 32, 16, 8, 4, 2, 1]
NLEVEL = len(LEVELS) + 1

STEPS = (["q"] * 2 + ["k"] * 2 + ["v"] * 4 + ["conv_c", "conv_x", "conv_b", "conv_g"] * 4
         + ["gla_gate"] * 4 + ["gate_a"] * 4 + ["gate_b"] * 4)
NSTEP = len(STEPS)
LAST_READER = {"q": "act", "k": "act", "conv_c": "act", "gate_a": "act", "gate_b": "act",
               "conv_x": "dve", "conv_b": "dve", "conv_g": "dve", "gla_gate": "dve"}


def hybrid_kernel(nc, x_prompt, x_sample, state_conv, state_gla, norm_g, w_in, conv_w, w_alpha2,
                  b_alpha, gla_norm_g, w_branch_a, w_branch_b, w_out, final_norm_g,
                  const_f32,
                  y_prompt, y_sample, new_conv_prompt, new_gla_prompt, new_conv_sample, new_gla_sample):
    D = x_prompt.shape[2]
    TP = x_prompt.shape[1]
    NS, LS = x_sample.shape[0], x_sample.shape[1]
    TS = NS * LS
    T = TP + TS
    H, DK, DV = state_gla.shape[2:]
    RANK = w_alpha2.shape[1]
    KT = D // P
    NT = TP // P
    KK, VV = DK // P, DV // P
    CH = KT // H
    UNIT = KT * P
    KQ = 4
    HALF = T // 2
    LAST = T - P
    S0 = P - TS
    NB = NT + NS
    assert (KT, NT, KK, VV, CH, TS, RANK) == (16, 4, 2, 4, 4, 64, 16)
    c_ga, c_gb, c_cb, c_cc, c_cx, c_cg = (n * D for n in range(6))
    c_q = 6 * D
    c_k = c_q + H * DK
    c_v = c_k + H * DK
    c_gg = c_v + H * DV
    c_lr = c_gg + H * DV

    w_in_k = w_in[0].rearrange("(k p) c -> p k c", p=P)
    w_a_k = w_branch_a[0].rearrange("(k p) c -> p k c", p=P)
    w_b_k = w_branch_b[0].rearrange("(k p) c -> p k c", p=P)
    w_o_k = w_out[0].rearrange("(k p) c -> p k c", p=P)
    xs_rows = x_sample.rearrange("s t d -> (s t) d")
    ys_rows = y_sample.rearrange("s t d -> (s t) d")

    za_d = nc.dram_tensor("za_d", [KT, P, 2, T], F32R, kind="Internal").ap()
    zb_d = nc.dram_tensor("zb_d", [KT, P, 2, T], F32R, kind="Internal").ap()
    gate_d = nc.dram_tensor("gate_d", [2, KT, P, T], F32, kind="Internal").ap()
    ma_d = nc.dram_tensor("ma_d", [KT, P, T], F32, kind="Internal").ap()

    ctx = ExitStack()
    with ctx:
        arena_bytes = nc.sbuf_usable_end - nc.sbuf_base - 64
        arena_bytes -= arena_bytes % 32
        base = (nc.sbuf_base + 31) // 32 * 32
        ctx.enter_context(nc.sbuf_tensor("arena", [P, arena_bytes // 4], F32))
        size = {F32: 4, F32R: 4, U8: 1}
        cursor = {"at": base}

        def put(name, shape, dt):
            t = nc.alloc_sbuf_tensor_at(name, shape, dt, offset=cursor["at"])
            n = size[dt]
            for s in shape[1:]:
                n *= s
            cursor["at"] += (n + 31) // 32 * 32
            return t

        raw = [put(f"raw{n}", [P, UNIT], F32) for n in range(2)]
        w_hi = [put(f"w_hi{n}", [P, UNIT], F32R) for n in range(2)]
        w_lo = [put(f"w_lo{n}", [P, UNIT], F32R) for n in range(2)]
        ident = put("ident", [P, P], F32)
        gate_tile = put("gate_tile", [P, 2, T], F32)
        mix_tile = put("mix_tile", [P, 2, T], F32)
        stat = put("stat", [P, 64], F32)
        eps = put("eps", [P, 1], F32)
        y_at = cursor["at"]
        act_y = put("act_y", [P, KT, 2, T], F32R)
        y_end = cursor["at"]
        g_at = cursor["at"]
        act_x = put("act_x", [P, KT, 2, T], F32R)
        assert cursor["at"] <= base + arena_bytes, cursor["at"] - base - arena_bytes

        cursor["at"] = y_at
        resid = put("resid", [P, NT + 1, D], F32)
        gfin = put("gfin", [P, D], F32)
        assert cursor["at"] <= y_end

        cursor["at"] = g_at
        x_rows = put("x_rows", [P, NT + 1, D], F32)
        vec_rows = put("vec_rows", [P, P], F32)
        conv_rows = put("conv_rows", [2 * NS, D], F32)
        staging_end = cursor["at"]

        cursor["at"] = g_at
        qk = put("qk", [P, 2, KK, T], F32)
        o_t = nc.alloc_sbuf_tensor_at("o_t", [P, VV, T], F32, offset=g_at)
        cum = put("cum", [P, KK, T], F32)
        dec = put("dec", [P, KK, T], F32)
        qe = put("qe", [P, KK, T], F32)
        v_rows = put("v_rows", [P, NT + 1, DV], F32)
        scores = put("scores", [P, T], F32)
        kd_rows = put("kd_rows", [P, NT + 1, DK], F32)
        kd_seq = put("kd_seq", [P, 2, DK], F32)
        states = put("states", [P, 2, KK, DV], F32)
        s_prompt = put("s_prompt", [P, KK, DV], F32)
        z_tile = put("z_tile", [P, 2, T], F32R)
        u_tile = put("u_tile", [P, TP + 2 + NS * (LS + 2)], F32)
        ssq = put("ssq", [P, P], F32)
        rstd = put("rstd", [P, P], F32)
        decay_end = put("decay_end", [P, KK, NB], F32)
        w2h = put("w2h", [RANK, DK], F32)
        conv_tail = put("conv_tail", [P, CH, 2 * NS + 2], F32)
        cursor["at"] = max(cursor["at"], staging_end)
        lr_t = put("lr_t", [P, T], F32)
        cvec = put("cvec", [P, 76], F32)
        conv_state = put("conv_state", [P, KT, 2 * NS], F32)
        masks = put("masks", [P, NLEVEL, P], U8)
        reset = put("reset", [P, T], F32)
        seq_sel = put("seq_sel", [P, NS], F32)
        mean_w = put("mean_w", [P, P], F32)
        print("workspace", cursor["at"] - g_at, "of", KT * 2 * T * 4)
        assert cursor["at"] <= g_at + KT * 2 * T * 4

        acc = [ctx.enter_context(nc.psum_tensor(f"acc{n}", [P, 1024], F32)) for n in range(2)]
        bank = ctx.enter_context(nc.psum_tensor("bank", [P, 4, 512], F32))
        A0 = 512 - HALF

        cbal, cconv, cgla = KT, KT + 8, KT + 8 + 3 * KT

        S = {}

        def sem(name):
            S[name] = ctx.enter_context(nc.semaphore(name))
            return S[name]

        const_in = sem("const_in")
        x_in = [sem(f"x_in{n}") for n in range(NT + 1)]
        raw_in = [sem(f"raw_in{n}") for n in range(2)]
        lr_zero = sem("lr_zero")
        hi_ready, lo_ready, unit_done = sem("hi_ready"), sem("lo_ready"), sem("unit_done")
        act_freed, dve_freed = sem("act_freed"), sem("dve_freed")
        act_self, dve_self, passed = sem("act_self"), sem("dve_self"), sem("passed")
        sq_done, ms_ready, rms_in, x_scaled, vec_t, vec_ready, cst_t, cst_ready = (
            sem(n) for n in ("sq_done", "ms_ready", "rms_in", "x_scaled", "vec_t", "vec_ready", "cst_t", "cst_ready"))
        xt_done, h_hi, h_lo = sem("xt_done"), sem("h_hi"), sem("h_lo")
        w2_in, logits, abs_done, neg_part, soft_part, cum_ready = (
            sem(n) for n in ("w2_in", "logits", "abs_done", "neg_part", "soft_part", "cum_ready"))
        eb_ready, qe_ready, kd_diff, kd_exp, kd_ready, kd_turned, kd_saved = (
            sem(n) for n in ("eb_ready", "qe_ready", "kd_diff", "kd_exp", "kd_ready", "kd_turned", "kd_saved"))
        lvl_diff, lvl_exp, lvl_ready, gram_done, lvl_merged = (
            sem(n) for n in ("lvl_diff", "lvl_exp", "lvl_ready", "gram_done", "lvl_merged"))
        v_act, v_dve = sem("v_act"), sem("v_dve")
        seq_kd, seq_mm, seq_upd = sem("seq_kd"), sem("seq_mm"), sem("seq_upd")
        st_in = [sem(f"st_in{n}") for n in range(2)]
        st_out = [sem(f"st_out{n}") for n in range(2)]
        inter_saved, chunk_mm, chunk_sq, chunk_state, sp_out = (
            sem(n) for n in ("inter_saved", "chunk_mm", "chunk_sq", "chunk_state", "sp_out"))
        ssq_ready, mean_mm, rms_ready, o_ready = sem("ssq_ready"), sem("mean_mm"), sem("rms_ready"), sem("o_ready")
        cg_sig, z_f32, z_hi, z_out = (
            sem(n) for n in ("cg_sig", "z_f32", "z_hi", "z_out"))
        tail_ready, tail_turned, tail_saved, tail_out = (
            sem(n) for n in ("tail_ready", "tail_turned", "tail_saved", "tail_out"))
        gate_out = [sem(f"gate_out{n}") for n in range(2)]
        xa_in, yb_in = sem("xa_in"), sem("yb_in")
        gate_in = [sem(f"gate_in{n}") for n in range(2)]
        ma_out = [sem(f"ma_out{n}") for n in range(2)]
        ma_in = [sem(f"ma_in{n}") for n in range(2)]
        mix_sum, mix_hi, mix_lo = sem("mix_sum"), sem("mix_hi"), sem("mix_lo")
        resid_in, out_sum, mean_sq, rms_out, y_ready, y_out = (
            sem(n) for n in ("resid_in", "out_sum", "mean_sq", "rms_out", "y_ready", "y_out"))

        START = 1

        block = ctx.enter_context(nc.Block())

        U_BODY = 1
        U_A = U_BODY + H * NSTEP
        U_B = U_A + KT
        U_O = U_B + KT
        U_END = U_O + KT
        act_upto = [sum(LAST_READER.get(k) == "act" for k in STEPS[:s + 1]) for s in range(NSTEP)]
        dve_upto = [sum(LAST_READER.get(k) == "dve" for k in STEPS[:s + 1]) for s in range(NSTEP)]
        ACT_PER, DVE_PER = act_upto[-1], dve_upto[-1]
        ACT0 = 1

        def wait_turn(eng, s, value):
            eng.wait_ge(s, value)
            eng.sem_inc(passed, 1)

        def load_unit(sp, u, src, par):
            if not isinstance(u, int) or u >= 2:
                wait_turn(sp, lo_ready, u - 1 + START)
            k, c = src.shape[1], src.shape[2]
            sp.dma_start(raw[par][:, :].rearrange("p (k c) -> p k c", k=k), src).then_inc(raw_in[par], 16)

        def round_hi(act, u, par, turns):
            act.wait_ge(raw_in[par], 16 * turns)
            if not isinstance(u, int) or u >= 2:
                act.wait_ge(unit_done, u - 1 + START)
            nc.scalar.activation(w_hi[par][:, :], raw[par][:, :], ACT.Copy).then_inc(hi_ready, 1)

        def subtract_lo(dve, u, par):
            dve.wait_ge(hi_ready, u + 1)
            nc.vector.tensor_tensor(w_lo[par][:, :], raw[par][:, :], w_hi[par][:, :].bitcast(F32),
                                    ALU.subtract).then_inc(lo_ready, 1)

        PASSES = ((0, 0), (0, 1), (1, 0))

        def channel_unit(pe, u, par, x):
            pe.wait_ge(lo_ready, u + 1 + START)
            out = acc[par]
            for k in range(KT):
                for n, (a, b) in enumerate(PASSES):
                    w = (w_hi, w_lo)[a][par][:, k * P:(k + 1) * P]
                    for j in range(2):
                        mm = nc.tensor.matmul(out[:, A0 + j * HALF:A0 + (j + 1) * HALF], w,
                                              x[:, k, b, j * HALF:(j + 1) * HALF],
                                              start=(k == 0 and n == 0), stop=(k == KT - 1 and n == 2))
            mm.then_inc(unit_done, 1)

        def token_unit(pe, u, par, q, x, slot, before_first=(), before_last=()):
            pe.wait_ge(lo_ready, u + 1 + START)
            for s, n in before_first:
                pe.wait_ge(s, n)
            for kk in range(KQ):
                k = q * KQ + kk
                for t in range(NT + 1):
                    if t == NT and kk == 0:
                        for s, n in before_last:
                            pe.wait_ge(s, n)
                    out = bank[:, t, :] if t < NT else acc[slot][:, 0:512]
                    t0 = t * P if t < NT else LAST
                    for n, (a, b) in enumerate(PASSES):
                        mm = nc.tensor.matmul(out, x[:, k, b, t0:t0 + P],
                                              (w_hi, w_lo)[a][par][:, kk * 512:(kk + 1) * 512],
                                              start=(k == 0 and n == 0), stop=(k == KT - 1 and n == 2))
            mm.then_inc(unit_done, 1)

        def par_of(s):
            return (U_BODY + s) % 2

        def turns_of(i, u_lit, per):
            return (per // 2) * i + (u_lit // 2 + 1)

        @block.sync
        def _(sp):
            for t in range(NT):
                sp.dma_start(x_rows[:, t, :], x_prompt[0, t * P:(t + 1) * P, :]).then_inc(x_in[t], 16)
            sp.dma_start(x_rows[0:TS, NT, :], xs_rows).then_inc(x_in[NT], 16)
            sp.wait_ge(lr_zero, 1)
            sp.dma_start(raw[0][:, :].rearrange("p (k c) -> p k c", k=KT)[:, :, 0:RANK],
                         w_in_k[:, :, c_lr:c_lr + RANK]).then_inc(raw_in[0], 16)

            def step_src(i, s):
                kind = STEPS[s]
                n = s - STEPS.index(kind)
                if kind in ("q", "k"):
                    c = (c_q if kind == "q" else c_k) + n * P + i * DK
                    return w_in_k[:, :, bass.ds(c, P)]
                if kind == "v":
                    return w_in_k[:, n * KQ:(n + 1) * KQ, bass.ds(i * DV + c_v, DV)]
                if kind.startswith("conv"):
                    n //= 4
                c0 = {"conv_c": c_cc, "conv_x": c_cx, "conv_b": c_cb, "conv_g": c_cg,
                      "gla_gate": c_gg, "gate_a": c_ga, "gate_b": c_gb}[kind]
                return w_in_k[:, :, bass.ds(i * (CH * P) + (c0 + n * P), P)]

            with sp.Fori(0, H) as i:
                for s in range(NSTEP):
                    load_unit(sp, i * NSTEP + (U_BODY + s), step_src(i, s), par_of(s))
            for u0, w in ((U_A, w_a_k), (U_B, w_b_k)):
                with sp.Fori(0, KT // 2) as i:
                    for n in range(2):
                        load_unit(sp, i * 2 + (u0 + n), w[:, :, bass.ds(i * (2 * P) + n * P, P)], (u0 + n) % 2)
            with sp.Fori(0, KT // KQ) as i:
                for q in range(4):
                    load_unit(sp, i * 4 + (U_O + q), w_o_k[:, q * KQ:(q + 1) * KQ, bass.ds(i * 512, 512)],
                              (U_O + q) % 2)

        @block.gpsimd
        def _(pool):
            nc.gpsimd.memset(raw[0][:, :], 0.0).then_inc(lr_zero, 1)
            pool.dma_start(ident[:, :], const_f32[:, 0:P]).then_inc(const_in, 16)
            pool.dma_start(vec_rows[0:KT, :], norm_g[0].rearrange("(k p) -> k p", p=P)).then_inc(const_in, 16)
            pool.dma_start(vec_rows[cbal:cbal + 8, :], b_alpha[0].rearrange("(k p) -> k p", p=P)).then_inc(const_in, 16)
            pool.dma_start(vec_rows[cconv:cconv + 3 * KT, :],
                           conv_w[0].rearrange("j (k p) -> (j k) p", p=P)).then_inc(const_in, 16)
            pool.dma_start(vec_rows[cgla:cgla + VV, :],
                           gla_norm_g[0].rearrange("(k p) -> k p", p=P)).then_inc(const_in, 16)
            pool.dma_start(conv_rows[:, :], state_conv[0].rearrange("s r d -> (s r) d")).then_inc(const_in, 16)
            pool.dma_start(reset[:, :], const_f32[:, P:P + T]).then_inc(const_in, 16)
            pool.dma_start(seq_sel[:, :], const_f32[:, P + T:P + T + NS]).then_inc(const_in, 16)
            mask_stage = mix_tile[:, :, :].rearrange("p a t -> p (a t)")[:, 0:NLEVEL * P]
            pool.dma_start(mask_stage, const_f32[:, P + T + NS:P + T + NS + NLEVEL * P]).then_inc(const_in, 16)
            pool.wait_ge(const_in, 16 * 9)
            pool.wait_ge(xt_done, KT)
            with pool.Fori(0, H) as i:
                pool.dma_start(w2h[:, :], w_alpha2[0, :, bass.ds(i * DK, DK)]).then_inc(w2_in, 16)

                def load_state(j):
                    if j >= 2:
                        wait_turn(pool, st_out[j % 2], i * (8 * NS) + 16 * (j // 2))
                    pool.dma_start(states[:, j % 2, :, :],
                                   state_gla[0, j, bass.ds(i, 1), :, :].rearrange("h (k p) v -> p (h k) v", p=P)
                                   ).then_inc(st_in[j % 2], 16)

                def wait_z(m):
                    step = STEPS.index("conv_g") + 4 * m if m < 4 else STEPS.index("gla_gate") + m - 4
                    wait_turn(pool, dve_freed, i * DVE_PER + dve_upto[step] + START)

                load_state(0)
                load_state(1)
                for j in range(NS):
                    wait_turn(pool, seq_upd, i * NS + (j + 1))
                    pool.dma_start(new_gla_sample[0, j, bass.ds(i, 1), :, :].rearrange("h (k p) v -> p (h k) v", p=P),
                                   states[:, j % 2, :, :]).then_inc(st_out[j % 2], 16)
                    if j + 2 < NS:
                        load_state(j + 2)
                    if j in (2, 6):
                        n = j // 4
                        wait_z(n)
                        pool.dma_start(za_d[bass.ds(i * CH + n, 1)].rearrange("k p h t -> p (k h) t"),
                                       z_tile[:, :, :]).then_inc(z_out, 16)
                for n in (2, 3):
                    wait_z(n)
                    pool.dma_start(za_d[bass.ds(i * CH + n, 1)].rearrange("k p h t -> p (k h) t"),
                                   z_tile[:, :, :]).then_inc(z_out, 16)
                    if n == 2:
                        wait_turn(pool, chunk_state, i * NT + NT)
                        pool.dma_start(new_gla_prompt[0, 0, bass.ds(i, 1), :, :].rearrange("h (k p) v -> p (h k) v", p=P),
                                       s_prompt[:, :, :]).then_inc(sp_out, 16)
                for n in range(4):
                    wait_z(4 + n)
                    pool.dma_start(zb_d[bass.ds(i * CH + n, 1)].rearrange("k p h t -> p (k h) t"),
                                   z_tile[:, :, :]).then_inc(z_out, 16)
                    if n == 0:
                        wait_turn(pool, tail_saved, i + 1)
                        pool.dma_start(new_conv_prompt[0, 0, :, bass.ds(i * (CH * P), CH * P)],
                                       mix_tile[0:2, 0, 0:CH * P]).then_inc(tail_out, 16)
                        pool.dma_start(new_conv_sample[0, :, :, bass.ds(i * (CH * P), CH * P)].rearrange("s r d -> (s r) d"),
                                       mix_tile[2:2 + 2 * NS, 0, 0:CH * P]).then_inc(tail_out, 16)
                for n in range(8):
                    wait_turn(pool, act_freed, i * ACT_PER + (ACT0 + act_upto[STEPS.index("gate_a") + n]) + START)
                    pool.dma_start(gate_d[n // 4, bass.ds(i * CH + n % 4, 1)].rearrange("k p t -> p (k t)"),
                                   gate_tile[:, n % 2, :]).then_inc(gate_out[n % 2], 16)
                    if n == 0:
                        wait_turn(pool, z_out, i * 128 + 128)
                        wait_turn(pool, sp_out, i * 16 + 16)
                        wait_turn(pool, tail_out, i * 32 + 32)
                        wait_turn(pool, st_out[0], i * (8 * NS) + 8 * NS)
                        wait_turn(pool, st_out[1], i * (8 * NS) + 8 * NS)
                wait_turn(pool, gate_out[0], i * 64 + 64)
                wait_turn(pool, gate_out[1], i * 64 + 64)
            pool.dma_start(act_x[:, :, :, :].rearrange("p k h t -> p k (h t)"),
                           za_d.rearrange("k p h t -> p k (h t)")).then_inc(xa_in, 16)
            pool.wait_ge(unit_done, U_A + START)
            pool.dma_start(act_y[:, :, :, :].rearrange("p k h t -> p k (h t)"),
                           zb_d.rearrange("k p h t -> p k (h t)")).then_inc(yb_in, 16)
            for n in range(2):
                pool.dma_start(gate_tile[:, n, :], gate_d[0, n]).then_inc(gate_in[n], 16)
            with pool.Fori(0, KT // 2) as i:
                for n in range(2):
                    wait_turn(pool, dve_freed, i * 2 + (H * DVE_PER + n + 1) + START)
                    pool.dma_start(ma_d[bass.ds(i * 2 + n, 1)].rearrange("k p t -> p (k t)"),
                                   mix_tile[:, n, :]).then_inc(ma_out[n], 16)
                    wait_turn(pool, ma_out[n], i * 16 + 16)
                    pool.dma_start(gate_tile[:, n, :],
                                   gate_d.rearrange("g k p t -> (g k) p t")[bass.ds(i * 2 + (n + 2), 1)]
                                   .rearrange("k p t -> p (k t)")).then_inc(gate_in[n], 16)
            for n in range(2):
                pool.wait_ge(ma_out[n], 16 * (KT // 2))
                pool.dma_start(mix_tile[:, n, :], ma_d[n]).then_inc(ma_in[n], 16)

            def next_b(i, n):
                wait_turn(pool, mix_lo, i * 2 + (n + 1))
                pool.dma_start(mix_tile[:, n, :], ma_d[bass.ds(i * 2 + (n + 2), 1)].rearrange("k p t -> p (k t)")
                               ).then_inc(ma_in[n], 16)
                pool.dma_start(gate_tile[:, n, :], gate_d[1, bass.ds(i * 2 + (n + 2), 1)].rearrange("k p t -> p (k t)")
                               ).then_inc(gate_in[n], 16)

            with pool.Fori(0, KT // 2 - 1) as i:
                for n in range(2):
                    next_b(i, n)
            pool.wait_ge(unit_done, U_O + START)
            for t in range(NT):
                pool.dma_start(resid[:, t, :], x_prompt[0, t * P:(t + 1) * P, :]).then_inc(resid_in, 16)
            pool.dma_start(resid[S0:P, NT, :], xs_rows).then_inc(resid_in, 16)
            pool.dma_start(gfin[:, :], final_norm_g.partition_broadcast(P)).then_inc(resid_in, 16)
            for t in range(NT + 1):
                pool.wait_ge(y_ready, t + 1)
                if t < NT:
                    pool.dma_start(y_prompt[0, t * P:(t + 1) * P, :], resid[:, t, :]).then_inc(y_out, 16)
                else:
                    pool.dma_start(ys_rows, resid[S0:P, NT, :]).then_inc(y_out, 16)
            pool.wait_ge(y_out, 16 * (NT + 1))

        def prompt_blocks(t, n):
            return t[:, :, 0:TP].rearrange("p k (c n) -> p k c n", n=n)

        def sample_blocks(t, n):
            return t[:, :, TP:T].rearrange("p k (c n) -> p k c n", n=n)

        @block.scalar
        def _(act):
            A = nc.scalar.activation
            act.sem_inc(act_freed, START)
            for t in range(NT + 1):
                act.wait_ge(x_in[t], 16)
                n = P if t < NT else TS
                if t:
                    act.wait_ge(sq_done, t)
                A(bank[0:n, :, :].rearrange("p b c -> p (b c)"), x_rows[0:n, t, :], ACT.Square,
                  accum_out=stat[0:n, t:t + 1]).then_inc(sq_done, 1)
                act.wait_ge(ms_ready, t + 1)
                A(stat[0:n, 16 + t:17 + t], stat[0:n, 8 + t:9 + t], ACT.Sqrt).then_inc(rms_in, 1)
            for k in range(KT):
                act.wait_ge(xt_done, k + 1)
                if k == 0:
                    act.wait_ge(vec_ready, 1)
                A(act_y[:, k, 0, :], acc[k % 2][:, 0:T], ACT.Copy, scale=cvec[:, k:k + 1]).then_inc(h_hi, 1)
            round_hi(act, 0, 0, 1)
            act.wait_ge(unit_done, 1 + START)
            round_hi(act, 1, 1, 1)
            A(lr_t[:, :], acc[0][:, A0:A0 + T], ACT.Copy).then_inc(act_freed, 1)

            with act.Fori(0, H) as i:
                for s, kind in enumerate(STEPS):
                    n = s - STEPS.index(kind)
                    u1 = i * NSTEP + (U_BODY + s + 1)
                    round_hi(act, u1, par_of(s + 1), turns_of(i, U_BODY + s + 1, NSTEP))
                    par = par_of(s)
                    out = acc[par][:, A0:A0 + T]
                    if kind != "v" or n == 3:
                        act.wait_ge(unit_done, i * NSTEP + (U_BODY + s + 1) + START)
                    if kind == "q":
                        A(qk[:, 0, n, :], out, ACT.Copy, scale=DK ** -0.5).then_inc(act_freed, 1)
                    if kind == "k":
                        A(qk[:, 1, n, :], out, ACT.Copy).then_inc(act_freed, 1)
                    if kind == "v" and n == 3:
                        A(v_rows[:, 0:2, :], bank[:, 0:2, :], ACT.Copy).then_inc(v_act, 1)
                    if kind in ("conv_c", "conv_g", "gla_gate"):
                        act.wait_ge(dve_freed, i * DVE_PER + dve_upto[s - 1] + START)
                    if kind == "conv_c":
                        A(mix_tile[:, 0, :], out, ACT.Copy).then_inc(act_freed, 1)
                    if kind == "conv_g":
                        A(mix_tile[:, 0, :], out, ACT.Sigmoid).then_inc(cg_sig, 1)
                    if kind == "gla_gate":
                        A(mix_tile[:, 1, :], out, ACT.Sigmoid).then_inc(cg_sig, 1)
                    if kind in ("conv_g", "gla_gate"):
                        m = n // 4 if kind == "conv_g" else 4 + n
                        act.wait_ge(z_f32, i * 8 + (m + 1))
                        if m:
                            act.wait_ge(z_out, i * 128 + 16 * m)
                        A(z_tile[:, 0, :], mix_tile[:, 1, :], ACT.Copy).then_inc(z_hi, 1)
                    if kind in ("gate_a", "gate_b"):
                        m = n if kind == "gate_a" else 4 + n
                        if m >= 2:
                            act.wait_ge(gate_out[m % 2], i * 64 + 16 * (m // 2))
                        else:
                            act.wait_ge(w2_in, i * 16 + 16)
                        A(gate_tile[:, m % 2, :], out, ACT.Sigmoid).then_inc(act_freed, 1)

                    if s == 1:
                        act.wait_ge(logits, i + 1)
                        for kk in range(KK):
                            ap = bank[:, 2 * kk:2 * kk + 2, :].rearrange("p b c -> p (b c)")[:, A0:A0 + T]
                            ins = A(dec[:, kk, :], ap, ACT.Abs, bias=cvec[:, bass.ds(i * KK + (cbal + kk), 1)])
                        ins.then_inc(abs_done, 1)
                        act.wait_ge(abs_done, i + 1)
                        A(dec[:, :, :], dec[:, :, :], ACT.Exp, scale=-1.0).then_inc(act_self, 1)
                        act.wait_ge(act_self, i + 1)
                        A(dec[:, :, :], dec[:, :, :], ACT.Ln, bias=1.0).then_inc(soft_part, 1)
                    if s == 2:
                        act.wait_ge(cum_ready, i + 1)
                        A(decay_end[:, :, 0:NT], prompt_blocks(cum, P)[:, :, :, P - 1], ACT.Exp, scale=1 / TAU)
                        A(decay_end[:, :, NT:NB], sample_blocks(cum, LS)[:, :, :, LS - 1], ACT.Exp, scale=1 / TAU)
                        A(qe[:, :, :], cum[:, :, :], ACT.Exp, scale=1 / TAU).then_inc(eb_ready, 1)
                    if s == 3:
                        act.wait_ge(kd_diff, i + 1)
                        A(dec[:, :, :], dec[:, :, :], ACT.Exp, scale=-1 / TAU).then_inc(kd_exp, 1)
                    if s == 8:
                        act.wait_ge(kd_turned, i + 1)
                        A(kd_rows[:, 0:NT, :], bank[:, 0:2, :], ACT.Copy)
                        A(kd_rows[S0:P, NT, :], bank[S0:P, 2, 0:DK], ACT.Copy).then_inc(kd_saved, 1)
                    if 8 <= s < 8 + len(LEVELS):
                        l = s - 8
                        act.wait_ge(lvl_diff, i * len(LEVELS) + (l + 1))
                        for half, sign in ((0, -1), (1, 1)):
                            B = LEVELS[l]
                            tt = T if 2 * B <= LS else TP
                            ap = dec[:, :, 0:tt].rearrange("p k (c n) -> p k c n", n=2 * B)[
                                :, :, :, half * B:(half + 1) * B]
                            ins = A(ap, ap, ACT.Exp, scale=sign / TAU)
                        ins.then_inc(lvl_exp, 1)
                    if s == 16:
                        act.wait_ge(seq_mm, i * NS + NS)
                        act.wait_ge(lvl_merged, i * NLEVEL + NLEVEL)
                        A(o_t[:, :, TP:T], bank[:, 2, 0:VV * TS].rearrange("p (v t) -> p v t", v=VV),
                          ACT.Copy).then_inc(inter_saved, 1)
                    if 17 <= s < 17 + NT:
                        c = s - 17
                        act.wait_ge(chunk_mm, i * (NT + 1) + (c + 1))
                        ap = bank[:, 2, :].rearrange("p (v t) -> p v t", v=VV)
                        if c:
                            act.wait_ge(ssq_ready, i * (NT + 1) + c)
                        A(dec[:, 0, 0:512].rearrange("p (v t) -> p v t", v=VV), ap, ACT.Square)
                        A(o_t[:, :, c * P:(c + 1) * P], ap, ACT.Copy).then_inc(chunk_sq, 1)
                    if 18 <= s <= 18 + NT:
                        c = s - 18
                        w = P if c < NT else TS
                        act.wait_ge(mean_mm, i * (NT + 1) + (c + 1))
                        A(rstd[:, 0:w], bank[:, 3, 0:w], ACT.Sqrt, bias=eps[:, :]).then_inc(rms_ready, 1)
                    if kind == "gate_b" and n == 0:
                        act.wait_ge(z_out, i * 128 + 128)
                    if s == 24:
                        act.wait_ge(tail_turned, i + 1)
                        A(mix_tile[0:2 * NS + 2, 0, 0:CH * P], bank[0:2 * NS + 2, 0, :], ACT.Copy).then_inc(tail_saved, 1)
            with act.Fori(0, KT // 2) as i:
                for n in range(2):
                    u1 = U_A + n + 1
                    round_hi(act, i * 2 + u1, u1 % 2, turns_of(i, u1, 2))
            with act.Fori(0, KT // 2) as i:
                for n in range(2):
                    u1 = U_B + n + 1
                    round_hi(act, i * 2 + u1, u1 % 2, turns_of(i, u1, 2))
                    act.wait_ge(mix_sum, i * 2 + (n + 1))
                    A(act_x[:, bass.ds(i * 2 + n, 1), 0, :].rearrange("p k t -> p (k t)"), gate_tile[:, n, :],
                      ACT.Copy).then_inc(mix_hi, 1)

            def out_group(i, last):
                for q in range(4):
                    u1 = U_O + q + 1
                    if not (last and q == 3):
                        round_hi(act, i * 4 + u1, u1 % 2, turns_of(i, u1, 4))
                act.wait_ge(out_sum, i * (NT + 1) + (NT + 1) + START)
                for t in range(NT + 1):
                    r0 = 0 if t < NT else S0
                    ins = A(mix_tile[r0:P, 0, 0:512], resid[r0:P, t, bass.ds(i * 512, 512)], ACT.Square,
                            accum_out=stat[r0:P, bass.ds(i * (NT + 1) + t, 1)])
                    ins.then_inc(act_self, 1)
                    act.wait_ge(act_self, i * (NT + 1) + (H + t + 1))

            with act.Fori(0, KT // KQ - 1) as i:
                out_group(i, False)
            out_group(KT // KQ - 1, True)
            for n in range(2):
                act.wait_ge(mean_sq, n + 1)
                r0, t0, t1 = ((0, 0, NT), (S0, NT, NT + 1))[n]
                A(stat[r0:P, 52 + t0:52 + t1], stat[r0:P, 46 + t0:46 + t1], ACT.Sqrt).then_inc(rms_out, 1)

        @block.tensor
        def _(pe):
            pe.sem_inc(unit_done, START)
            pe.wait_ge(const_in, 16 * 9)
            nc.tensor.transpose(acc[0][:, 0:76], vec_rows[0:76, :], ident[0:76, 0:76]).then_inc(vec_t, 1)
            for k in range(KT):
                t = nc.tensor.transpose(acc[1][:, k * 2 * NS:(k + 1) * 2 * NS], conv_rows[:, k * P:(k + 1) * P],
                                        ident[0:2 * NS, 0:2 * NS])
            t.then_inc(cst_t, 1)
            pe.wait_ge(x_scaled, NT + 1)
            for k in range(KT):
                if k == 0:
                    pe.wait_ge(vec_ready, 1)
                elif k == 1:
                    pe.wait_ge(cst_ready, 1)
                else:
                    pe.wait_ge(h_lo, k - 1)
                for t in range(NT + 1):
                    n = P if t < NT else TS
                    tr = nc.tensor.transpose(acc[k % 2][:, t * P:t * P + n], x_rows[0:n, t, k * P:(k + 1) * P],
                                             ident[0:n, 0:n])
                tr.then_inc(xt_done, 1)
            pe.wait_ge(h_lo, KT)
            channel_unit(pe, 0, 0, act_y)

            with pe.Fori(0, H) as i:
                for s, kind in enumerate(STEPS):
                    u, par = i * NSTEP + (U_BODY + s), par_of(s)
                    n = s - STEPS.index(kind)
                    if kind != "v":
                        if s >= 2:
                            k2 = STEPS[s - 2]
                        else:
                            k2 = STEPS[s - 2 + NSTEP]
                        if k2 == "v":
                            if s == 8:
                                pass
                            else:
                                pe.wait_ge(v_act, i + 1)
                                pe.wait_ge(v_dve, i + 1)
                        elif LAST_READER[k2] == "act":
                            c = ACT0 + (act_upto[s - 2] if s >= 2 else act_upto[s - 2 + NSTEP] - ACT_PER)
                            pe.wait_ge(act_freed, i * ACT_PER + c + START)
                        else:
                            c = dve_upto[s - 2] if s >= 2 else dve_upto[s - 2 + NSTEP] - DVE_PER
                            pe.wait_ge(dve_freed, i * DVE_PER + c + START)
                        channel_unit(pe, u, par, act_y)
                    else:
                        first = [(neg_part, i + 1)] if n == 0 else []
                        last = [(act_freed, i * ACT_PER + ACT0 + 4 + START)] if n == 0 else []
                        token_unit(pe, u, par, n, act_y, par_of(7), first, last)

                    if s == 1:
                        pe.wait_ge(w2_in, i * 16 + 16)
                        for kk in range(KK):
                            ap = bank[:, 2 * kk:2 * kk + 2, :].rearrange("p b c -> p (b c)")
                            for j in range(2):
                                mm = nc.tensor.matmul(ap[:, A0 + j * HALF:A0 + (j + 1) * HALF],
                                                      w2h[:, kk * P:(kk + 1) * P],
                                                      lr_t[0:RANK, j * HALF:(j + 1) * HALF], start=True, stop=True)
                        mm.then_inc(logits, 1)
                    if s == 8:
                        pe.wait_ge(kd_ready, i + 1)
                        pe.wait_ge(v_act, i + 1)
                        pe.wait_ge(v_dve, i + 1)
                        for c in range(NT + 1):
                            t0 = c * P if c < NT else LAST
                            for kk in range(KK):
                                o = (c * KK + kk) * P
                                tr = nc.tensor.transpose(bank[:, o // 512, o % 512:o % 512 + P],
                                                         dec[:, kk, t0:t0 + P], ident[:, :])
                        tr.then_inc(kd_turned, 1)
                    if 9 <= s <= 16:
                        l = j = s - 9
                        if l:
                            pe.wait_ge(lvl_merged, i * NLEVEL + l)
                        if j == 0:
                            pe.wait_ge(qe_ready, i + 1)
                            pe.wait_ge(kd_saved, i + 1)
                        pe.wait_ge(st_in[j % 2], i * (8 * NS) + 16 * (j // 2 + 1))
                        pe.wait_ge(seq_kd, i * NS + (j + 1))
                        if j:
                            pe.wait_ge(seq_upd, i * NS + j)
                        for v in range(VV):
                            for kk in range(KK):
                                nc.tensor.matmul(bank[:, 2, v * TS + j * LS:v * TS + (j + 1) * LS],
                                                 states[:, j % 2, kk, v * P:(v + 1) * P],
                                                 qe[:, kk, TP + j * LS:TP + (j + 1) * LS],
                                                 start=(kk == 0), stop=(kk == KK - 1))
                        for kk in range(KK):
                            mm = nc.tensor.matmul(bank[:, kk, :], kd_seq[S0:P, j % 2, kk * P:(kk + 1) * P],
                                                  v_rows[S0:P, NT, :], start=True, stop=True)
                        mm.then_inc(seq_mm, 1)
                        if l < len(LEVELS):
                            pe.wait_ge(lvl_ready, i * len(LEVELS) + (l + 1))
                            key = qry = dec
                        else:
                            key, qry = qk[:, 1], qk[:, 0]
                        sample = l == len(LEVELS) or 2 * LEVELS[l] <= LS
                        for c in range(NT):
                            for kk in range(KK):
                                mm = nc.tensor.matmul(bank[:, 3, c * P:(c + 1) * P],
                                                      key[:, kk, c * P:(c + 1) * P],
                                                      qry[:, kk, c * P:(c + 1) * P],
                                                      start=(kk == 0), stop=(kk == KK - 1))
                        if sample:
                            pe.wait_ge(kd_saved, i + 1)
                            for kk in range(KK):
                                mm = nc.tensor.matmul(bank[:, 2, 256:256 + TS], key[:, kk, LAST:T],
                                                      qry[:, kk, TP:T], start=(kk == 0), stop=(kk == KK - 1))
                        mm.then_inc(gram_done, 1)
                    if 17 <= s <= 17 + NT:
                        c = s - 17
                        if c == 0:
                            pe.wait_ge(inter_saved, i + 1)
                            pe.wait_ge(lvl_merged, i * NLEVEL + NLEVEL)
                            pe.wait_ge(seq_upd, i * NS + NS)
                        else:
                            pe.wait_ge(chunk_sq, i * NT + c)
                            pe.wait_ge(chunk_state, i * NT + c)
                        if c < NT:
                            for v in range(VV):
                                out = bank[:, 2, v * P:(v + 1) * P]
                                nc.tensor.matmul(out, v_rows[:, c, v * P:(v + 1) * P], scores[:, c * P:(c + 1) * P],
                                                 start=True, stop=(c == 0))
                                for kk in range(KK if c else 0):
                                    nc.tensor.matmul(out, s_prompt[:, kk, v * P:(v + 1) * P],
                                                     qe[:, kk, c * P:(c + 1) * P], start=False, stop=(kk == KK - 1))
                            for kk in range(KK):
                                mm = nc.tensor.matmul(bank[:, kk, :], kd_rows[:, c, kk * P:(kk + 1) * P],
                                                      v_rows[:, c, :], start=True, stop=True)
                        else:
                            for v in range(VV):
                                mm = nc.tensor.matmul(bank[:, 2, v * TS:(v + 1) * TS],
                                                      v_rows[S0:P, NT, v * P:(v + 1) * P], scores[S0:P, TP:T],
                                                      start=True, stop=True)
                        mm.then_inc(chunk_mm, 1)
                    if 18 <= s <= 18 + NT:
                        c = s - 18
                        w = P if c < NT else TS
                        pe.wait_ge(ssq_ready, i * (NT + 1) + (c + 1))
                        if c:
                            pe.wait_ge(o_ready, i * (NT + 1) + c)
                        nc.tensor.matmul(bank[:, 3, 0:w], mean_w[:, :], ssq[:, 0:w], start=True, stop=True
                                         ).then_inc(mean_mm, 1)
                    if s == 24:
                        pe.wait_ge(tail_ready, i * CH + CH)
                        for c in range(CH):
                            tr = nc.tensor.transpose(bank[0:2 * NS + 2, 0, c * P:(c + 1) * P],
                                                     conv_tail[:, c, :], ident[:, :])
                        tr.then_inc(tail_turned, 1)

            pe.wait_ge(xa_in, 16)
            with pe.Fori(0, KT // 2) as i:
                for n in range(2):
                    pe.wait_ge(act_freed, ACT0 + H * ACT_PER + START)
                    if n == 0:
                        pe.wait_ge(dve_freed, i * 2 + (H * DVE_PER - 1) + START)
                    else:
                        pe.wait_ge(dve_freed, i * 2 + H * DVE_PER + START)
                    channel_unit(pe, i * 2 + (U_A + n), (U_A + n) % 2, act_x)
            pe.wait_ge(yb_in, 16)
            with pe.Fori(0, KT // 2) as i:
                for n in range(2):
                    pe.wait_ge(dve_freed, i * 2 + (H * DVE_PER + KT + n - 1) + START)
                    channel_unit(pe, i * 2 + (U_B + n), (U_B + n) % 2, act_y)
            pe.wait_ge(mix_lo, KT)
            with pe.Fori(0, KT // KQ) as i:
                for q in range(4):
                    first = [(out_sum, i * (NT + 1) + START), (dve_freed, H * DVE_PER + 2 * KT + START)] if q == 0 else []
                    token_unit(pe, i * 4 + (U_O + q), (U_O + q) % 2, q, act_x, 0, first)

        @block.vector
        def _(dve):
            V = nc.vector
            for sm in (lo_ready, dve_freed, out_sum):
                dve.sem_inc(sm, START)
            V.memset(eps[:, :], EPS)
            dve.wait_ge(vec_t, 1)
            V.tensor_copy(cvec[:, :], acc[0][:, 0:76]).then_inc(vec_ready, 1)
            dve.wait_ge(cst_t, 1)
            V.tensor_copy(conv_state[:, :, :].rearrange("p k r -> p (k r)"), acc[1][:, 0:KT * 2 * NS]
                          ).then_inc(cst_ready, 1)
            V.memset(mean_w[:, :], 1.0 / DV)
            dve.wait_ge(const_in, 16 * 9)
            V.tensor_copy(masks[:, :, :].rearrange("p l t -> p (l t)"),
                          mix_tile[:, :, :].rearrange("p a t -> p (a t)")[:, 0:NLEVEL * P])
            for t in range(NT + 1):
                n = P if t < NT else TS
                dve.wait_ge(sq_done, t + 1)
                V.tensor_scalar(stat[0:n, 8 + t:9 + t], stat[0:n, t:t + 1], 1.0 / D, EPS, ALU.mult, ALU.add
                                ).then_inc(ms_ready, 1)
                dve.wait_ge(rms_in, t + 1)
                V.reciprocal(stat[0:n, 24 + t:25 + t], stat[0:n, 16 + t:17 + t]).then_inc(dve_self, 1)
                dve.wait_ge(dve_self, t + 1)
                V.tensor_scalar(x_rows[0:n, t, :], x_rows[0:n, t, :], stat[0:n, 24 + t:25 + t], None, ALU.mult
                                ).then_inc(x_scaled, 1)
            SELF0 = NT + 1
            for k in range(KT):
                dve.wait_ge(h_hi, k + 1)
                V.scalar_tensor_tensor(out=act_y[:, k, 1, :], in0=acc[k % 2][:, 0:T], scalar=cvec[:, k:k + 1],
                                       in1=act_y[:, k, 0, :].bitcast(F32), op0=ALU.mult, op1=ALU.subtract
                                       ).then_inc(h_lo, 1)
            subtract_lo(dve, 0, 0)
            subtract_lo(dve, 1, 1)

            count = [0]
            SELF_PER = 28

            with dve.Fori(0, H) as i:
                count[0] = 0

                def link(ins):
                    count[0] += 1
                    ins.then_inc(dve_self, 1)
                    dve.wait_ge(dve_self, i * SELF_PER + (SELF0 + count[0]))

                def level_diff(l):
                    B = LEVELS[l]
                    ins = None
                    for view, ok in ((prompt_blocks, True), (sample_blocks, 2 * B <= LS)):
                        if ok:
                            c = view(cum, 2 * B)
                            for kk in range(KK):
                                ref = c[:, kk, :, B - 1:B].to_broadcast(list(c[:, kk].shape))
                                ins = V.tensor_tensor(view(dec, 2 * B)[:, kk], c[:, kk], ref, ALU.subtract)
                    ins.then_inc(lvl_diff, 1)

                def level_mult(l):
                    B = LEVELS[l]
                    tt = T if 2 * B <= LS else TP
                    dve.wait_ge(lvl_exp, i * len(LEVELS) + (l + 1))
                    for half, src in ((0, 1), (1, 0)):
                        for kk in range(KK):
                            a = dec[:, kk, 0:tt].rearrange("p (c n) -> p c n", n=2 * B)[:, :, half * B:(half + 1) * B]
                            b = qk[:, src, kk, 0:tt].rearrange("p (c n) -> p c n", n=2 * B)[:, :, half * B:(half + 1) * B]
                            ins = V.tensor_tensor(a, a, b, ALU.mult)
                    ins.then_inc(lvl_ready, 1)

                for s, kind in enumerate(STEPS):
                    n = s - STEPS.index(kind)
                    par = par_of(s)
                    out = acc[par][:, A0:A0 + T]
                    subtract_lo(dve, i * NSTEP + (U_BODY + s + 1), par_of(s + 1))
                    if kind == "v" and n == 3:
                        dve.wait_ge(unit_done, i * NSTEP + (U_BODY + s + 1) + START)
                        V.tensor_copy(v_rows[:, 2:4, :], bank[:, 2:4, :])
                        V.tensor_copy(v_rows[S0:P, NT, :], acc[par_of(7)][S0:P, 0:512]).then_inc(v_dve, 1)
                    if kind == "conv_x":
                        c = n // 4
                        if c == 0:
                            V.memset(u_tile[:, 0:2], 0.0)
                        us = u_tile[:, TP + 2:].rearrange("p (s l) -> p s l", s=NS)
                        V.tensor_copy(us[:, :, 0:2], conv_state[:, bass.ds(i * CH + c, 1), :]
                                      .rearrange("p k (s r) -> p (k s) r", r=2))
                        dve.wait_ge(act_freed, i * ACT_PER + (ACT0 + act_upto[s - 1]) + START)
                        dve.wait_ge(unit_done, i * NSTEP + (U_BODY + s + 1) + START)
                        V.tensor_tensor(u_tile[:, 2:TP + 2], mix_tile[:, 0, 0:TP], out[:, 0:TP], ALU.mult)
                        link(V.tensor_tensor(us[:, :, 2:], mix_tile[:, 0, TP:T].rearrange("p (s l) -> p s l", s=NS),
                                             out[:, TP:T].rearrange("p (s l) -> p s l", s=NS), ALU.mult))
                        V.tensor_copy(conv_tail[:, c, 0:2], u_tile[:, TP:TP + 2])
                        V.tensor_copy(conv_tail[:, c, 2:].rearrange("p (s r) -> p s r", r=2), us[:, :, LS:LS + 2]
                                      ).then_inc(tail_ready, 1)
                        cw = [cvec[:, bass.ds(i * CH + (cconv + j * KT + c), 1)] for j in range(3)]
                        y1 = mix_tile[:, 1, 0:TP]
                        y2 = mix_tile[:, 1, TP:T].rearrange("p (s l) -> p s l", s=NS)
                        V.tensor_scalar(y1, u_tile[:, 0:TP], cw[0], None, ALU.mult)
                        link(V.tensor_scalar(y2, us[:, :, 0:LS], cw[0], None, ALU.mult))
                        for j in (1, 2):
                            V.scalar_tensor_tensor(out=y1, in0=u_tile[:, j:TP + j], scalar=cw[j], in1=y1,
                                                   op0=ALU.mult, op1=ALU.add)
                            ins = V.scalar_tensor_tensor(out=y2, in0=us[:, :, j:LS + j], scalar=cw[j], in1=y2,
                                                         op0=ALU.mult, op1=ALU.add)
                            if j == 1:
                                link(ins)
                        ins.then_inc(dve_freed, 1)
                    if kind == "conv_b":
                        dve.wait_ge(dve_freed, i * DVE_PER + dve_upto[s - 1] + START)
                        dve.wait_ge(unit_done, i * NSTEP + (U_BODY + s + 1) + START)
                        V.tensor_tensor(mix_tile[:, 1, :], mix_tile[:, 1, :], out, ALU.mult).then_inc(dve_freed, 1)
                    if kind == "conv_g":
                        m = n // 4
                        dve.wait_ge(dve_freed, i * DVE_PER + dve_upto[s - 1] + START)
                        dve.wait_ge(cg_sig, i * 8 + (m + 1))
                        link(V.tensor_tensor(mix_tile[:, 0, :], mix_tile[:, 0, :], out, ALU.mult))
                        V.tensor_tensor(mix_tile[:, 1, :], mix_tile[:, 1, :], mix_tile[:, 0, :], ALU.mult
                                        ).then_inc(z_f32, 1)
                    if kind == "gla_gate":
                        m = 4 + n
                        dve.wait_ge(cg_sig, i * 8 + (m + 1))
                        link(V.scalar_tensor_tensor(out=mix_tile[:, 1, :], in0=out,
                                                    scalar=cvec[:, cgla + n:cgla + n + 1],
                                                    in1=mix_tile[:, 1, :], op0=ALU.mult, op1=ALU.mult))
                        V.tensor_tensor(mix_tile[:, 1, :], mix_tile[:, 1, :], o_t[:, n, :], ALU.mult
                                        ).then_inc(z_f32, 1)
                    if kind in ("conv_g", "gla_gate"):
                        dve.wait_ge(z_hi, i * 8 + (m + 1))
                        V.tensor_tensor(z_tile[:, 1, :], mix_tile[:, 1, :], z_tile[:, 0, :].bitcast(F32),
                                        ALU.subtract).then_inc(dve_freed, 1)

                    if s == 1:
                        dve.wait_ge(abs_done, i + 1)
                        for kk in range(KK):
                            ap = bank[:, 2 * kk:2 * kk + 2, :].rearrange("p b c -> p (b c)")[:, A0:A0 + T]
                            ins = V.tensor_scalar(cum[:, kk, :], ap, cvec[:, bass.ds(i * KK + (cbal + kk), 1)], 0.0,
                                                  ALU.add, ALU.min)
                        ins.then_inc(neg_part, 1)
                        dve.wait_ge(neg_part, i + 1)
                        dve.wait_ge(soft_part, i + 1)
                        link(V.tensor_tensor(dec[:, :, :], cum[:, :, :], dec[:, :, :], ALU.subtract))
                        for kk in range(KK):
                            ins = V.tensor_tensor_scan(cum[:, kk, :], reset[:, :], dec[:, kk, :], 0.0, ALU.mult, ALU.add)
                        ins.then_inc(cum_ready, 1)
                    if s == 2:
                        dve.wait_ge(eb_ready, i + 1)
                        V.tensor_tensor(qe[:, :, :], qe[:, :, :], qk[:, 0, :, :], ALU.mult).then_inc(qe_ready, 1)
                    if s == 3:
                        dve.wait_ge(cum_ready, i + 1)
                        for view, w in ((prompt_blocks, P), (sample_blocks, LS)):
                            for kk in range(KK):
                                c = view(cum, w)[:, kk]
                                ins = V.tensor_tensor(view(dec, w)[:, kk], c, c[:, :, w - 1:w].to_broadcast(list(c.shape)),
                                                      ALU.subtract)
                        ins.then_inc(kd_diff, 1)
                        dve.wait_ge(kd_exp, i + 1)
                        dve.wait_ge(act_freed, i * ACT_PER + ACT0 + 4 + START)
                        V.tensor_tensor(dec[:, :, :], dec[:, :, :], qk[:, 1, :, :], ALU.mult).then_inc(kd_ready, 1)
                    if s == 8:
                        V.memset(scores[:, :], 0.0)
                        dve.wait_ge(kd_turned, i + 1)
                        level_diff(0)
                        level_mult(0)
                        dve.wait_ge(kd_saved, i + 1)
                    if 9 <= s <= 16:
                        l = s - 9
                        wait_turn(dve, gram_done, i * NLEVEL + (l + 1))
                        m = masks[:, l, :].unsqueeze(1).to_broadcast([P, NT, P])
                        ins = V.copy_predicated(scores[:, 0:TP].rearrange("p (c t) -> p c t", c=NT), m,
                                                bank[:, 3, :].rearrange("p (c t) -> p c t", c=NT))
                        if l == len(LEVELS) or 2 * LEVELS[l] <= LS:
                            ins = V.copy_predicated(scores[S0:P, TP:T], masks[S0:P, l, S0:P], bank[S0:P, 2, 256:256 + TS])
                        ins.then_inc(lvl_merged, 1)
                        if l + 1 < len(LEVELS):
                            level_diff(l + 1)
                            level_mult(l + 1)
                        j = s - 9
                        dve.wait_ge(seq_mm, i * NS + (j + 1))
                        for kk in range(KK):
                            st = states[:, j % 2, kk, :]
                            ins = V.scalar_tensor_tensor(out=st, in0=st, scalar=decay_end[:, kk, NT + j:NT + j + 1],
                                                         in1=bank[:, kk, :], op0=ALU.mult, op1=ALU.add)
                        ins.then_inc(seq_upd, 1)
                    if 8 <= s <= 15:
                        j = s - 8
                        if j >= 2:
                            dve.wait_ge(seq_mm, i * NS + (j - 1))
                        V.tensor_scalar(kd_seq[S0:P, j % 2, :], kd_rows[S0:P, NT, :], seq_sel[S0:P, j:j + 1], None,
                                        ALU.mult).then_inc(seq_kd, 1)
                    if 17 <= s <= 17 + NT:
                        c = s - 17
                        dve.wait_ge(chunk_mm, i * (NT + 1) + (c + 1))
                        if c < NT:
                            for kk in range(KK):
                                st = s_prompt[:, kk, :]
                                if c == 0:
                                    ins = V.tensor_copy(st, bank[:, kk, :])
                                else:
                                    ins = V.scalar_tensor_tensor(out=st, in0=st, scalar=decay_end[:, kk, c:c + 1],
                                                                 in1=bank[:, kk, :], op0=ALU.mult, op1=ALU.add)
                            ins.then_inc(chunk_state, 1)
                            w = P
                            sq = dec[:, 0, 0:VV * P].rearrange("p (v t) -> p v t", v=VV)
                            dve.wait_ge(chunk_sq, i * NT + (c + 1))
                        else:
                            w = TS
                            dve.wait_ge(inter_saved, i + 1)
                            o_s = o_t[:, :, TP:T]
                            link(V.tensor_tensor(o_s, o_s, bank[:, 2, 0:VV * TS].rearrange("p (v t) -> p v t", v=VV),
                                                 ALU.add))
                            sq = dec[:, 0, 0:VV * TS].rearrange("p (v t) -> p v t", v=VV)
                            link(V.tensor_tensor(sq, o_s, o_s, ALU.mult))
                        if c:
                            dve.wait_ge(rms_ready, i * (NT + 1) + c)
                            norm = c - 1
                            link(V.reciprocal(rstd[:, :], rstd[:, :]))
                            for v in range(VV):
                                ov = o_t[:, v, norm * P:(norm + 1) * P]
                                ins = V.tensor_tensor(ov, ov, rstd[:, :], ALU.mult)
                            ins.then_inc(o_ready, 1)
                        V.tensor_reduce(ssq[:, 0:w], sq.rearrange("p v t -> p t v"), AX_X, ALU.add).then_inc(ssq_ready, 1)
                    if s == 18 + NT:
                        dve.wait_ge(rms_ready, i * (NT + 1) + (NT + 1))
                        link(V.reciprocal(rstd[:, 0:TS], rstd[:, 0:TS]))
                        for v in range(VV):
                            ov = o_t[:, v, TP:T]
                            ins = V.tensor_tensor(ov, ov, rstd[:, 0:TS], ALU.mult)
                        ins.then_inc(o_ready, 1)
                        dve.wait_ge(o_ready, i * (NT + 1) + (NT + 1))
                dve.wait_ge(sp_out, i * 16 + 16)
                assert count[0] == SELF_PER, count[0]

            with dve.Fori(0, KT // 2) as i:
                for n in range(2):
                    u1 = U_A + n + 1
                    subtract_lo(dve, i * 2 + u1, u1 % 2)
                    dve.wait_ge(unit_done, i * 2 + u1 + START)
                    dve.wait_ge(gate_in[n], i * 16 + 16)
                    V.tensor_tensor(mix_tile[:, n, :], gate_tile[:, n, :], acc[(U_A + n) % 2][:, A0:A0 + T], ALU.mult
                                    ).then_inc(dve_freed, 1)
            with dve.Fori(0, KT // 2) as i:
                for n in range(2):
                    u1 = U_B + n + 1
                    subtract_lo(dve, i * 2 + u1, u1 % 2)
                    dve.wait_ge(unit_done, i * 2 + u1 + START)
                    dve.wait_ge(gate_in[n], i * 16 + (KT // 2 + 1) * 16)
                    dve.wait_ge(ma_in[n], i * 16 + 16)
                    g = gate_tile[:, n, :]
                    V.tensor_tensor(g, g, acc[(U_B + n) % 2][:, A0:A0 + T], ALU.mult).then_inc(dve_freed, 1)
                    dve.wait_ge(dve_freed, i * 2 + (H * DVE_PER + KT + n + 1) + START)
                    V.tensor_tensor(g, g, mix_tile[:, n, :], ALU.add).then_inc(mix_sum, 1)
                    dve.wait_ge(mix_hi, i * 2 + (n + 1))
                    xk = act_x[:, bass.ds(i * 2 + n, 1), :, :].rearrange("p k h t -> p (k h) t")
                    V.tensor_tensor(xk[:, 1, :], g, xk[:, 0, :].bitcast(F32), ALU.subtract).then_inc(mix_lo, 1)

            def out_group(i, last):
                for q in range(4):
                    u1 = U_O + q + 1
                    if not (last and q == 3):
                        subtract_lo(dve, i * 4 + u1, u1 % 2)
                dve.wait_ge(unit_done, i * 4 + (U_O + 4) + START)
                for t in range(NT + 1):
                    r0 = 0 if t < NT else S0
                    src = bank[:, t, :] if t < NT else acc[0][S0:P, 0:512]
                    dst = resid[r0:P, t, bass.ds(i * 512, 512)]
                    V.tensor_tensor(dst, dst, src, ALU.add).then_inc(out_sum, 1)

            dve.wait_ge(resid_in, 16 * (NT + 2))
            with dve.Fori(0, KT // KQ - 1) as i:
                out_group(i, False)
            out_group(KT // KQ - 1, True)
            dve.wait_ge(act_self, H + 4 * (NT + 1))
            part = stat[:, 0:4 * (NT + 1)].rearrange("p (g t) -> p t g", g=4)
            z0 = SELF0 + H * SELF_PER
            for n, (r0, t0, t1) in enumerate(((0, 0, NT), (S0, NT, NT + 1))):
                V.tensor_reduce(stat[r0:P, 40 + t0:40 + t1], part[r0:P, t0:t1, :], AX_X, ALU.add).then_inc(dve_self, 1)
                dve.wait_ge(dve_self, z0 + 2 * n + 1)
                V.tensor_scalar(stat[r0:P, 46 + t0:46 + t1], stat[r0:P, 40 + t0:40 + t1], 1.0 / D, EPS, ALU.mult, ALU.add
                                ).then_inc(mean_sq, 1)
                dve.wait_ge(rms_out, n + 1)
                V.reciprocal(stat[r0:P, 52 + t0:52 + t1], stat[r0:P, 52 + t0:52 + t1]).then_inc(dve_self, 1)
                dve.wait_ge(dve_self, z0 + 2 * n + 2)
            for t in range(NT + 1):
                r0 = 0 if t < NT else S0
                V.scalar_tensor_tensor(out=resid[r0:P, t, :], in0=resid[r0:P, t, :], scalar=stat[r0:P, 52 + t:53 + t],
                                       in1=gfin[r0:P, :], op0=ALU.mult, op1=ALU.mult).then_inc(y_ready, 1)


_INS = ["x_prompt", "x_sample", "state_conv", "state_gla", "norm_g", "w_in", "conv_w", "w_alpha2", "b_alpha",
        "gla_norm_g", "w_branch_a", "w_branch_b", "w_out", "final_norm_g"]


def _constants(tp, ns, ls):
    import numpy as np
    t = np.arange(P)
    tokens = np.arange(tp + ns * ls)
    start = np.where(tokens < tp, tokens % P == 0, (tokens - tp) % ls == 0)
    reset = np.broadcast_to(1.0 - start, (P, tokens.size))
    rows = t - (P - ns * ls)
    sel = (rows[:, None] // ls == np.arange(ns)[None, :]) & (rows[:, None] >= 0)
    m = []
    s, q = t[:, None], t[None, :]
    for b in LEVELS:
        m.append((s // (2 * b) == q // (2 * b)) & (s % (2 * b) < b) & (q % (2 * b) >= b))
    m.append(s == q)
    return np.concatenate([np.eye(P), reset, sel] + m, axis=1).astype(np.float32)


def kernel(**inputs):
    import numpy as _np
    import concourse.bacc as _bacc
    from concourse import mybir as _mybir
    from concourse.bass_utils import run_bass_kernel_spmd as _run

    nc = _bacc.Bacc("TRN2", target_bir_lowering=False, num_devices=1)
    arrays, args = {}, []
    for name in _INS:
        a = _np.ascontiguousarray(inputs[name])
        arrays[f"in_{name}"] = a
        args.append(nc.dram_tensor(f"in_{name}", a.shape, _mybir.dt.from_np(a.dtype), kind="ExternalInput").ap())
    b, tp, d = inputs["x_prompt"].shape
    ns, ls, _ = inputs["x_sample"].shape
    a = _constants(tp, ns, ls)
    arrays["in_const_f32"] = a
    args.append(nc.dram_tensor("in_const_f32", a.shape, _mybir.dt.float32, kind="ExternalInput").ap())
    depth, _, r, _ = inputs["state_conv"].shape
    gla = inputs["state_gla"].shape
    outs = [(b, tp, d), (ns, ls, d), (depth, b, r, d), (depth, b) + tuple(gla[2:]), (depth, ns, r, d), tuple(gla)]
    for n, shape in enumerate(outs):
        args.append(nc.dram_tensor(f"out_{n}", shape, _mybir.dt.float32, kind="ExternalOutput").ap())
    hybrid_kernel(nc, *args)
    res = _run(nc, [arrays], core_ids=[0])
    return tuple(res.results[0][f"out_{n}"] for n in range(len(outs)))
```

```python
from contextlib import ExitStack

import concourse.bass as bass
from concourse import mybir

ALU = mybir.AluOpType
ACT = mybir.ActivationFunctionType
AX_X = mybir.AxisListType.X
F32 = mybir.dt.float32
F32R = mybir.dt.float32r
U8 = mybir.dt.uint8

P = 128
EPS = 1e-6
TAU = 16.0

LEVELS = [64, 32, 16, 8, 4, 2, 1]
NLEVEL = len(LEVELS) + 1

STEPS = (["q"] * 2 + ["k"] * 2 + ["v"] * 4 + ["conv_c", "conv_x", "conv_b", "conv_g"] * 4
         + ["gla_gate"] * 4 + ["gate_a"] * 4 + ["gate_b"] * 4)
NSTEP = len(STEPS)
LAST_READER = {"q": "act", "k": "act", "v": "act", "conv_c": "act", "gate_a": "act", "gate_b": "act",
               "conv_x": "dve", "conv_b": "dve", "conv_g": "dve", "gla_gate": "dve"}


def hybrid_kernel(nc, x_prompt, x_sample, state_conv, state_gla, norm_g, w_in, conv_w, w_alpha2,
                  b_alpha, gla_norm_g, w_branch_a, w_branch_b, w_out, final_norm_g,
                  const_f32,
                  y_prompt, y_sample, new_conv_prompt, new_gla_prompt, new_conv_sample, new_gla_sample):
    D = x_prompt.shape[2]
    TP = x_prompt.shape[1]
    NS, LS = x_sample.shape[0], x_sample.shape[1]
    TS = NS * LS
    T = TP + TS
    H, DK, DV = state_gla.shape[2:]
    RANK = w_alpha2.shape[1]
    KT = D // P
    NT = TP // P
    KK, VV = DK // P, DV // P
    CH = KT // H
    UNIT = KT * P
    SCALED_BY_DVE, SCALED_BY_ACT = (0, 1, 2), (3, 4)
    HALF = T // 2
    LAST = T - P
    S0 = P - TS
    NB = NT + NS
    assert (KT, NT, KK, VV, CH, TS, RANK) == (16, 4, 2, 4, 4, 64, 16)
    c_ga, c_gb, c_cb, c_cc, c_cx, c_cg = (n * D for n in range(6))
    c_q = 6 * D
    c_k = c_q + H * DK
    c_v = c_k + H * DK
    c_gg = c_v + H * DV
    c_lr = c_gg + H * DV

    w_in_k = w_in[0].rearrange("(k p) c -> p k c", p=P)
    w_a_k = w_branch_a[0].rearrange("(k p) c -> p k c", p=P)
    w_b_k = w_branch_b[0].rearrange("(k p) c -> p k c", p=P)
    w_o_k = w_out[0].rearrange("(k p) c -> p k c", p=P)
    xs_rows = x_sample.rearrange("s t d -> (s t) d")
    ys_rows = y_sample.rearrange("s t d -> (s t) d")

    za_d = nc.dram_tensor("za_d", [KT, P, 2, T], F32R, kind="Internal").ap()
    zb_d = nc.dram_tensor("zb_d", [KT, P, 2, T], F32R, kind="Internal").ap()
    gate_d = nc.dram_tensor("gate_d", [2, KT, P, T], F32, kind="Internal").ap()
    ma_d = nc.dram_tensor("ma_d", [KT, P, T], F32, kind="Internal").ap()

    ctx = ExitStack()
    with ctx:
        arena_bytes = nc.sbuf_usable_end - nc.sbuf_base - 64
        arena_bytes -= arena_bytes % 32
        base = (nc.sbuf_base + 31) // 32 * 32
        ctx.enter_context(nc.sbuf_tensor("arena", [P, arena_bytes // 4], F32))
        size = {F32: 4, F32R: 4, U8: 1}
        cursor = {"at": base}

        def put(name, shape, dt):
            t = nc.alloc_sbuf_tensor_at(name, shape, dt, offset=cursor["at"])
            n = size[dt]
            for s in shape[1:]:
                n *= s
            cursor["at"] += (n + 31) // 32 * 32
            return t

        raw = [put(f"raw{n}", [P, UNIT], F32) for n in range(2)]
        w_hi = [put(f"w_hi{n}", [P, UNIT], F32R) for n in range(2)]
        w_lo = [put(f"w_lo{n}", [P, UNIT], F32R) for n in range(2)]
        ident = put("ident", [P, P], F32)
        gate_tile = put("gate_tile", [P, 2, T], F32)
        mix_tile = put("mix_tile", [P, 2, T], F32)
        stat = put("stat", [P, 64], F32)
        eps = put("eps", [P, 1], F32)
        v2 = put("v2", [P, 2, DV], F32R)
        nsq = put("nsq", [P, P], F32)
        parts = put("parts", [P, KT * (NT + 1)], F32)
        y_at = cursor["at"]
        act_y = put("act_y", [P, KT, 2, T], F32R)
        y_end = cursor["at"]
        g_at = cursor["at"]
        act_x = put("act_x", [P, KT, 2, T], F32R)
        assert cursor["at"] <= base + arena_bytes, cursor["at"] - base - arena_bytes

        cursor["at"] = y_at
        resid = put("resid", [P, NT + 1, D], F32)
        gfin = put("gfin", [P, D], F32)
        assert cursor["at"] <= y_end

        cursor["at"] = g_at
        x_rows = put("x_rows", [P, NT + 1, D], F32)
        vec_rows = put("vec_rows", [P, P], F32)
        conv_rows = put("conv_rows", [2 * NS, D], F32)
        g_rows = put("g_rows", [P, D], F32)
        staging_end = cursor["at"]

        cursor["at"] = g_at
        qk = put("qk", [P, 2, KK, T], F32)
        o_t = nc.alloc_sbuf_tensor_at("o_t", [P, VV, T], F32, offset=g_at)
        cum = put("cum", [P, KK, T], F32)
        dec = put("dec", [P, KK, T], F32)
        qe = put("qe", [P, KK, T], F32)
        v_rows = put("v_rows", [P, NT + 1, DV], F32)
        scores = put("scores", [P, T], F32)
        kd_rows = put("kd_rows", [P, NT + 1, DK], F32)
        kd_seq = put("kd_seq", [P, 2, DK], F32R)
        states = put("states", [P, 2, KK, DV], F32)
        s_prompt = put("s_prompt", [P, KK, DV], F32)
        z_tile = put("z_tile", [P, 2, T], F32R)
        u_tile = put("u_tile", [P, TP + 2 + NS * (LS + 2)], F32)
        ssq = put("ssq", [P, P], F32)
        rstd = put("rstd", [P, P], F32)
        decay_end = put("decay_end", [P, KK, NB], F32)
        w2h = put("w2h", [RANK, DK], F32)
        conv_tail = put("conv_tail", [P, CH, 2 * NS + 2], F32)
        cursor["at"] = max(cursor["at"], staging_end)
        lr_t = put("lr_t", [P, T], F32)
        cvec = put("cvec", [P, 64], F32)
        conv_state = put("conv_state", [P, KT, 2 * NS], F32)
        masks = put("masks", [P, NLEVEL, P], U8)
        reset = put("reset", [P, T], F32)
        seq_sel = put("seq_sel", [P, NS], F32)
        mean_w = put("mean_w", [P, P], F32)
        assert cursor["at"] <= g_at + KT * 2 * T * 4

        acc = [ctx.enter_context(nc.psum_tensor(f"acc{n}", [P, 1024], F32)) for n in range(2)]
        bank = ctx.enter_context(nc.psum_tensor("bank", [P, 4, 512], F32))
        A0 = 512 - HALF

        cbal, cconv, cgla = 0, 8, 8 + 3 * KT
        NVEC = cgla + VV
        G4 = 4
        NXT = (NT + 1) * (KT // G4)

        S = {}

        def sem(name):
            S[name] = ctx.enter_context(nc.semaphore(name))
            return S[name]

        const_in, ident_in, g_in = sem("const_in"), sem("ident_in"), sem("g_in")
        x_in = [sem(f"x_in{n}") for n in range(NT + 1)]
        raw_in = [sem(f"raw_in{n}") for n in range(2)]
        lr_zero = sem("lr_zero")
        hi_ready, lo_ready, unit_done = sem("hi_ready"), sem("lo_ready"), sem("unit_done")
        act_freed, dve_freed = sem("act_freed"), sem("dve_freed")
        act_self, dve_self, passed = sem("act_self"), sem("dve_self"), sem("passed")
        sq_done, ms_ready, rms_in, x_scaled, vec_t, vec_ready, cst_t, cst_ready = (
            sem(n) for n in ("sq_done", "ms_ready", "rms_in", "x_scaled", "vec_t", "vec_ready", "cst_t", "cst_ready"))
        xt_done, h_hi, h_lo = sem("xt_done"), sem("h_hi"), sem("h_lo")
        w2_in, logits, abs_done, neg_part, soft_part, cum_ready = (
            sem(n) for n in ("w2_in", "logits", "abs_done", "neg_part", "soft_part", "cum_ready"))
        eb_ready, qe_ready, kd_diff, kd_exp, kd_ready, kd_turned, kd_saved = (
            sem(n) for n in ("eb_ready", "qe_ready", "kd_diff", "kd_exp", "kd_ready", "kd_turned", "kd_saved"))
        lvl_diff, lvl_exp, lvl_ready, gram_done, lvl_merged = (
            sem(n) for n in ("lvl_diff", "lvl_exp", "lvl_ready", "gram_done", "lvl_merged"))
        v_turned, v_saved = sem("v_turned"), sem("v_saved")
        v2_hi, v2_ready = sem("v2_hi"), sem("v2_ready")
        seq_kd, seq_mm, seq_upd = sem("seq_kd"), sem("seq_mm"), sem("seq_upd")
        st_in = [sem(f"st_in{n}") for n in range(2)]
        st_out = [sem(f"st_out{n}") for n in range(2)]
        inter_saved, chunk_mm, chunk_sq, chunk_state, sp_out = (
            sem(n) for n in ("inter_saved", "chunk_mm", "chunk_sq", "chunk_state", "sp_out"))
        ssq_ready, mean_mm, rms_ready, o_ready = sem("ssq_ready"), sem("mean_mm"), sem("rms_ready"), sem("o_ready")
        cg_sig, z_f32, z_hi, z_out = (
            sem(n) for n in ("cg_sig", "z_f32", "z_hi", "z_out"))
        tail_ready, tail_turned, tail_saved, tail_out = (
            sem(n) for n in ("tail_ready", "tail_turned", "tail_saved", "tail_out"))
        gate_out = [sem(f"gate_out{n}") for n in range(2)]
        xa_in, yb_in = sem("xa_in"), sem("yb_in")
        gate_in = [sem(f"gate_in{n}") for n in range(2)]
        ma_out = [sem(f"ma_out{n}") for n in range(2)]
        ma_in = [sem(f"ma_in{n}") for n in range(2)]
        mix_sum, mix_hi, mix_lo = sem("mix_sum"), sem("mix_hi"), sem("mix_lo")
        resid_in, out_turned, out_sum, squared, weighted, mean_sq, rms_out, y_rstd = (
            sem(n) for n in ("resid_in", "out_turned", "out_sum", "squared", "weighted", "mean_sq", "rms_out", "y_rstd"))
        y_dve, y_act, y_out_sp, y_out = sem("y_dve"), sem("y_act"), sem("y_out_sp"), sem("y_out")

        START = 1

        block = ctx.enter_context(nc.Block())

        U_BODY = 1
        U_A = U_BODY + H * NSTEP
        U_B = U_A + KT
        U_O = U_B + KT
        U_END = U_O + KT
        act_upto = [sum(LAST_READER.get(k) == "act" for k in STEPS[:s + 1]) for s in range(NSTEP)]
        dve_upto = [sum(LAST_READER.get(k) == "dve" for k in STEPS[:s + 1]) for s in range(NSTEP)]
        ACT_PER, DVE_PER = act_upto[-1], dve_upto[-1]
        ACT0 = 1

        def wait_turn(eng, s, value):
            eng.wait_ge(s, value)
            eng.sem_inc(passed, 1)

        def load_unit(sp, u, src, par):
            if not isinstance(u, int) or u >= 2:
                wait_turn(sp, lo_ready, u - 1 + START)
            k, c = src.shape[1], src.shape[2]
            sp.dma_start(raw[par][:, :].rearrange("p (k c) -> p k c", k=k), src).then_inc(raw_in[par], 16)

        def round_hi(act, u, par, turns):
            act.wait_ge(raw_in[par], 16 * turns)
            if not isinstance(u, int) or u >= 2:
                act.wait_ge(unit_done, u - 1 + START)
            nc.scalar.activation(w_hi[par][:, :], raw[par][:, :], ACT.Copy).then_inc(hi_ready, 1)

        def subtract_lo(dve, u, par):
            dve.wait_ge(hi_ready, u + 1)
            nc.vector.tensor_tensor(w_lo[par][:, :], raw[par][:, :], w_hi[par][:, :].bitcast(F32),
                                    ALU.subtract).then_inc(lo_ready, 1)

        PASSES = ((0, 0), (0, 1), (1, 0))

        def channel_unit(pe, u, par, x, last_tile=None):
            pe.wait_ge(lo_ready, u + 1 + START)
            out = acc[par]
            for k in range(KT):
                if last_tile and k == KT - 1:
                    pe.wait_ge(*last_tile)
                for n, (a, b) in enumerate(PASSES):
                    w = (w_hi, w_lo)[a][par][:, k * P:(k + 1) * P]
                    for j in range(2):
                        mm = nc.tensor.matmul(out[:, A0 + j * HALF:A0 + (j + 1) * HALF], w,
                                              x[:, k, b, j * HALF:(j + 1) * HALF],
                                              start=(k == 0 and n == 0), stop=(k == KT - 1 and n == 2))
            mm.then_inc(unit_done, 1)

        def par_of(s):
            return (U_BODY + s) % 2

        def turns_of(i, u_lit, per):
            return (per // 2) * i + (u_lit // 2 + 1)

        @block.sync
        def _(sp):
            sp.dma_start(ident[:, :], const_f32[:, 0:P]).then_inc(ident_in, 16)
            for t in range(NT):
                sp.dma_start(x_rows[:, t, :], x_prompt[0, t * P:(t + 1) * P, :]).then_inc(x_in[t], 16)
            sp.dma_start(x_rows[0:TS, NT, :], xs_rows).then_inc(x_in[NT], 16)
            sp.wait_ge(lr_zero, 1)
            sp.dma_start(raw[0][:, :].rearrange("p (k c) -> p k c", k=KT)[:, :, 0:RANK],
                         w_in_k[:, :, c_lr:c_lr + RANK]).then_inc(raw_in[0], 16)

            def step_src(i, s):
                kind = STEPS[s]
                n = s - STEPS.index(kind)
                if kind in ("q", "k"):
                    c = (c_q if kind == "q" else c_k) + n * P + i * DK
                    return w_in_k[:, :, bass.ds(c, P)]
                if kind == "v":
                    return w_in_k[:, :, bass.ds(i * DV + (c_v + n * P), P)]
                if kind.startswith("conv"):
                    n //= 4
                c0 = {"conv_c": c_cc, "conv_x": c_cx, "conv_b": c_cb, "conv_g": c_cg,
                      "gla_gate": c_gg, "gate_a": c_ga, "gate_b": c_gb}[kind]
                return w_in_k[:, :, bass.ds(i * (CH * P) + (c0 + n * P), P)]

            with sp.Fori(0, H) as i:
                for s in range(NSTEP):
                    load_unit(sp, i * NSTEP + (U_BODY + s), step_src(i, s), par_of(s))
            for u0, w in ((U_A, w_a_k), (U_B, w_b_k), (U_O, w_o_k)):
                with sp.Fori(0, KT // 2) as i:
                    for n in range(2):
                        load_unit(sp, i * 2 + (u0 + n), w[:, :, bass.ds(i * (2 * P) + n * P, P)], (u0 + n) % 2)
            for t in SCALED_BY_DVE:
                sp.wait_ge(y_dve, SCALED_BY_DVE.index(t) + 1)
                sp.dma_start(y_prompt[0, t * P:(t + 1) * P, :], resid[:, t, :]).then_inc(y_out_sp, 16)
            sp.wait_ge(y_out_sp, 16 * len(SCALED_BY_DVE))

        @block.gpsimd
        def _(pool):
            nc.gpsimd.memset(raw[0][:, :], 0.0).then_inc(lr_zero, 1)
            pool.dma_start(g_rows[:, :], norm_g[0].partition_broadcast(P)).then_inc(g_in, 16)
            pool.dma_start(vec_rows[cbal:cbal + 8, :], b_alpha[0].rearrange("(k p) -> k p", p=P)).then_inc(const_in, 16)
            pool.dma_start(vec_rows[cconv:cconv + 3 * KT, :],
                           conv_w[0].rearrange("j (k p) -> (j k) p", p=P)).then_inc(const_in, 16)
            pool.dma_start(vec_rows[cgla:cgla + VV, :],
                           gla_norm_g[0].rearrange("(k p) -> k p", p=P)).then_inc(const_in, 16)
            pool.dma_start(conv_rows[:, :], state_conv[0].rearrange("s r d -> (s r) d")).then_inc(const_in, 16)
            pool.dma_start(reset[:, :], const_f32[:, P:P + T]).then_inc(const_in, 16)
            pool.dma_start(seq_sel[:, :], const_f32[:, P + T:P + T + NS]).then_inc(const_in, 16)
            mask_stage = mix_tile[:, :, :].rearrange("p a t -> p (a t)")[:, 0:NLEVEL * P]
            pool.dma_start(mask_stage, const_f32[:, P + T + NS:P + T + NS + NLEVEL * P]).then_inc(const_in, 16)
            pool.wait_ge(const_in, 16 * 7)
            pool.wait_ge(xt_done, NXT)
            pool.wait_ge(vec_ready, 1)
            pool.wait_ge(cst_ready, 1)
            def head(i, last):
                pool.dma_start(w2h[:, :], w_alpha2[0, :, bass.ds(i * DK, DK)]).then_inc(w2_in, 16)

                def load_state(j):
                    if j >= 2:
                        wait_turn(pool, st_out[j % 2], i * (8 * NS) + 16 * (j // 2))
                    pool.dma_start(states[:, j % 2, :, :],
                                   state_gla[0, j, bass.ds(i, 1), :, :].rearrange("h (k p) v -> p (h k) v", p=P)
                                   ).then_inc(st_in[j % 2], 16)

                def wait_z(m):
                    step = STEPS.index("conv_g") + 4 * m if m < 4 else STEPS.index("gla_gate") + m - 4
                    wait_turn(pool, dve_freed, i * DVE_PER + dve_upto[step] + START)

                load_state(0)
                load_state(1)
                for j in range(NS):
                    wait_turn(pool, seq_upd, i * NS + (j + 1))
                    pool.dma_start(new_gla_sample[0, j, bass.ds(i, 1), :, :].rearrange("h (k p) v -> p (h k) v", p=P),
                                   states[:, j % 2, :, :]).then_inc(st_out[j % 2], 16)
                    if j + 2 < NS:
                        load_state(j + 2)
                    if j in (2, 6):
                        n = j // 4
                        wait_z(n)
                        pool.dma_start(za_d[bass.ds(i * CH + n, 1)].rearrange("k p h t -> p (k h) t"),
                                       z_tile[:, :, :]).then_inc(z_out, 16)
                for n in (2, 3):
                    wait_z(n)
                    pool.dma_start(za_d[bass.ds(i * CH + n, 1)].rearrange("k p h t -> p (k h) t"),
                                   z_tile[:, :, :]).then_inc(z_out, 16)
                    if n == 2:
                        wait_turn(pool, chunk_state, i * NT + NT)
                        pool.dma_start(new_gla_prompt[0, 0, bass.ds(i, 1), :, :].rearrange("h (k p) v -> p (h k) v", p=P),
                                       s_prompt[:, :, :]).then_inc(sp_out, 16)
                for n in range(4):
                    wait_z(4 + n)
                    pool.dma_start(zb_d[bass.ds(i * CH + n, 1)].rearrange("k p h t -> p (k h) t"),
                                   z_tile[:, :, :]).then_inc(z_out, 16)
                    if n == 0:
                        wait_turn(pool, tail_saved, i + 1)
                        pool.dma_start(new_conv_prompt[0, 0, :, bass.ds(i * (CH * P), CH * P)],
                                       mix_tile[0:2, 0, 0:CH * P]).then_inc(tail_out, 16)
                        pool.dma_start(new_conv_sample[0, :, :, bass.ds(i * (CH * P), CH * P)].rearrange("s r d -> (s r) d"),
                                       mix_tile[2:2 + 2 * NS, 0, 0:CH * P]).then_inc(tail_out, 16)
                for n in range(8):
                    wait_turn(pool, act_freed, i * ACT_PER + (ACT0 + act_upto[STEPS.index("gate_a") + n]) + START)
                    pool.dma_start(gate_d[n // 4, bass.ds(i * CH + n % 4, 1)].rearrange("k p t -> p (k t)"),
                                   gate_tile[:, n % 2, :]).then_inc(gate_out[n % 2], 16)
                    if n == 0:
                        wait_turn(pool, z_out, i * 128 + 128)
                        wait_turn(pool, sp_out, i * 16 + 16)
                        wait_turn(pool, tail_out, i * 32 + 32)
                        wait_turn(pool, st_out[0], i * (8 * NS) + 8 * NS)
                        wait_turn(pool, st_out[1], i * (8 * NS) + 8 * NS)
                        if last:
                            pool.dma_start(act_x[:, :, :, :].rearrange("p k h t -> p k (h t)"),
                                           za_d.rearrange("k p h t -> p k (h t)")).then_inc(xa_in, 16)
                wait_turn(pool, gate_out[0], i * 64 + 64)
                wait_turn(pool, gate_out[1], i * 64 + 64)
            with pool.Fori(0, H - 1) as i:
                head(i, False)
            head(H - 1, True)
            pool.wait_ge(unit_done, U_A + START)
            pool.dma_start(act_y[:, :, :, :].rearrange("p k h t -> p k (h t)"),
                           zb_d.rearrange("k p h t -> p k (h t)")).then_inc(yb_in, 16)
            for n in range(2):
                pool.dma_start(gate_tile[:, n, :], gate_d[0, n]).then_inc(gate_in[n], 16)
            with pool.Fori(0, KT // 2) as i:
                for n in range(2):
                    wait_turn(pool, dve_freed, i * 2 + (H * DVE_PER + n + 1) + START)
                    pool.dma_start(ma_d[bass.ds(i * 2 + n, 1)].rearrange("k p t -> p (k t)"),
                                   mix_tile[:, n, :]).then_inc(ma_out[n], 16)
                    wait_turn(pool, ma_out[n], i * 16 + 16)
                    pool.dma_start(gate_tile[:, n, :],
                                   gate_d.rearrange("g k p t -> (g k) p t")[bass.ds(i * 2 + (n + 2), 1)]
                                   .rearrange("k p t -> p (k t)")).then_inc(gate_in[n], 16)
            for n in range(2):
                pool.wait_ge(ma_out[n], 16 * (KT // 2))
                pool.dma_start(mix_tile[:, n, :], ma_d[n]).then_inc(ma_in[n], 16)

            def next_b(i, n):
                wait_turn(pool, mix_lo, i * 2 + (n + 1))
                pool.dma_start(mix_tile[:, n, :], ma_d[bass.ds(i * 2 + (n + 2), 1)].rearrange("k p t -> p (k t)")
                               ).then_inc(ma_in[n], 16)
                pool.dma_start(gate_tile[:, n, :], gate_d[1, bass.ds(i * 2 + (n + 2), 1)].rearrange("k p t -> p (k t)")
                               ).then_inc(gate_in[n], 16)

            with pool.Fori(0, KT // 2 - 1) as i:
                for n in range(2):
                    next_b(i, n)
            pool.wait_ge(unit_done, U_O + START)
            for t in range(NT):
                pool.dma_start(resid[:, t, :], x_prompt[0, t * P:(t + 1) * P, :]).then_inc(resid_in, 16)
            pool.dma_start(resid[0:S0, NT, :], x_prompt[0, LAST:TP, :]).then_inc(resid_in, 16)
            pool.dma_start(resid[S0:P, NT, :], xs_rows).then_inc(resid_in, 16)
            pool.dma_start(gfin[:, :], final_norm_g.partition_broadcast(P)).then_inc(resid_in, 16)
            for t in SCALED_BY_ACT:
                pool.wait_ge(y_act, SCALED_BY_ACT.index(t) + 1)
                if t < NT:
                    pool.dma_start(y_prompt[0, t * P:(t + 1) * P, :], resid[:, t, :]).then_inc(y_out, 16)
                else:
                    pool.dma_start(ys_rows, resid[S0:P, NT, :]).then_inc(y_out, 16)
            pool.wait_ge(y_out, 16 * len(SCALED_BY_ACT))

        def queries(tokens, l):
            if l == len(LEVELS):
                return tokens
            B = LEVELS[l]
            return tokens.rearrange("p (c n) -> p c n", n=2 * B)[:, :, B:2 * B]

        def prompt_blocks(t, n):
            return t[:, :, 0:TP].rearrange("p k (c n) -> p k c n", n=n)

        def sample_blocks(t, n):
            return t[:, :, TP:T].rearrange("p k (c n) -> p k c n", n=n)

        @block.scalar
        def _(act):
            A = nc.scalar.activation
            act.sem_inc(act_freed, START)
            def row_root(t):
                n = P if t < NT else TS
                act.wait_ge(x_in[t], 16)
                if t:
                    act.wait_ge(sq_done, t)
                A(bank[0:n, :, :].rearrange("p b c -> p (b c)"), x_rows[0:n, t, :], ACT.Square,
                  accum_out=stat[0:n, t:t + 1]).then_inc(sq_done, 1)
                act.wait_ge(ms_ready, t + 1)
                A(stat[0:n, 16 + t:17 + t], stat[0:n, 8 + t:9 + t], ACT.Sqrt).then_inc(rms_in, 1)

            row_root(0)
            for t in range(NT + 1):
                if t < NT:
                    row_root(t + 1)
                n = P if t < NT else TS
                for g in range(KT // G4):
                    act.wait_ge(xt_done, t * (KT // G4) + g + 1)
                    A(act_y[:, g * G4:(g + 1) * G4, 0, t * P:t * P + n],
                      acc[g // 2][:, g % 2 * 512:g % 2 * 512 + G4 * n].rearrange("p (k t) -> p k t", k=G4),
                      ACT.Copy).then_inc(h_hi, 1)
            round_hi(act, 0, 0, 1)
            act.wait_ge(unit_done, 1 + START)
            round_hi(act, 1, 1, 1)
            A(lr_t[:, :], acc[0][:, A0:A0 + T], ACT.Copy).then_inc(act_freed, 1)

            with act.Fori(0, H) as i:
                for s, kind in enumerate(STEPS):
                    n = s - STEPS.index(kind)
                    u1 = i * NSTEP + (U_BODY + s + 1)
                    round_hi(act, u1, par_of(s + 1), turns_of(i, U_BODY + s + 1, NSTEP))
                    par = par_of(s)
                    out = acc[par][:, A0:A0 + T]
                    act.wait_ge(unit_done, i * NSTEP + (U_BODY + s + 1) + START)
                    if kind == "q":
                        A(qk[:, 0, n, :], out, ACT.Copy, scale=DK ** -0.5).then_inc(act_freed, 1)
                    if kind == "k":
                        A(qk[:, 1, n, :], out, ACT.Copy).then_inc(act_freed, 1)
                    if kind == "v":
                        if n < 2:
                            act.wait_ge(dve_freed, i * DVE_PER + START)
                        else:
                            act.wait_ge(v_turned, i * VV + (n - 1))
                        A(mix_tile[:, n % 2, :], out, ACT.Copy).then_inc(act_freed, 1)
                    if kind in ("conv_c", "conv_g", "gla_gate"):
                        act.wait_ge(dve_freed, i * DVE_PER + dve_upto[s - 1] + START)
                    if s == 8:
                        act.wait_ge(v_turned, i * VV + (VV - 1))
                    if kind == "conv_c":
                        A(mix_tile[:, 0, :], out, ACT.Copy).then_inc(act_freed, 1)
                    if kind == "conv_g":
                        A(mix_tile[:, 0, :], out, ACT.Sigmoid).then_inc(cg_sig, 1)
                    if kind == "gla_gate":
                        A(mix_tile[:, 1, :], out, ACT.Sigmoid).then_inc(cg_sig, 1)
                    if kind in ("conv_g", "gla_gate"):
                        m = n // 4 if kind == "conv_g" else 4 + n
                        act.wait_ge(z_f32, i * 8 + (m + 1))
                        if m:
                            act.wait_ge(z_out, i * 128 + 16 * m)
                        A(z_tile[:, 0, :], mix_tile[:, 1, :], ACT.Copy).then_inc(z_hi, 1)
                    if kind in ("gate_a", "gate_b"):
                        m = n if kind == "gate_a" else 4 + n
                        if m >= 2:
                            act.wait_ge(gate_out[m % 2], i * 64 + 16 * (m // 2))
                        else:
                            act.wait_ge(w2_in, i * 16 + 16)
                        A(gate_tile[:, m % 2, :], out, ACT.Sigmoid).then_inc(act_freed, 1)

                    if s == 1:
                        act.wait_ge(logits, i + 1)
                        for kk in range(KK):
                            ap = bank[:, 2 * kk:2 * kk + 2, :].rearrange("p b c -> p (b c)")[:, A0:A0 + T]
                            ins = A(dec[:, kk, :], ap, ACT.Abs, bias=cvec[:, bass.ds(i * KK + (cbal + kk), 1)])
                        ins.then_inc(abs_done, 1)
                        act.wait_ge(abs_done, i + 1)
                        A(dec[:, :, :], dec[:, :, :], ACT.Exp, scale=-1.0).then_inc(act_self, 1)
                        act.wait_ge(act_self, i + 1)
                        A(dec[:, :, :], dec[:, :, :], ACT.Ln, bias=1.0).then_inc(soft_part, 1)
                    if s == 2:
                        act.wait_ge(cum_ready, i + 1)
                        A(decay_end[:, :, 0:NT], prompt_blocks(cum, P)[:, :, :, P - 1], ACT.Exp, scale=1 / TAU)
                        A(decay_end[:, :, NT:NB], sample_blocks(cum, LS)[:, :, :, LS - 1], ACT.Exp, scale=1 / TAU)
                        A(qe[:, :, :], cum[:, :, :], ACT.Exp, scale=1 / TAU).then_inc(eb_ready, 1)
                    if s == 3:
                        act.wait_ge(kd_diff, i + 1)
                        A(dec[:, :, :], dec[:, :, :], ACT.Exp, scale=-1 / TAU).then_inc(kd_exp, 1)
                    if s == 4:
                        act.wait_ge(kd_turned, i + 1)
                        A(kd_rows[:, 0:NT, :], bank[:, 0:2, :], ACT.Copy)
                        A(kd_rows[S0:P, NT, :], bank[S0:P, 2, 0:DK], ACT.Copy).then_inc(kd_saved, 1)
                    if s == 8:
                        act.wait_ge(v_saved, i * VV + VV)
                        A(v2[S0:P, 0, :], v_rows[S0:P, NT, :], ACT.Copy)
                        A(v2[0:TS, 0, :], v_rows[S0:P, NT, :], ACT.Copy).then_inc(v2_hi, 1)
                    if 8 <= s < 8 + len(LEVELS):
                        l = s - 8
                        act.wait_ge(lvl_diff, i * len(LEVELS) + (l + 1))
                        for half, sign in ((0, -1), (1, 1)):
                            B = LEVELS[l]
                            tt = T if 2 * B <= LS else TP
                            ap = dec[:, :, 0:tt].rearrange("p k (c n) -> p k c n", n=2 * B)[
                                :, :, :, half * B:(half + 1) * B]
                            ins = A(ap, ap, ACT.Exp, scale=sign / TAU)
                        ins.then_inc(lvl_exp, 1)
                    if s == 16:
                        act.wait_ge(seq_mm, i * NS + NS)
                        act.wait_ge(lvl_merged, i * NLEVEL + NLEVEL)
                        A(o_t[:, :, TP:T], bank[:, 2, 0:VV * TS].rearrange("p (v t) -> p v t", v=VV),
                          ACT.Copy).then_inc(inter_saved, 1)
                    if 17 <= s < 17 + NT:
                        c = s - 17
                        act.wait_ge(chunk_mm, i * (NT + 1) + (c + 1))
                        ap = bank[:, 2, :].rearrange("p (v t) -> p v t", v=VV)
                        if c:
                            act.wait_ge(ssq_ready, i * (NT + 1) + c)
                        A(dec[:, 0, 0:512].rearrange("p (v t) -> p v t", v=VV), ap, ACT.Square)
                        A(o_t[:, :, c * P:(c + 1) * P], ap, ACT.Copy).then_inc(chunk_sq, 1)
                    if 18 <= s <= 18 + NT:
                        c = s - 18
                        w = P if c < NT else TS
                        act.wait_ge(mean_mm, i * (NT + 1) + (c + 1))
                        A(rstd[:, 0:w], bank[:, 3, 0:w], ACT.Sqrt, bias=eps[:, :]).then_inc(rms_ready, 1)
                    if kind == "gate_b" and n == 0:
                        act.wait_ge(z_out, i * 128 + 128)
                    if s == 24:
                        act.wait_ge(tail_turned, i + 1)
                        A(mix_tile[0:2 * NS + 2, 0, 0:CH * P], bank[0:2 * NS + 2, 0, :], ACT.Copy).then_inc(tail_saved, 1)
            with act.Fori(0, KT // 2) as i:
                for n in range(2):
                    u1 = U_A + n + 1
                    round_hi(act, i * 2 + u1, u1 % 2, turns_of(i, u1, 2))
            with act.Fori(0, KT // 2) as i:
                for n in range(2):
                    u1 = U_B + n + 1
                    round_hi(act, i * 2 + u1, u1 % 2, turns_of(i, u1, 2))
                    act.wait_ge(mix_sum, i * 2 + (n + 1))
                    A(act_x[:, bass.ds(i * 2 + n, 1), 0, :].rearrange("p k t -> p (k t)"), gate_tile[:, n, :],
                      ACT.Copy).then_inc(mix_hi, 1)

            def squares(m):
                act.wait_ge(out_sum, m + 1 + START)
                if not isinstance(m, int) or m >= 1:
                    act.wait_ge(squared, m)
                for t in range(NT + 1):
                    ins = A(mix_tile[:, :, :].rearrange("p a t -> p (a t)")[:, t * P:(t + 1) * P],
                            resid[:, t, bass.ds(m * P, P)], ACT.Square,
                            accum_out=parts[:, bass.ds(m * (NT + 1) + t, 1)])
                ins.then_inc(squared, 1)

            def out_tiles(i, first, last):
                for n in range(2):
                    u1 = U_O + n + 1
                    if not (last and n == 1):
                        round_hi(act, i * 2 + u1, u1 % 2, turns_of(i, u1, 2))
                    act.wait_ge(unit_done, i * 2 + u1 + START)
                    if not first:
                        act.wait_ge(out_turned, i * 2 + (n - 1))
                    A(gate_tile[:, n, :], acc[(U_O + n) % 2][:, A0:A0 + T], ACT.Copy).then_inc(act_freed, 1)
                    if not (first and n == 0):
                        squares(i * 2 + (n - 1))

            out_tiles(0, True, False)
            with act.Fori(1, KT // 2 - 1) as i:
                out_tiles(i, False, False)
            out_tiles(KT // 2 - 1, False, True)
            squares(KT - 1)
            act.wait_ge(mean_sq, 1)
            A(stat[:, 16:16 + NT + 1], stat[:, 8:8 + NT + 1], ACT.Sqrt).then_inc(rms_out, 1)
            act.wait_ge(y_rstd, 1)
            act.wait_ge(weighted, KT)
            for t in SCALED_BY_ACT:
                A(resid[:, t, :], resid[:, t, :], ACT.Copy, scale=stat[:, 24 + t:25 + t]).then_inc(y_act, 1)

        @block.tensor
        def _(pe):
            pe.sem_inc(unit_done, START)
            pe.wait_ge(ident_in, 16)
            for t in range(NT + 1):
                n = P if t < NT else TS
                pe.wait_ge(x_scaled, t + 1)
                for g in range(KT // G4):
                    if t:
                        pe.wait_ge(h_lo, (t - 1) * (KT // G4) + g + 1)
                    for k in range(G4):
                        o = g % 2 * 512 + k * n
                        tr = nc.tensor.transpose(acc[g // 2][:, o:o + n],
                                                 x_rows[0:n, t, (g * G4 + k) * P:(g * G4 + k + 1) * P],
                                                 ident[0:n, 0:n])
                    tr.then_inc(xt_done, 1)
            pe.wait_ge(const_in, 16 * 7)
            nc.tensor.transpose(bank[:, 0, 0:NVEC], vec_rows[0:NVEC, :], ident[0:NVEC, 0:NVEC]).then_inc(vec_t, 1)
            for k in range(KT):
                tr = nc.tensor.transpose(bank[:, 1, k * 2 * NS:(k + 1) * 2 * NS], conv_rows[:, k * P:(k + 1) * P],
                                         ident[0:2 * NS, 0:2 * NS])
            tr.then_inc(cst_t, 1)
            pe.wait_ge(h_lo, NXT)
            channel_unit(pe, 0, 0, act_y)

            with pe.Fori(0, H) as i:
                for s, kind in enumerate(STEPS):
                    u, par = i * NSTEP + (U_BODY + s), par_of(s)
                    n = s - STEPS.index(kind)
                    if s >= 2:
                        k2, back = s - 2, 0
                    else:
                        k2, back = s - 2 + NSTEP, 1
                    if LAST_READER[STEPS[k2]] == "act":
                        pe.wait_ge(act_freed, i * ACT_PER + (ACT0 + act_upto[k2] - back * ACT_PER) + START)
                    else:
                        pe.wait_ge(dve_freed, i * DVE_PER + (dve_upto[k2] - back * DVE_PER) + START)
                    channel_unit(pe, u, par, act_y)

                    if s == 1:
                        pe.wait_ge(w2_in, i * 16 + 16)
                        for kk in range(KK):
                            ap = bank[:, 2 * kk:2 * kk + 2, :].rearrange("p b c -> p (b c)")
                            for j in range(2):
                                mm = nc.tensor.matmul(ap[:, A0 + j * HALF:A0 + (j + 1) * HALF],
                                                      w2h[:, kk * P:(kk + 1) * P],
                                                      lr_t[0:RANK, j * HALF:(j + 1) * HALF], start=True, stop=True)
                        mm.then_inc(logits, 1)
                    if 5 <= s <= 8:
                        m = s - 5
                        pe.wait_ge(act_freed, i * ACT_PER + (ACT0 + act_upto[s - 1]) + START)
                        if m == 0:
                            pe.wait_ge(kd_saved, i + 1)
                        if m >= 2:
                            pe.wait_ge(v_saved, i * VV + (m - 1))
                        for c in range(NT + 1):
                            t0 = c * P if c < NT else LAST
                            b, o = 2 * (m % 2) + c // 4, c % 4 * P
                            tr = nc.tensor.transpose(bank[:, b, o:o + P], mix_tile[:, m % 2, t0:t0 + P], ident[:, :])
                        tr.then_inc(v_turned, 1)
                    if s == 4:
                        pe.wait_ge(kd_ready, i + 1)
                        for c in range(NT + 1):
                            t0 = c * P if c < NT else LAST
                            for kk in range(KK):
                                o = (c * KK + kk) * P
                                tr = nc.tensor.transpose(bank[:, o // 512, o % 512:o % 512 + P],
                                                         dec[:, kk, t0:t0 + P], ident[:, :])
                        tr.then_inc(kd_turned, 1)
                    if 9 <= s <= 16:
                        l = j = s - 9
                        if l:
                            pe.wait_ge(lvl_merged, i * NLEVEL + l)
                        if j == 0:
                            pe.wait_ge(qe_ready, i + 1)
                            pe.wait_ge(v2_ready, i + 1)
                        pe.wait_ge(st_in[j % 2], i * (8 * NS) + 16 * (j // 2 + 1))
                        pe.wait_ge(seq_kd, i * NS + (j + 1))
                        if j:
                            pe.wait_ge(seq_upd, i * NS + j)
                        for v in range(VV):
                            for kk in range(KK):
                                nc.tensor.matmul(bank[:, 2, v * TS + j * LS:v * TS + (j + 1) * LS],
                                                 states[:, j % 2, kk, v * P:(v + 1) * P],
                                                 qe[:, kk, TP + j * LS:TP + (j + 1) * LS],
                                                 start=(kk == 0), stop=(kk == KK - 1))
                        for kk in range(KK):
                            for n2 in range(2):
                                mm = nc.tensor.matmul(bank[:, kk, :], kd_seq[:, j % 2, kk * P:(kk + 1) * P],
                                                      v2[:, n2, :], start=(n2 == 0), stop=(n2 == 1))
                        mm.then_inc(seq_mm, 1)
                        if l < len(LEVELS):
                            pe.wait_ge(lvl_ready, i * len(LEVELS) + (l + 1))
                            key = qry = dec
                        else:
                            key, qry = qk[:, 1], qk[:, 0]
                        sample = l == len(LEVELS) or 2 * LEVELS[l] <= LS
                        for c in range(NT):
                            for kk in range(KK):
                                qs = queries(qry[:, kk, c * P:(c + 1) * P], l)
                                w = P if l == len(LEVELS) else P // 2
                                mm = nc.tensor.matmul(bank[:, 3, c * w:(c + 1) * w],
                                                      key[:, kk, c * P:(c + 1) * P], qs,
                                                      start=(kk == 0), stop=(kk == KK - 1))
                        if sample:
                            for kk in range(KK):
                                qs = queries(qry[:, kk, TP:T], l)
                                w = TS if l == len(LEVELS) else TS // 2
                                mm = nc.tensor.matmul(bank[:, 2, 256:256 + w], key[:, kk, LAST:T], qs,
                                                      start=(kk == 0), stop=(kk == KK - 1))
                        mm.then_inc(gram_done, 1)
                    if 17 <= s <= 17 + NT:
                        c = s - 17
                        if c == 0:
                            pe.wait_ge(inter_saved, i + 1)
                            pe.wait_ge(lvl_merged, i * NLEVEL + NLEVEL)
                            pe.wait_ge(seq_upd, i * NS + NS)
                        else:
                            pe.wait_ge(chunk_sq, i * NT + c)
                            pe.wait_ge(chunk_state, i * NT + c)
                        if c < NT:
                            for v in range(VV):
                                out = bank[:, 2, v * P:(v + 1) * P]
                                nc.tensor.matmul(out, v_rows[:, c, v * P:(v + 1) * P], scores[:, c * P:(c + 1) * P],
                                                 start=True, stop=(c == 0))
                                for kk in range(KK if c else 0):
                                    nc.tensor.matmul(out, s_prompt[:, kk, v * P:(v + 1) * P],
                                                     qe[:, kk, c * P:(c + 1) * P], start=False, stop=(kk == KK - 1))
                            for kk in range(KK):
                                mm = nc.tensor.matmul(bank[:, kk, :], kd_rows[:, c, kk * P:(kk + 1) * P],
                                                      v_rows[:, c, :], start=True, stop=True)
                        else:
                            for v in range(VV):
                                mm = nc.tensor.matmul(bank[:, 2, v * TS:(v + 1) * TS],
                                                      v_rows[S0:P, NT, v * P:(v + 1) * P], scores[S0:P, TP:T],
                                                      start=True, stop=True)
                        mm.then_inc(chunk_mm, 1)
                    if 18 <= s <= 18 + NT:
                        c = s - 18
                        w = P if c < NT else TS
                        pe.wait_ge(ssq_ready, i * (NT + 1) + (c + 1))
                        if c:
                            pe.wait_ge(o_ready, i * (NT + 1) + c)
                        nc.tensor.matmul(bank[:, 3, 0:w], mean_w[:, :], ssq[:, 0:w], start=True, stop=True
                                         ).then_inc(mean_mm, 1)
                    if s == 24:
                        pe.wait_ge(tail_ready, i * CH + CH)
                        for c in range(CH):
                            tr = nc.tensor.transpose(bank[0:2 * NS + 2, 0, c * P:(c + 1) * P],
                                                     conv_tail[:, c, :], ident[:, :])
                        tr.then_inc(tail_turned, 1)

            pe.wait_ge(xa_in, 16)
            with pe.Fori(0, KT // 2) as i:
                for n in range(2):
                    pe.wait_ge(act_freed, ACT0 + H * ACT_PER + START)
                    if n == 0:
                        pe.wait_ge(dve_freed, i * 2 + (H * DVE_PER - 1) + START)
                    else:
                        pe.wait_ge(dve_freed, i * 2 + H * DVE_PER + START)
                    channel_unit(pe, i * 2 + (U_A + n), (U_A + n) % 2, act_x)
            pe.wait_ge(yb_in, 16)
            with pe.Fori(0, KT // 2) as i:
                for n in range(2):
                    pe.wait_ge(dve_freed, i * 2 + (H * DVE_PER + KT + n - 1) + START)
                    channel_unit(pe, i * 2 + (U_B + n), (U_B + n) % 2, act_y)
            def turn_out(m, n, unordered):
                pe.wait_ge(act_freed, m + (ACT0 + H * ACT_PER + 1) + START)
                if unordered:
                    pe.wait_ge(out_sum, m - 1 + START)
                for c in range(NT + 1):
                    t0 = c * P if c < NT else LAST
                    b, o = 2 * n + c // 4, c % 4 * P
                    tr = nc.tensor.transpose(bank[:, b, o:o + P], gate_tile[:, n, t0:t0 + P], ident[:, :])
                tr.then_inc(out_turned, 1)

            def out_tiles(i, first):
                for n in range(2):
                    u = i * 2 + (U_O + n)
                    if first:
                        pe.wait_ge(dve_freed, H * DVE_PER + 2 * KT - 1 + n + START)
                        channel_unit(pe, u, (U_O + n) % 2, act_x, (mix_lo, KT))
                    else:
                        pe.wait_ge(act_freed, i * 2 + (ACT0 + H * ACT_PER + n - 1) + START)
                        channel_unit(pe, u, (U_O + n) % 2, act_x)
                    if not (first and n == 0):
                        turn_out(i * 2 + (n - 1), 1 - n, not first)

            out_tiles(0, True)
            with pe.Fori(1, KT // 2) as i:
                out_tiles(i, False)
            turn_out(KT - 1, 1, True)

        @block.vector
        def _(dve):
            V = nc.vector
            for sm in (lo_ready, dve_freed, out_sum):
                dve.sem_inc(sm, START)
            V.memset(eps[:, :], EPS)
            count = [0]
            base = [0]

            def link(ins):
                count[0] += 1
                ins.then_inc(dve_self, 1)
                dve.wait_ge(dve_self, base[0] + count[0])

            def refined(root, ms, eps_ap, one, two):
                link(V.reciprocal(one, root))
                if eps_ap is None:
                    link(V.tensor_tensor(two, ms, one, ALU.mult))
                else:
                    link(V.scalar_tensor_tensor(out=two, in0=ms, scalar=eps_ap, in1=one, op0=ALU.add, op1=ALU.mult))
                link(V.tensor_tensor(two, two, one, ALU.mult))
                link(V.tensor_scalar(two, two, -0.5, 1.5, ALU.mult, ALU.add))
                link(V.tensor_tensor(one, one, two, ALU.mult))

            V.memset(mean_w[:, :], 1.0 / DV)

            def scale_rows(t):
                n = P if t < NT else TS
                dve.wait_ge(sq_done, t + 1)
                V.tensor_scalar(stat[0:n, 8 + t:9 + t], stat[0:n, t:t + 1], 1.0 / D, EPS, ALU.mult, ALU.add
                                ).then_inc(ms_ready, 1)
                dve.wait_ge(rms_in, t + 1)
                refined(stat[0:n, 16 + t:17 + t], stat[0:n, 8 + t:9 + t], None, stat[0:n, 24 + t:25 + t],
                        stat[0:n, 32 + t:33 + t])
                if t == 0:
                    dve.wait_ge(g_in, 16)
                V.scalar_tensor_tensor(out=x_rows[0:n, t, :], in0=x_rows[0:n, t, :], scalar=stat[0:n, 24 + t:25 + t],
                                       in1=g_rows[0:n, :], op0=ALU.mult, op1=ALU.mult).then_inc(x_scaled, 1)

            scale_rows(0)
            for t in range(NT + 1):
                if t < NT:
                    scale_rows(t + 1)
                n = P if t < NT else TS
                for g in range(KT // G4):
                    dve.wait_ge(h_hi, t * (KT // G4) + g + 1)
                    hk = act_y[:, g * G4:(g + 1) * G4, :, t * P:t * P + n]
                    V.tensor_tensor(hk[:, :, 1, :],
                                    acc[g // 2][:, g % 2 * 512:g % 2 * 512 + G4 * n].rearrange("p (k t) -> p k t", k=G4),
                                    hk[:, :, 0, :].bitcast(F32), ALU.subtract).then_inc(h_lo, 1)
            dve.wait_ge(const_in, 16 * 7)
            V.tensor_copy(masks[:, :, :].rearrange("p l t -> p (l t)"),
                          mix_tile[:, :, :].rearrange("p a t -> p (a t)")[:, 0:NLEVEL * P])
            dve.wait_ge(vec_t, 1)
            V.tensor_copy(cvec[:, 0:NVEC], bank[:, 0, 0:NVEC]).then_inc(vec_ready, 1)
            dve.wait_ge(cst_t, 1)
            V.tensor_copy(conv_state[:, :, :].rearrange("p k r -> p (k r)"), bank[:, 1, 0:KT * 2 * NS]
                          ).then_inc(cst_ready, 1)
            SELF0 = count[0]
            subtract_lo(dve, 0, 0)
            subtract_lo(dve, 1, 1)

            SELF_PER = 56

            with dve.Fori(0, H) as i:
                count[0] = 0
                base[0] = i * SELF_PER + SELF0

                def level_diff(l):
                    B = LEVELS[l]
                    ins = None
                    for view, ok in ((prompt_blocks, True), (sample_blocks, 2 * B <= LS)):
                        if ok:
                            c = view(cum, 2 * B)
                            for kk in range(KK):
                                ref = c[:, kk, :, B - 1:B].to_broadcast(list(c[:, kk].shape))
                                ins = V.tensor_tensor(view(dec, 2 * B)[:, kk], c[:, kk], ref, ALU.subtract)
                    ins.then_inc(lvl_diff, 1)

                def level_mult(l):
                    B = LEVELS[l]
                    tt = T if 2 * B <= LS else TP
                    dve.wait_ge(lvl_exp, i * len(LEVELS) + (l + 1))
                    for half, src in ((0, 1), (1, 0)):
                        for kk in range(KK):
                            a = dec[:, kk, 0:tt].rearrange("p (c n) -> p c n", n=2 * B)[:, :, half * B:(half + 1) * B]
                            b = qk[:, src, kk, 0:tt].rearrange("p (c n) -> p c n", n=2 * B)[:, :, half * B:(half + 1) * B]
                            ins = V.tensor_tensor(a, a, b, ALU.mult)
                    ins.then_inc(lvl_ready, 1)

                for s, kind in enumerate(STEPS):
                    n = s - STEPS.index(kind)
                    par = par_of(s)
                    out = acc[par][:, A0:A0 + T]
                    subtract_lo(dve, i * NSTEP + (U_BODY + s + 1), par_of(s + 1))
                    if 5 <= s <= 8:
                        m = s - 5
                        dve.wait_ge(v_turned, i * VV + (m + 1))
                        two = bank[:, 2 * (m % 2):2 * (m % 2) + 2, :].rearrange("p b c -> p (b c)")
                        ins = V.tensor_copy(v_rows[:, :, m * P:(m + 1) * P],
                                            two[:, 0:(NT + 1) * P].rearrange("p (t c) -> p t c", c=P))
                        ins.then_inc(v_saved, 1)
                    if kind == "conv_x":
                        c = n // 4
                        if c == 0:
                            V.memset(u_tile[:, 0:2], 0.0)
                        us = u_tile[:, TP + 2:].rearrange("p (s l) -> p s l", s=NS)
                        V.tensor_copy(us[:, :, 0:2], conv_state[:, bass.ds(i * CH + c, 1), :]
                                      .rearrange("p k (s r) -> p (k s) r", r=2))
                        dve.wait_ge(act_freed, i * ACT_PER + (ACT0 + act_upto[s - 1]) + START)
                        dve.wait_ge(unit_done, i * NSTEP + (U_BODY + s + 1) + START)
                        V.tensor_tensor(u_tile[:, 2:TP + 2], mix_tile[:, 0, 0:TP], out[:, 0:TP], ALU.mult)
                        link(V.tensor_tensor(us[:, :, 2:], mix_tile[:, 0, TP:T].rearrange("p (s l) -> p s l", s=NS),
                                             out[:, TP:T].rearrange("p (s l) -> p s l", s=NS), ALU.mult))
                        V.tensor_copy(conv_tail[:, c, 0:2], u_tile[:, TP:TP + 2])
                        V.tensor_copy(conv_tail[:, c, 2:].rearrange("p (s r) -> p s r", r=2), us[:, :, LS:LS + 2]
                                      ).then_inc(tail_ready, 1)
                        cw = [cvec[:, bass.ds(i * CH + (cconv + j * KT + c), 1)] for j in range(3)]
                        y1 = mix_tile[:, 1, 0:TP]
                        y2 = mix_tile[:, 1, TP:T].rearrange("p (s l) -> p s l", s=NS)
                        V.tensor_scalar(y1, u_tile[:, 0:TP], cw[0], None, ALU.mult)
                        link(V.tensor_scalar(y2, us[:, :, 0:LS], cw[0], None, ALU.mult))
                        for j in (1, 2):
                            V.scalar_tensor_tensor(out=y1, in0=u_tile[:, j:TP + j], scalar=cw[j], in1=y1,
                                                   op0=ALU.mult, op1=ALU.add)
                            ins = V.scalar_tensor_tensor(out=y2, in0=us[:, :, j:LS + j], scalar=cw[j], in1=y2,
                                                         op0=ALU.mult, op1=ALU.add)
                            if j == 1:
                                link(ins)
                        ins.then_inc(dve_freed, 1)
                    if kind == "conv_b":
                        dve.wait_ge(dve_freed, i * DVE_PER + dve_upto[s - 1] + START)
                        dve.wait_ge(unit_done, i * NSTEP + (U_BODY + s + 1) + START)
                        V.tensor_tensor(mix_tile[:, 1, :], mix_tile[:, 1, :], out, ALU.mult).then_inc(dve_freed, 1)
                    if kind == "conv_g":
                        m = n // 4
                        dve.wait_ge(dve_freed, i * DVE_PER + dve_upto[s - 1] + START)
                        dve.wait_ge(cg_sig, i * 8 + (m + 1))
                        link(V.tensor_tensor(mix_tile[:, 0, :], mix_tile[:, 0, :], out, ALU.mult))
                        V.tensor_tensor(mix_tile[:, 1, :], mix_tile[:, 1, :], mix_tile[:, 0, :], ALU.mult
                                        ).then_inc(z_f32, 1)
                    if kind == "gla_gate":
                        m = 4 + n
                        dve.wait_ge(cg_sig, i * 8 + (m + 1))
                        link(V.scalar_tensor_tensor(out=mix_tile[:, 1, :], in0=out,
                                                    scalar=cvec[:, cgla + n:cgla + n + 1],
                                                    in1=mix_tile[:, 1, :], op0=ALU.mult, op1=ALU.mult))
                        V.tensor_tensor(mix_tile[:, 1, :], mix_tile[:, 1, :], o_t[:, n, :], ALU.mult
                                        ).then_inc(z_f32, 1)
                    if kind in ("conv_g", "gla_gate"):
                        dve.wait_ge(z_hi, i * 8 + (m + 1))
                        V.tensor_tensor(z_tile[:, 1, :], mix_tile[:, 1, :], z_tile[:, 0, :].bitcast(F32),
                                        ALU.subtract).then_inc(dve_freed, 1)

                    if s == 1:
                        dve.wait_ge(abs_done, i + 1)
                        for kk in range(KK):
                            ap = bank[:, 2 * kk:2 * kk + 2, :].rearrange("p b c -> p (b c)")[:, A0:A0 + T]
                            ins = V.tensor_scalar(cum[:, kk, :], ap, cvec[:, bass.ds(i * KK + (cbal + kk), 1)], 0.0,
                                                  ALU.add, ALU.min)
                        ins.then_inc(neg_part, 1)
                        dve.wait_ge(neg_part, i + 1)
                        dve.wait_ge(soft_part, i + 1)
                        link(V.tensor_tensor(dec[:, :, :], cum[:, :, :], dec[:, :, :], ALU.subtract))
                        for kk in range(KK):
                            ins = V.tensor_tensor_scan(cum[:, kk, :], reset[:, :], dec[:, kk, :], 0.0, ALU.mult, ALU.add)
                        ins.then_inc(cum_ready, 1)
                    if s == 2:
                        dve.wait_ge(eb_ready, i + 1)
                        V.tensor_tensor(qe[:, :, :], qe[:, :, :], qk[:, 0, :, :], ALU.mult).then_inc(qe_ready, 1)
                    if s == 3:
                        dve.wait_ge(cum_ready, i + 1)
                        for view, w in ((prompt_blocks, P), (sample_blocks, LS)):
                            for kk in range(KK):
                                c = view(cum, w)[:, kk]
                                ins = V.tensor_tensor(view(dec, w)[:, kk], c, c[:, :, w - 1:w].to_broadcast(list(c.shape)),
                                                      ALU.subtract)
                        ins.then_inc(kd_diff, 1)
                        dve.wait_ge(kd_exp, i + 1)
                        dve.wait_ge(act_freed, i * ACT_PER + ACT0 + 4 + START)
                        V.tensor_tensor(dec[:, :, :], dec[:, :, :], qk[:, 1, :, :], ALU.mult).then_inc(kd_ready, 1)
                    if s == 8:
                        for half in (slice(S0, P), slice(0, TS)):
                            dve.wait_ge(v2_hi, i + 1)
                            ins = V.tensor_tensor(v2[half, 1, :], v_rows[S0:P, NT, :], v2[S0:P, 0, :].bitcast(F32),
                                                  ALU.subtract)
                        ins.then_inc(v2_ready, 1)
                        V.memset(scores[:, :], 0.0)
                        dve.wait_ge(kd_turned, i + 1)
                        level_diff(0)
                        level_mult(0)
                        dve.wait_ge(kd_saved, i + 1)
                    if 9 <= s <= 16:
                        l = s - 9
                        wait_turn(dve, gram_done, i * NLEVEL + (l + 1))
                        w = P if l == len(LEVELS) else P // 2
                        for c in range(NT):
                            dst, m = queries(scores[:, c * P:(c + 1) * P], l), queries(masks[:, l, :], l)
                            src = bank[:, 3, c * w:(c + 1) * w]
                            if w < P:
                                src = src.rearrange("p (c n) -> p c n", n=LEVELS[l])
                            ins = V.copy_predicated(dst, m, src)
                        if l == len(LEVELS) or 2 * LEVELS[l] <= LS:
                            w = TS if l == len(LEVELS) else TS // 2
                            src = bank[S0:P, 2, 256:256 + w]
                            if w < TS:
                                src = src.rearrange("p (c n) -> p c n", n=LEVELS[l])
                            ins = V.copy_predicated(queries(scores[S0:P, TP:T], l), queries(masks[S0:P, l, S0:P], l), src)
                        ins.then_inc(lvl_merged, 1)
                        if l + 1 < len(LEVELS):
                            level_diff(l + 1)
                            level_mult(l + 1)
                        j = s - 9
                        dve.wait_ge(seq_mm, i * NS + (j + 1))
                        for kk in range(KK):
                            st = states[:, j % 2, kk, :]
                            ins = V.scalar_tensor_tensor(out=st, in0=st, scalar=decay_end[:, kk, NT + j:NT + j + 1],
                                                         in1=bank[:, kk, :], op0=ALU.mult, op1=ALU.add)
                        ins.then_inc(seq_upd, 1)
                    if 8 <= s <= 15:
                        j = s - 8
                        if j >= 2:
                            dve.wait_ge(seq_mm, i * NS + (j - 1))
                        link(V.tensor_scalar(kd_seq[S0:P, j % 2, :], kd_rows[S0:P, NT, :], seq_sel[S0:P, j:j + 1],
                                             None, ALU.mult))
                        V.scalar_tensor_tensor(out=kd_seq[0:TS, j % 2, :], in0=kd_rows[S0:P, NT, :],
                                               scalar=seq_sel[S0:P, j:j + 1],
                                               in1=kd_seq[S0:P, j % 2, :].bitcast(F32),
                                               op0=ALU.mult, op1=ALU.subtract).then_inc(seq_kd, 1)
                    if 17 <= s <= 17 + NT:
                        c = s - 17
                        dve.wait_ge(chunk_mm, i * (NT + 1) + (c + 1))
                        if c < NT:
                            for kk in range(KK):
                                st = s_prompt[:, kk, :]
                                if c == 0:
                                    ins = V.tensor_copy(st, bank[:, kk, :])
                                else:
                                    ins = V.scalar_tensor_tensor(out=st, in0=st, scalar=decay_end[:, kk, c:c + 1],
                                                                 in1=bank[:, kk, :], op0=ALU.mult, op1=ALU.add)
                            ins.then_inc(chunk_state, 1)
                            w = P
                            sq = dec[:, 0, 0:VV * P].rearrange("p (v t) -> p v t", v=VV)
                            dve.wait_ge(chunk_sq, i * NT + (c + 1))
                        else:
                            w = TS
                            dve.wait_ge(inter_saved, i + 1)
                            o_s = o_t[:, :, TP:T]
                            link(V.tensor_tensor(o_s, o_s, bank[:, 2, 0:VV * TS].rearrange("p (v t) -> p v t", v=VV),
                                                 ALU.add))
                            sq = dec[:, 0, 0:VV * TS].rearrange("p (v t) -> p v t", v=VV)
                            link(V.tensor_tensor(sq, o_s, o_s, ALU.mult))
                        if c:
                            dve.wait_ge(rms_ready, i * (NT + 1) + c)
                            norm = c - 1
                            refined(rstd[:, :], bank[:, 3, 0:P], eps[:, :], rstd[:, :], nsq[:, :])
                            for v in range(VV):
                                ov = o_t[:, v, norm * P:(norm + 1) * P]
                                ins = V.tensor_tensor(ov, ov, rstd[:, :], ALU.mult)
                            ins.then_inc(o_ready, 1)
                        V.tensor_reduce(ssq[:, 0:w], sq.rearrange("p v t -> p t v"), AX_X, ALU.add).then_inc(ssq_ready, 1)
                    if s == 18 + NT:
                        dve.wait_ge(rms_ready, i * (NT + 1) + (NT + 1))
                        refined(rstd[:, 0:TS], bank[:, 3, 0:TS], eps[:, :], rstd[:, 0:TS], nsq[:, 0:TS])
                        for v in range(VV):
                            ov = o_t[:, v, TP:T]
                            ins = V.tensor_tensor(ov, ov, rstd[:, 0:TS], ALU.mult)
                        ins.then_inc(o_ready, 1)
                        dve.wait_ge(o_ready, i * (NT + 1) + (NT + 1))
                dve.wait_ge(sp_out, i * 16 + 16)
                assert count[0] == SELF_PER, count[0]

            with dve.Fori(0, KT // 2) as i:
                for n in range(2):
                    u1 = U_A + n + 1
                    subtract_lo(dve, i * 2 + u1, u1 % 2)
                    dve.wait_ge(unit_done, i * 2 + u1 + START)
                    dve.wait_ge(gate_in[n], i * 16 + 16)
                    V.tensor_tensor(mix_tile[:, n, :], gate_tile[:, n, :], acc[(U_A + n) % 2][:, A0:A0 + T], ALU.mult
                                    ).then_inc(dve_freed, 1)
            with dve.Fori(0, KT // 2) as i:
                for n in range(2):
                    u1 = U_B + n + 1
                    subtract_lo(dve, i * 2 + u1, u1 % 2)
                    dve.wait_ge(unit_done, i * 2 + u1 + START)
                    dve.wait_ge(gate_in[n], i * 16 + (KT // 2 + 1) * 16)
                    dve.wait_ge(ma_in[n], i * 16 + 16)
                    g = gate_tile[:, n, :]
                    V.tensor_tensor(g, g, acc[(U_B + n) % 2][:, A0:A0 + T], ALU.mult).then_inc(dve_freed, 1)
                    dve.wait_ge(dve_freed, i * 2 + (H * DVE_PER + KT + n + 1) + START)
                    V.tensor_tensor(g, g, mix_tile[:, n, :], ALU.add).then_inc(mix_sum, 1)
                    dve.wait_ge(mix_hi, i * 2 + (n + 1))
                    xk = act_x[:, bass.ds(i * 2 + n, 1), :, :].rearrange("p k h t -> p (k h) t")
                    V.tensor_tensor(xk[:, 1, :], g, xk[:, 0, :].bitcast(F32), ALU.subtract).then_inc(mix_lo, 1)

            def add_turned(m, n):
                dve.wait_ge(out_turned, m + 1)
                two = bank[:, 2 * n:2 * n + 2, :].rearrange("p b c -> p (b c)")
                dst = resid[:, :, bass.ds(m * P, P)]
                V.tensor_tensor(dst, dst, two[:, 0:(NT + 1) * P].rearrange("p (t c) -> p t c", c=P), ALU.add
                                ).then_inc(out_sum, 1)

            def weight(m):
                dve.wait_ge(squared, m + 1)
                dst = resid[:, :, bass.ds(m * P, P)]
                g = gfin[:, bass.ds(m * P, P)].rearrange("p (o c) -> p o c", o=1).to_broadcast([P, NT + 1, P])
                V.tensor_tensor(dst, dst, g, ALU.mult).then_inc(weighted, 1)

            def out_tiles(i, first, last):
                for n in range(2):
                    u1 = U_O + n + 1
                    if not (last and n == 1):
                        subtract_lo(dve, i * 2 + u1, u1 % 2)
                    if first and n == 1:
                        dve.wait_ge(resid_in, 16 * (NT + 3))
                    if not (first and n == 0):
                        add_turned(i * 2 + (n - 1), 1 - n)
                    if not first:
                        weight(i * 2 + (n - 2))

            out_tiles(0, True, False)
            with dve.Fori(1, KT // 2 - 1) as i:
                out_tiles(i, False, False)
            out_tiles(KT // 2 - 1, False, True)
            add_turned(KT - 1, 1)
            weight(KT - 2)
            base[0], count[0] = SELF0 + H * SELF_PER, 0
            dve.wait_ge(squared, KT)
            link(V.tensor_reduce(stat[:, 0:NT + 1], parts[:, :].rearrange("p (m t) -> p t m", t=NT + 1), AX_X, ALU.add))
            V.tensor_scalar(stat[:, 8:8 + NT + 1], stat[:, 0:NT + 1], 1.0 / D, EPS, ALU.mult, ALU.add
                            ).then_inc(mean_sq, 1)
            weight(KT - 1)
            dve.wait_ge(rms_out, 1)
            refined(stat[:, 16:16 + NT + 1], stat[:, 8:8 + NT + 1], None, stat[:, 24:24 + NT + 1],
                    stat[:, 32:32 + NT + 1])
            dve.sem_inc(y_rstd, 1)
            dve.wait_ge(weighted, KT)
            for t in SCALED_BY_DVE:
                V.tensor_scalar(resid[:, t, :], resid[:, t, :], stat[:, 24 + t:25 + t], None, ALU.mult
                                ).then_inc(y_dve, 1)


_INS = ["x_prompt", "x_sample", "state_conv", "state_gla", "norm_g", "w_in", "conv_w", "w_alpha2", "b_alpha",
        "gla_norm_g", "w_branch_a", "w_branch_b", "w_out", "final_norm_g"]


def _constants(tp, ns, ls):
    import numpy as np
    t = np.arange(P)
    tokens = np.arange(tp + ns * ls)
    start = np.where(tokens < tp, tokens % P == 0, (tokens - tp) % ls == 0)
    reset = np.broadcast_to(1.0 - start, (P, tokens.size))
    rows = t - (P - ns * ls)
    sel = (rows[:, None] // ls == np.arange(ns)[None, :]) & (rows[:, None] >= 0)
    m = []
    s, q = t[:, None], t[None, :]
    for b in LEVELS:
        m.append((s // (2 * b) == q // (2 * b)) & (s % (2 * b) < b) & (q % (2 * b) >= b))
    m.append(s == q)
    return np.concatenate([np.eye(P), reset, sel] + m, axis=1).astype(np.float32)


def kernel(**inputs):
    import numpy as _np
    import concourse.bacc as _bacc
    from concourse import mybir as _mybir
    from concourse.bass_utils import run_bass_kernel_spmd as _run

    nc = _bacc.Bacc("TRN2", target_bir_lowering=False, num_devices=1)
    arrays, args = {}, []
    for name in _INS:
        a = _np.ascontiguousarray(inputs[name])
        arrays[f"in_{name}"] = a
        args.append(nc.dram_tensor(f"in_{name}", a.shape, _mybir.dt.from_np(a.dtype), kind="ExternalInput").ap())
    b, tp, d = inputs["x_prompt"].shape
    ns, ls, _ = inputs["x_sample"].shape
    a = _constants(tp, ns, ls)
    arrays["in_const_f32"] = a
    args.append(nc.dram_tensor("in_const_f32", a.shape, _mybir.dt.float32, kind="ExternalInput").ap())
    depth, _, r, _ = inputs["state_conv"].shape
    gla = inputs["state_gla"].shape
    outs = [(b, tp, d), (ns, ls, d), (depth, b, r, d), (depth, b) + tuple(gla[2:]), (depth, ns, r, d), tuple(gla)]
    for n, shape in enumerate(outs):
        args.append(nc.dram_tensor(f"out_{n}", shape, _mybir.dt.float32, kind="ExternalOutput").ap())
    hybrid_kernel(nc, *args)
    res = _run(nc, [arrays], core_ids=[0])
    return tuple(res.results[0][f"out_{n}"] for n in range(len(outs)))
```

```python
from contextlib import ExitStack

import concourse.bass as bass
from concourse import mybir

ALU = mybir.AluOpType
ACT = mybir.ActivationFunctionType
AX_X = mybir.AxisListType.X
F32 = mybir.dt.float32
F32R = mybir.dt.float32r
U8 = mybir.dt.uint8

P = 128
EPS = 1e-6
TAU = 16.0

LEVELS = [64, 32, 16, 8, 4, 2, 1]
NLEVEL = len(LEVELS) + 1

STEPS = (["q"] * 2 + ["k"] * 2 + ["v"] * 4 + ["conv_c", "conv_x", "conv_b", "conv_g"] * 4
         + ["gla_gate"] * 4 + ["gate_a"] * 4 + ["gate_b"] * 4)
NSTEP = len(STEPS)
SEQ_STEP = [7, 8, 10, 11, 12, 13, 14, 15]
LAST_READER = {"q": "act", "k": "act", "v": "act", "conv_c": "act", "gate_a": "act", "gate_b": "act",
               "conv_x": "dve", "conv_b": "dve", "conv_g": "dve", "gla_gate": "dve"}


def hybrid_kernel(nc, x_prompt, x_sample, state_conv, state_gla, norm_g, w_in, conv_w, w_alpha2,
                  b_alpha, gla_norm_g, w_branch_a, w_branch_b, w_out, final_norm_g,
                  const_f32,
                  y_prompt, y_sample, new_conv_prompt, new_gla_prompt, new_conv_sample, new_gla_sample):
    D = x_prompt.shape[2]
    TP = x_prompt.shape[1]
    NS, LS = x_sample.shape[0], x_sample.shape[1]
    TS = NS * LS
    T = TP + TS
    H, DK, DV = state_gla.shape[2:]
    RANK = w_alpha2.shape[1]
    KT = D // P
    NT = TP // P
    KK, VV = DK // P, DV // P
    CH = KT // H
    UNIT = KT * P
    LR_LO = 32
    G_S = TP // 2
    XA_STEP = 3
    SCALED_BY_DVE, SCALED_BY_ACT = (0, 1, 2), (3, 4)
    HALF = T // 2
    LAST = T - P
    S0 = P - TS
    NB = NT + NS
    assert (KT, NT, KK, VV, CH, TS, RANK) == (16, 4, 2, 4, 4, 64, 16)
    c_ga, c_gb, c_cb, c_cc, c_cx, c_cg = (n * D for n in range(6))
    c_q = 6 * D
    c_k = c_q + H * DK
    c_v = c_k + H * DK
    c_gg = c_v + H * DV
    c_lr = c_gg + H * DV

    w_in_k = w_in[0].rearrange("(k p) c -> p k c", p=P)
    w_a_k = w_branch_a[0].rearrange("(k p) c -> p k c", p=P)
    w_b_k = w_branch_b[0].rearrange("(k p) c -> p k c", p=P)
    w_o_k = w_out[0].rearrange("(k p) c -> p k c", p=P)
    xs_rows = x_sample.rearrange("s t d -> (s t) d")
    ys_rows = y_sample.rearrange("s t d -> (s t) d")

    za_d = nc.dram_tensor("za_d", [KT, P, 2, T], F32R, kind="Internal").ap()
    zb_d = nc.dram_tensor("zb_d", [KT, P, 2, T], F32R, kind="Internal").ap()
    gate_d = nc.dram_tensor("gate_d", [2, KT, P, T], F32, kind="Internal").ap()
    ma_d = nc.dram_tensor("ma_d", [KT, P, T], F32, kind="Internal").ap()

    ctx = ExitStack()
    with ctx:
        arena_bytes = nc.sbuf_usable_end - nc.sbuf_base - 64
        arena_bytes -= arena_bytes % 32
        base = (nc.sbuf_base + 31) // 32 * 32
        ctx.enter_context(nc.sbuf_tensor("arena", [P, arena_bytes // 4], F32))
        size = {F32: 4, F32R: 4, U8: 1}
        cursor = {"at": base}

        def put(name, shape, dt):
            t = nc.alloc_sbuf_tensor_at(name, shape, dt, offset=cursor["at"])
            n = size[dt]
            for s in shape[1:]:
                n *= s
            cursor["at"] += (n + 31) // 32 * 32
            return t

        raw = [put(f"raw{n}", [P, UNIT], F32) for n in range(2)]
        w_hi = [put(f"w_hi{n}", [P, UNIT], F32R) for n in range(2)]
        w_lo = [put(f"w_lo{n}", [P, UNIT], F32R) for n in range(2)]
        ident = put("ident", [P, P], F32)
        gate_at = cursor["at"]
        gate_tile = put("gate_tile", [P, 2, T], F32)
        s_hi = nc.alloc_sbuf_tensor_at("s_hi", [P, KK, DV], F32R, offset=gate_at)
        q_state = nc.alloc_sbuf_tensor_at("q_state", [P, DV], F32, offset=gate_at)
        assert KK * DV <= 2 * T
        mix_tile = put("mix_tile", [P, 2, T], F32)
        stat = put("stat", [P, 64], F32)
        eps = put("eps", [P, 1], F32)
        v2 = put("v2", [P, 2, DV], F32R)
        nsq = put("nsq", [P, P], F32)
        pair = put("pair", [P, TS], F32)
        parts = put("parts", [P, KT * (NT + 1)], F32)
        y_at = cursor["at"]
        act_y = put("act_y", [P, KT, 2, T], F32R)
        y_end = cursor["at"]
        g_at = cursor["at"]
        act_x = put("act_x", [P, KT, 2, T], F32R)
        assert cursor["at"] <= base + arena_bytes, cursor["at"] - base - arena_bytes

        cursor["at"] = y_at
        resid = put("resid", [P, NT + 1, D], F32)
        gfin = put("gfin", [P, D], F32)
        assert cursor["at"] <= y_end

        cursor["at"] = g_at
        x_rows = put("x_rows", [P, NT + 1, D], F32)
        vec_rows = put("vec_rows", [P, P], F32)
        conv_rows = put("conv_rows", [2 * NS, D], F32)
        g_rows = put("g_rows", [P, D], F32)
        staging_end = cursor["at"]

        cursor["at"] = g_at
        qk = put("qk", [P, 2, KK, T], F32)
        o_t = nc.alloc_sbuf_tensor_at("o_t", [P, VV, T], F32, offset=g_at)
        cum = put("cum", [P, KK, T], F32)
        dec = put("dec", [P, KK, T], F32)
        qe = put("qe", [P, KK, T], F32)
        v_rows = put("v_rows", [P, NT + 1, DV], F32)
        scores = put("scores", [P, T], F32)
        kd_rows = put("kd_rows", [P, NT + 1, DK], F32)
        kd_seq = put("kd_seq", [P, 2, DK], F32R)
        states = put("states", [P, 2, KK, DV], F32)
        prompt_at = cursor["at"]
        s_prompt = put("s_prompt", [P, KK, DV], F32)
        s_lo = nc.alloc_sbuf_tensor_at("s_lo", [P, KK, DV], F32R, offset=prompt_at)
        q_seq = put("q_seq", [P, KK, P], F32R)
        z_tile = put("z_tile", [P, 2, T], F32R)
        u_tile = put("u_tile", [P, TP + 2 + NS * (LS + 2)], F32)
        ssq = put("ssq", [P, P], F32)
        rstd = put("rstd", [P, P], F32)
        decay_end = put("decay_end", [P, KK, NB], F32)
        w2h = put("w2h", [LR_LO + RANK, DK], F32)
        conv_tail = put("conv_tail", [P, CH, 2 * NS + 2], F32)
        cursor["at"] = max(cursor["at"], staging_end)
        lr_t = put("lr_t", [P, T], F32)
        cvec = put("cvec", [P, 64], F32)
        conv_state = put("conv_state", [P, KT, 2 * NS], F32)
        masks = put("masks", [P, NLEVEL, P], U8)
        reset = put("reset", [P, T], F32)
        seq_sel = put("seq_sel", [P, NS], F32)
        mean_w = put("mean_w", [P, P], F32)
        assert cursor["at"] <= g_at + KT * 2 * T * 4

        acc = [ctx.enter_context(nc.psum_tensor(f"acc{n}", [P, 1024], F32)) for n in range(2)]
        bank = ctx.enter_context(nc.psum_tensor("bank", [P, 4, 512], F32))
        A0 = 512 - HALF

        cbal, cconv, cgla = 0, 8, 8 + 3 * KT
        NVEC = cgla + VV
        G4 = 4
        NXT = (NT + 1) * (KT // G4)

        S = {}

        def sem(name):
            S[name] = ctx.enter_context(nc.semaphore(name))
            return S[name]

        const_in, ident_in, g_in = sem("const_in"), sem("ident_in"), sem("g_in")
        x_in = [sem(f"x_in{n}") for n in range(NT + 1)]
        raw_in = [sem(f"raw_in{n}") for n in range(2)]
        lr_zero = sem("lr_zero")
        hi_ready, lo_ready, unit_done = sem("hi_ready"), sem("lo_ready"), sem("unit_done")
        act_freed, dve_freed = sem("act_freed"), sem("dve_freed")
        act_self, dve_self, passed = sem("act_self"), sem("dve_self"), sem("passed")
        sq_done, eps_set, rms_in, x_scaled, cst_t, cst_ready = (
            sem(n) for n in ("sq_done", "eps_set", "rms_in", "x_scaled", "cst_t", "cst_ready"))
        xt_done, h_hi, h_lo = sem("xt_done"), sem("h_hi"), sem("h_lo")
        lr_sum, w2_zero = sem("lr_sum"), sem("w2_zero")
        w2_in, logits, abs_done, neg_part, soft_part, cum_ready = (
            sem(n) for n in ("w2_in", "logits", "abs_done", "neg_part", "soft_part", "cum_ready"))
        eb_ready, qe_ready, kd_diff, kd_exp, kd_ready, kd_turned, kd_saved = (
            sem(n) for n in ("eb_ready", "qe_ready", "kd_diff", "kd_exp", "kd_ready", "kd_turned", "kd_saved"))
        lvl_diff, lvl_exp, lvl_ready, gram_done, lvl_merged = (
            sem(n) for n in ("lvl_diff", "lvl_exp", "lvl_ready", "gram_done", "lvl_merged"))
        v_turned, v_saved = sem("v_turned"), sem("v_saved")
        v2_hi, v2_ready = sem("v2_hi"), sem("v2_ready")
        state_hi, seq_split = sem("state_hi"), sem("seq_split")
        kd_hi, seq_kd, seq_mm, seq_upd = sem("kd_hi"), sem("seq_kd"), sem("seq_mm"), sem("seq_upd")
        st_in = [sem(f"st_in{n}") for n in range(2)]
        st_out = [sem(f"st_out{n}") for n in range(2)]
        inter_saved, chunk_mm, chunk_sq, chunk_state, sp_out = (
            sem(n) for n in ("inter_saved", "chunk_mm", "chunk_sq", "chunk_state", "sp_out"))
        ssq_ready, mean_mm, reps_set, o_ready = sem("ssq_ready"), sem("mean_mm"), sem("reps_set"), sem("o_ready")
        cg_sig, z_f32, z_hi, z_out = (
            sem(n) for n in ("cg_sig", "z_f32", "z_hi", "z_out"))
        tail_ready, tail_turned, tail_saved, tail_out = (
            sem(n) for n in ("tail_ready", "tail_turned", "tail_saved", "tail_out"))
        gate_out = [sem(f"gate_out{n}") for n in range(2)]
        xa_in, yb_in = sem("xa_in"), sem("yb_in")
        gate_in = [sem(f"gate_in{n}") for n in range(2)]
        ma_out = [sem(f"ma_out{n}") for n in range(2)]
        ma_in = [sem(f"ma_in{n}") for n in range(2)]
        mix_sum, mix_hi, mix_lo = sem("mix_sum"), sem("mix_hi"), sem("mix_lo")
        resid_in, out_turned, out_sum, squared, weighted, mean_sq, rms_out, y_rstd = (
            sem(n) for n in ("resid_in", "out_turned", "out_sum", "squared", "weighted", "mean_sq", "rms_out", "y_rstd"))
        y_dve, y_act, y_out_sp, y_out = sem("y_dve"), sem("y_act"), sem("y_out_sp"), sem("y_out")

        START = 1

        block = ctx.enter_context(nc.Block())

        U_BODY = 1
        U_A = U_BODY + H * NSTEP
        U_B = U_A + KT
        U_O = U_B + KT
        act_upto = [sum(LAST_READER.get(k) == "act" for k in STEPS[:s + 1]) for s in range(NSTEP)]
        dve_upto = [sum(LAST_READER.get(k) == "dve" for k in STEPS[:s + 1]) for s in range(NSTEP)]
        ACT_PER, DVE_PER = act_upto[-1], dve_upto[-1]
        ACT0 = 1

        def wait_turn(eng, s, value):
            eng.wait_ge(s, value)
            eng.sem_inc(passed, 1)

        def load_unit(sp, u, src, par):
            if not isinstance(u, int) or u >= 2:
                wait_turn(sp, lo_ready, u - 1 + START)
            k, c = src.shape[1], src.shape[2]
            sp.dma_start(raw[par][:, :].rearrange("p (k c) -> p k c", k=k), src).then_inc(raw_in[par], 16)

        def round_hi(act, u, par, turns):
            act.wait_ge(raw_in[par], 16 * turns)
            if not isinstance(u, int) or u >= 2:
                act.wait_ge(unit_done, u - 1 + START)
            nc.scalar.activation(w_hi[par][:, :], raw[par][:, :], ACT.Copy).then_inc(hi_ready, 1)

        def subtract_lo(dve, u, par):
            dve.wait_ge(hi_ready, u + 1)
            nc.vector.tensor_tensor(w_lo[par][:, :], raw[par][:, :], w_hi[par][:, :].bitcast(F32),
                                    ALU.subtract).then_inc(lo_ready, 1)

        PASSES = ((0, 0), (0, 1), (1, 0))

        def channel_unit(pe, u, par, x, last_tile=None):
            pe.wait_ge(lo_ready, u + 1 + START)
            out = acc[par]
            for k in range(KT):
                if last_tile and k == KT - 1:
                    pe.wait_ge(*last_tile)
                for n, (a, b) in enumerate(PASSES):
                    w = (w_hi, w_lo)[a][par][:, k * P:(k + 1) * P]
                    for j in range(2):
                        mm = nc.tensor.matmul(out[:, A0 + j * HALF:A0 + (j + 1) * HALF], w,
                                              x[:, k, b, j * HALF:(j + 1) * HALF],
                                              start=(k == 0 and n == 0), stop=(k == KT - 1 and n == 2))
            mm.then_inc(unit_done, 1)

        def par_of(s):
            return (U_BODY + s) % 2

        def turns_of(i, u_lit, per):
            return (per // 2) * i + (u_lit // 2 + 1)

        @block.sync
        def _(sp):
            sp.dma_start(ident[:, :], const_f32[:, 0:P]).then_inc(ident_in, 16)
            sp.dma_start(x_rows[:, 0, :], x_prompt[0, 0:P, :]).then_inc(x_in[0], 16)
            sp.dma_start(g_rows[:, :], norm_g[0].partition_broadcast(P)).then_inc(g_in, 16)
            for t in range(1, NT):
                sp.dma_start(x_rows[:, t, :], x_prompt[0, t * P:(t + 1) * P, :]).then_inc(x_in[t], 16)
            sp.dma_start(x_rows[0:TS, NT, :], xs_rows).then_inc(x_in[NT], 16)
            sp.wait_ge(lr_zero, 1)
            sp.dma_start(raw[0][:, :].rearrange("p (k c) -> p k c", k=KT)[:, :, 0:RANK],
                         w_in_k[:, :, c_lr:c_lr + RANK]).then_inc(raw_in[0], 16)

            def step_src(i, s):
                kind = STEPS[s]
                n = s - STEPS.index(kind)
                if kind in ("q", "k"):
                    c = (c_q if kind == "q" else c_k) + n * P + i * DK
                    return w_in_k[:, :, bass.ds(c, P)]
                if kind == "v":
                    return w_in_k[:, :, bass.ds(i * DV + (c_v + n * P), P)]
                if kind.startswith("conv"):
                    n //= 4
                c0 = {"conv_c": c_cc, "conv_x": c_cx, "conv_b": c_cb, "conv_g": c_cg,
                      "gla_gate": c_gg, "gate_a": c_ga, "gate_b": c_gb}[kind]
                return w_in_k[:, :, bass.ds(i * (CH * P) + (c0 + n * P), P)]

            with sp.Fori(0, H) as i:
                for s in range(NSTEP):
                    load_unit(sp, i * NSTEP + (U_BODY + s), step_src(i, s), par_of(s))
            for u0, w in ((U_A, w_a_k), (U_B, w_b_k), (U_O, w_o_k)):
                with sp.Fori(0, KT // 2) as i:
                    for n in range(2):
                        load_unit(sp, i * 2 + (u0 + n), w[:, :, bass.ds(i * (2 * P) + n * P, P)], (u0 + n) % 2)
            for t in SCALED_BY_DVE:
                sp.wait_ge(y_dve, SCALED_BY_DVE.index(t) + 1)
                sp.dma_start(y_prompt[0, t * P:(t + 1) * P, :], resid[:, t, :]).then_inc(y_out_sp, 16)
            sp.wait_ge(y_out_sp, 16 * len(SCALED_BY_DVE))

        @block.gpsimd
        def _(pool):
            nc.gpsimd.memset(raw[0][:, :], 0.0).then_inc(lr_zero, 1)
            pool.dma_start(vec_rows[cbal:cbal + 8, :], b_alpha[0].rearrange("(k p) -> k p", p=P)).then_inc(const_in, 16)
            pool.dma_start(vec_rows[cconv:cconv + 3 * KT, :],
                           conv_w[0].rearrange("j (k p) -> (j k) p", p=P)).then_inc(const_in, 16)
            pool.dma_start(vec_rows[cgla:cgla + VV, :],
                           gla_norm_g[0].rearrange("(k p) -> k p", p=P)).then_inc(const_in, 16)
            pool.dma_start(conv_rows[:, :], state_conv[0].rearrange("s r d -> (s r) d")).then_inc(const_in, 16)
            pool.dma_start(reset[:, :], const_f32[:, P:P + T]).then_inc(const_in, 16)
            pool.dma_start(seq_sel[:, :], const_f32[:, P + T:P + T + NS]).then_inc(const_in, 16)
            mask_stage = mix_tile[:, :, :].rearrange("p a t -> p (a t)")[:, 0:NLEVEL * P]
            pool.dma_start(mask_stage, const_f32[:, P + T + NS:P + T + NS + NLEVEL * P]).then_inc(const_in, 16)
            pool.wait_ge(const_in, 16 * 7)
            pool.wait_ge(xt_done, NXT)
            pool.wait_ge(cst_ready, 1)
            nc.gpsimd.memset(w2h[:, :], 0.0).then_inc(w2_zero, 1)
            pool.wait_ge(w2_zero, 1)
            def head(i, last):
                for r0 in (0, LR_LO):
                    pool.dma_start(w2h[r0:r0 + RANK, :], w_alpha2[0, :, bass.ds(i * DK, DK)]).then_inc(w2_in, 16)

                def load_state(j):
                    if j >= 2:
                        wait_turn(pool, st_out[j % 2], i * (8 * NS) + 16 * (j // 2))
                    pool.dma_start(states[:, j % 2, :, :],
                                   state_gla[0, j, bass.ds(i, 1), :, :].rearrange("h (k p) v -> p (h k) v", p=P)
                                   ).then_inc(st_in[j % 2], 16)

                def wait_z(m):
                    step = STEPS.index("conv_g") + 4 * m if m < 4 else STEPS.index("gla_gate") + m - 4
                    wait_turn(pool, dve_freed, i * DVE_PER + dve_upto[step] + START)

                load_state(0)
                load_state(1)
                for j in range(NS):
                    wait_turn(pool, seq_upd, i * NS + (j + 1))
                    pool.dma_start(new_gla_sample[0, j, bass.ds(i, 1), :, :].rearrange("h (k p) v -> p (h k) v", p=P),
                                   states[:, j % 2, :, :]).then_inc(st_out[j % 2], 16)
                    if j + 2 < NS:
                        load_state(j + 2)
                    if j in (2, 6):
                        n = j // 4
                        wait_z(n)
                        pool.dma_start(za_d[bass.ds(i * CH + n, 1)].rearrange("k p h t -> p (k h) t"),
                                       z_tile[:, :, :]).then_inc(z_out, 16)
                for n in (2, 3):
                    wait_z(n)
                    pool.dma_start(za_d[bass.ds(i * CH + n, 1)].rearrange("k p h t -> p (k h) t"),
                                   z_tile[:, :, :]).then_inc(z_out, 16)
                    if n == 2:
                        wait_turn(pool, chunk_state, i * NT + NT)
                        pool.dma_start(new_gla_prompt[0, 0, bass.ds(i, 1), :, :].rearrange("h (k p) v -> p (h k) v", p=P),
                                       s_prompt[:, :, :]).then_inc(sp_out, 16)
                for n in range(4):
                    wait_z(4 + n)
                    pool.dma_start(zb_d[bass.ds(i * CH + n, 1)].rearrange("k p h t -> p (k h) t"),
                                   z_tile[:, :, :]).then_inc(z_out, 16)
                    if n == 0:
                        wait_turn(pool, tail_saved, i + 1)
                        pool.dma_start(new_conv_prompt[0, 0, :, bass.ds(i * (CH * P), CH * P)],
                                       mix_tile[0:2, 0, 0:CH * P]).then_inc(tail_out, 16)
                        pool.dma_start(new_conv_sample[0, :, :, bass.ds(i * (CH * P), CH * P)].rearrange("s r d -> (s r) d"),
                                       mix_tile[2:2 + 2 * NS, 0, 0:CH * P]).then_inc(tail_out, 16)
                for n in range(8):
                    wait_turn(pool, act_freed, i * ACT_PER + (ACT0 + act_upto[STEPS.index("gate_a") + n]) + START)
                    pool.dma_start(gate_d[n // 4, bass.ds(i * CH + n % 4, 1)].rearrange("k p t -> p (k t)"),
                                   gate_tile[:, n % 2, :]).then_inc(gate_out[n % 2], 16)
                    if n == 0:
                        wait_turn(pool, z_out, i * 128 + 128)
                        wait_turn(pool, sp_out, i * 16 + 16)
                        wait_turn(pool, tail_out, i * 32 + 32)
                        wait_turn(pool, st_out[0], i * (8 * NS) + 8 * NS)
                        wait_turn(pool, st_out[1], i * (8 * NS) + 8 * NS)
                    if last and XA_STEP * n < KT:
                        k0, k1 = XA_STEP * n, min(XA_STEP * (n + 1), KT)
                        pool.dma_start(act_x[:, k0:k1, :, :].rearrange("p k h t -> p k (h t)"),
                                       za_d[k0:k1].rearrange("k p h t -> p k (h t)")).then_inc(xa_in, 16)
                wait_turn(pool, gate_out[0], i * 64 + 64)
                wait_turn(pool, gate_out[1], i * 64 + 64)
            with pool.Fori(0, H - 1) as i:
                head(i, False)
            head(H - 1, True)
            pool.wait_ge(unit_done, U_A + START)
            for n in range(2):
                pool.dma_start(gate_tile[:, n, :], gate_d[0, n]).then_inc(gate_in[n], 16)
            with pool.Fori(0, KT // 2) as i:
                pool.dma_start(act_y[:, bass.ds(i * 2, 2), :, :].rearrange("p k h t -> p k (h t)"),
                               zb_d[bass.ds(i * 2, 2)].rearrange("k p h t -> p k (h t)")).then_inc(yb_in, 16)
                for n in range(2):
                    wait_turn(pool, dve_freed, i * 2 + (H * DVE_PER + n + 1) + START)
                    pool.dma_start(ma_d[bass.ds(i * 2 + n, 1)].rearrange("k p t -> p (k t)"),
                                   mix_tile[:, n, :]).then_inc(ma_out[n], 16)
                    wait_turn(pool, ma_out[n], i * 16 + 16)
                    pool.dma_start(gate_tile[:, n, :],
                                   gate_d.rearrange("g k p t -> (g k) p t")[bass.ds(i * 2 + (n + 2), 1)]
                                   .rearrange("k p t -> p (k t)")).then_inc(gate_in[n], 16)
            for n in range(2):
                pool.wait_ge(ma_out[n], 16 * (KT // 2))
                pool.dma_start(mix_tile[:, n, :], ma_d[n]).then_inc(ma_in[n], 16)

            def next_b(i, n):
                wait_turn(pool, mix_lo, i * 2 + (n + 1))
                pool.dma_start(mix_tile[:, n, :], ma_d[bass.ds(i * 2 + (n + 2), 1)].rearrange("k p t -> p (k t)")
                               ).then_inc(ma_in[n], 16)
                pool.dma_start(gate_tile[:, n, :], gate_d[1, bass.ds(i * 2 + (n + 2), 1)].rearrange("k p t -> p (k t)")
                               ).then_inc(gate_in[n], 16)

            with pool.Fori(0, KT // 2 - 1) as i:
                for n in range(2):
                    next_b(i, n)
            pool.wait_ge(unit_done, U_O + START)
            for t in range(NT):
                pool.dma_start(resid[:, t, :], x_prompt[0, t * P:(t + 1) * P, :]).then_inc(resid_in, 16)
            pool.dma_start(resid[0:S0, NT, :], x_prompt[0, LAST:TP, :]).then_inc(resid_in, 16)
            pool.dma_start(resid[S0:P, NT, :], xs_rows).then_inc(resid_in, 16)
            pool.dma_start(gfin[:, :], final_norm_g.partition_broadcast(P)).then_inc(resid_in, 16)
            for t in SCALED_BY_ACT:
                pool.wait_ge(y_act, SCALED_BY_ACT.index(t) + 1)
                if t < NT:
                    pool.dma_start(y_prompt[0, t * P:(t + 1) * P, :], resid[:, t, :]).then_inc(y_out, 16)
                else:
                    pool.dma_start(ys_rows, resid[S0:P, NT, :]).then_inc(y_out, 16)
            pool.wait_ge(y_out, 16 * len(SCALED_BY_ACT))

        def queries(tokens, l):
            if l == len(LEVELS):
                return tokens
            B = LEVELS[l]
            return tokens.rearrange("p (c n) -> p c n", n=2 * B)[:, :, B:2 * B]

        def row_blocks(g):
            W = TS // 2
            return [slice(r, r + W) for r in (S0 + g * W, g * W, P - (g + 1) * W, (1 - g) * W)]

        def key_rows(l):
            return P if l == len(LEVELS) else P - LEVELS[l]

        def prompt_blocks(t, n):
            return t[:, :, 0:TP].rearrange("p k (c n) -> p k c n", n=n)

        def sample_blocks(t, n):
            return t[:, :, TP:T].rearrange("p k (c n) -> p k c n", n=n)

        def lr_parts(h):
            prompt = bank[:, 2:4, :].rearrange("p b (q h t) -> p (b q) h t", q=2, h=2)
            return prompt[:, :, h, :], bank[:, 0, h * TS:(h + 1) * TS]

        @block.scalar
        def _(act):
            A = nc.scalar.activation
            act.sem_inc(act_freed, START)
            def row_root(t):
                n = P if t < NT else TS
                act.wait_ge(x_in[t], 16)
                if t:
                    act.wait_ge(sq_done, t)
                A(w_lo[1][0:n, :], x_rows[0:n, t, :], ACT.Square,
                  accum_out=stat[0:n, t:t + 1]).then_inc(sq_done, 1)
                act.wait_ge(sq_done, t + 1)
                A(stat[0:n, 16 + t:17 + t], stat[0:n, t:t + 1], ACT.Sqrt, bias=eps[0:n, :], scale=1.0 / D
                  ).then_inc(rms_in, 1)

            act.wait_ge(eps_set, 1)
            A(stat[:, 40:41], eps[:, :], ACT.Sqrt)
            row_root(0)
            row_root(1)
            for t in range(NT + 1):
                if t + 2 <= NT:
                    row_root(t + 2)
                if t == 1:
                    round_hi(act, 0, 0, 1)
                if t == NT:
                    round_hi(act, 1, 1, 1)
                n = P if t < NT else TS
                for g in range(KT // G4):
                    act.wait_ge(xt_done, t * (KT // G4) + g + 1)
                    A(act_y[:, g * G4:(g + 1) * G4, 0, t * P:t * P + n],
                      acc[g // 2][:, g % 2 * 512:g % 2 * 512 + G4 * n].rearrange("p (k t) -> p k t", k=G4),
                      ACT.Copy).then_inc(h_hi, 1)
            act.wait_ge(unit_done, 1 + START)
            A(lr_t[:, 0:TP].rearrange("p (c t) -> p c t", c=NT), lr_parts(0)[0], ACT.Copy)
            A(lr_t[:, TP:T], lr_parts(0)[1], ACT.Copy).then_inc(act_freed, 1)

            with act.Fori(0, H) as i:
                for s, kind in enumerate(STEPS):
                    n = s - STEPS.index(kind)
                    u1 = i * NSTEP + (U_BODY + s + 1)
                    par = par_of(s)
                    out = acc[par][:, A0:A0 + T]
                    if 9 <= s <= 16:
                        j = s - 9
                        if j == 0:
                            act.wait_ge(w2_in, i * 32 + 32)
                        else:
                            act.wait_ge(seq_mm, i * NS + j)
                        act.wait_ge(st_in[j % 2], i * (8 * NS) + 16 * (j // 2 + 1))
                        A(s_hi[:, :, :], states[:, j % 2, :, :], ACT.Copy).then_inc(state_hi, 1)
                    round_hi(act, u1, par_of(s + 1), turns_of(i, U_BODY + s + 1, NSTEP))
                    act.wait_ge(unit_done, i * NSTEP + (U_BODY + s + 1) + START)
                    if kind == "q":
                        A(qk[:, 0, n, :], out, ACT.Copy, scale=DK ** -0.5).then_inc(act_freed, 1)
                    if kind == "k":
                        A(qk[:, 1, n, :], out, ACT.Copy).then_inc(act_freed, 1)
                    if kind == "v":
                        if n < 2:
                            act.wait_ge(dve_freed, i * DVE_PER + START)
                        else:
                            act.wait_ge(v_turned, i * VV + (n - 1))
                        A(mix_tile[:, n % 2, :], out, ACT.Copy).then_inc(act_freed, 1)
                    if kind in ("conv_c", "conv_g", "gla_gate"):
                        act.wait_ge(dve_freed, i * DVE_PER + dve_upto[s - 1] + START)
                    if s == 8:
                        act.wait_ge(v_turned, i * VV + (VV - 1))
                    if kind == "conv_c":
                        A(mix_tile[:, 0, :], out, ACT.Copy).then_inc(act_freed, 1)
                    if kind == "conv_g":
                        A(mix_tile[:, 0, :], out, ACT.Sigmoid).then_inc(cg_sig, 1)
                    if kind == "gla_gate":
                        A(mix_tile[:, 1, :], out, ACT.Sigmoid).then_inc(cg_sig, 1)
                    if kind in ("conv_g", "gla_gate"):
                        m = n // 4 if kind == "conv_g" else 4 + n
                        act.wait_ge(z_f32, i * 8 + (m + 1))
                        if m:
                            act.wait_ge(z_out, i * 128 + 16 * m)
                        A(z_tile[:, 0, :], mix_tile[:, 1, :], ACT.Copy).then_inc(z_hi, 1)
                    if kind in ("gate_a", "gate_b"):
                        m = n if kind == "gate_a" else 4 + n
                        if m >= 2:
                            act.wait_ge(gate_out[m % 2], i * 64 + 16 * (m // 2))
                        else:
                            act.wait_ge(w2_in, i * 32 + 32)
                        A(gate_tile[:, m % 2, :], out, ACT.Sigmoid).then_inc(act_freed, 1)

                    if s == 1:
                        act.wait_ge(logits, i + 1)
                        for kk in range(KK):
                            ap = bank[:, 2 * kk:2 * kk + 2, :].rearrange("p b c -> p (b c)")[:, A0:A0 + T]
                            ins = A(dec[:, kk, :], ap, ACT.Abs, bias=cvec[:, bass.ds(i * KK + (cbal + kk), 1)])
                        ins.then_inc(abs_done, 1)
                        act.wait_ge(abs_done, i + 1)
                        A(dec[:, :, :], dec[:, :, :], ACT.Exp, scale=-1.0).then_inc(act_self, 1)
                        act.wait_ge(act_self, i + 1)
                        A(dec[:, :, :], dec[:, :, :], ACT.Ln, bias=1.0).then_inc(soft_part, 1)
                    if s == 2:
                        act.wait_ge(cum_ready, i + 1)
                        A(decay_end[:, :, 0:NT], prompt_blocks(cum, P)[:, :, :, P - 1], ACT.Exp, scale=1 / TAU)
                        A(decay_end[:, :, NT:NB], sample_blocks(cum, LS)[:, :, :, LS - 1], ACT.Exp, scale=1 / TAU)
                        A(qe[:, :, :], cum[:, :, :], ACT.Exp, scale=1 / TAU).then_inc(eb_ready, 1)
                    if s == 3:
                        act.wait_ge(kd_diff, i + 1)
                        A(dec[:, :, :], dec[:, :, :], ACT.Exp, scale=-1 / TAU).then_inc(kd_exp, 1)
                    if s == 4:
                        act.wait_ge(kd_turned, i + 1)
                        A(kd_rows[:, 0:NT, :], bank[:, 0:2, :], ACT.Copy)
                        A(kd_rows[S0:P, NT, :], bank[S0:P, 2, 0:DK], ACT.Copy).then_inc(kd_saved, 1)
                    if s == 8:
                        act.wait_ge(v_saved, i * VV + VV)
                        for g in range(2):
                            own, under, _, _ = row_blocks(g)
                            A(v2[own, g, :], v_rows[own, NT, :], ACT.Copy)
                            ins = A(v2[under, g, :], v_rows[own, NT, :], ACT.Copy)
                        ins.then_inc(v2_hi, 1)
                    if s in SEQ_STEP:
                        j = SEQ_STEP.index(s)
                        act.wait_ge(kd_saved, i + 1)
                        if j >= 2:
                            act.wait_ge(seq_mm, i * NS + (j - 1))
                        own, _, by_lo, _ = row_blocks(j // (NS // 2))
                        for rows in (own, by_lo):
                            ins = A(kd_seq[rows, j % 2, :], kd_rows[own, NT, :], ACT.Copy, scale=seq_sel[own, j:j + 1])
                        ins.then_inc(kd_hi, 1)
                    if s == 7 or 9 <= s < 8 + len(LEVELS):
                        l = 0 if s == 7 else s - 8
                        act.wait_ge(lvl_diff, i * len(LEVELS) + (l + 1))
                        for half, sign in ((0, -1), (1, 1)):
                            B = LEVELS[l]
                            tt = T if 2 * B <= LS else TP
                            ap = dec[:, :, 0:tt].rearrange("p k (c n) -> p k c n", n=2 * B)[
                                :, :, :, half * B:(half + 1) * B]
                            ins = A(ap, ap, ACT.Exp, scale=sign / TAU)
                        ins.then_inc(lvl_exp, 1)
                    if s == 16:
                        act.wait_ge(seq_mm, i * NS + NS)
                        A(q_state[:, :], bank[:, 2, :], ACT.Copy).then_inc(inter_saved, 1)
                    if 17 <= s < 17 + NT:
                        c = s - 17
                        act.wait_ge(chunk_mm, i * (NT + 1) + (c + 1))
                        ap = bank[:, 2, :].rearrange("p (v t) -> p v t", v=VV)
                        if c:
                            act.wait_ge(ssq_ready, i * (NT + 1) + c)
                        A(dec[:, 0, 0:512].rearrange("p (v t) -> p v t", v=VV), ap, ACT.Square)
                        A(o_t[:, :, c * P:(c + 1) * P], ap, ACT.Copy).then_inc(chunk_sq, 1)
                    if 18 <= s <= 18 + NT:
                        c = s - 18
                        w = P if c < NT else TS
                        act.wait_ge(mean_mm, i * (NT + 1) + (c + 1))
                        A(rstd[:, 0:w], bank[:, 3, 0:w], ACT.Sqrt, bias=eps[:, :]).then_inc(reps_set, 1)
                    if kind == "gate_b" and n == 0:
                        act.wait_ge(z_out, i * 128 + 128)
                    if s == 24:
                        act.wait_ge(tail_turned, i + 1)
                        A(mix_tile[0:2 * NS + 2, 0, 0:CH * P], bank[0:2 * NS + 2, 0, :], ACT.Copy).then_inc(tail_saved, 1)
            with act.Fori(0, KT // 2) as i:
                for n in range(2):
                    u1 = U_A + n + 1
                    round_hi(act, i * 2 + u1, u1 % 2, turns_of(i, u1, 2))
            with act.Fori(0, KT // 2) as i:
                for n in range(2):
                    u1 = U_B + n + 1
                    round_hi(act, i * 2 + u1, u1 % 2, turns_of(i, u1, 2))
                    act.wait_ge(mix_sum, i * 2 + (n + 1))
                    A(act_x[:, bass.ds(i * 2 + n, 1), 0, :].rearrange("p k t -> p (k t)"), gate_tile[:, n, :],
                      ACT.Copy).then_inc(mix_hi, 1)

            def squares(m):
                act.wait_ge(out_sum, m + 1 + START)
                if not isinstance(m, int) or m >= 1:
                    act.wait_ge(squared, m)
                for t in range(NT + 1):
                    ins = A(mix_tile[:, :, :].rearrange("p a t -> p (a t)")[:, t * P:(t + 1) * P],
                            resid[:, t, bass.ds(m * P, P)], ACT.Square,
                            accum_out=parts[:, bass.ds(m * (NT + 1) + t, 1)])
                ins.then_inc(squared, 1)

            def out_tiles(i, first, last):
                for n in range(2):
                    u1 = U_O + n + 1
                    if not (last and n == 1):
                        round_hi(act, i * 2 + u1, u1 % 2, turns_of(i, u1, 2))
                    act.wait_ge(unit_done, i * 2 + u1 + START)
                    if not first:
                        act.wait_ge(out_turned, i * 2 + (n - 1))
                    A(gate_tile[:, n, :], acc[(U_O + n) % 2][:, A0:A0 + T], ACT.Copy).then_inc(act_freed, 1)
                    if not (first and n == 0):
                        squares(i * 2 + (n - 1))

            A(stat[:, 40:41], eps[:, :], ACT.Sqrt)
            out_tiles(0, True, False)
            with act.Fori(1, KT // 2 - 1) as i:
                out_tiles(i, False, False)
            out_tiles(KT // 2 - 1, False, True)
            squares(KT - 1)
            act.wait_ge(mean_sq, 1)
            A(stat[:, 16:16 + NT + 1], stat[:, 8:8 + NT + 1], ACT.Sqrt).then_inc(rms_out, 1)
            act.wait_ge(y_rstd, 1)
            act.wait_ge(weighted, KT)
            for t in SCALED_BY_ACT:
                A(resid[:, t, :], resid[:, t, :], ACT.Copy, scale=stat[:, 24 + t:25 + t]).then_inc(y_act, 1)

        @block.tensor
        def _(pe):
            pe.sem_inc(unit_done, START)
            pe.wait_ge(ident_in, 16)

            def forget_code(t):
                n = P if t < NT else TS
                out = bank[:, 2 + t // 2, t % 2 * 256:t % 2 * 256 + 2 * n] if t < NT else bank[:, 0, 0:2 * n]
                for k in range(KT):
                    mm = nc.tensor.matmul(out, w_hi[0][:, k * P:(k + 1) * P],
                                          act_y[:, k, :, t * P:t * P + n], start=(k == 0), stop=(k == KT - 1))
                return mm

            def stay_warm(n):
                for _ in range(n):
                    nc.tensor.transpose(bank[:, 0, 0:P], ident[:, :], ident[:, :])

            WARM = (40, 10, 8, 5, 0)
            for t in range(NT + 1):
                n = P if t < NT else TS
                stay_warm(WARM[t])
                pe.wait_ge(x_scaled, t + 1)
                for g in range(KT // G4):
                    if t:
                        pe.wait_ge(h_lo, (t - 1) * (KT // G4) + g + 1)
                    for k in range(G4):
                        o = g % 2 * 512 + k * n
                        tr = nc.tensor.transpose(acc[g // 2][:, o:o + n],
                                                 x_rows[0:n, t, (g * G4 + k) * P:(g * G4 + k + 1) * P],
                                                 ident[0:n, 0:n])
                    tr.then_inc(xt_done, 1)
                if t == 1:
                    pe.wait_ge(lo_ready, 1 + START)
                if t:
                    forget_code(t - 1)
            pe.wait_ge(const_in, 16 * 7)
            nc.tensor.transpose(bank[:, 1, 256:256 + NVEC], vec_rows[0:NVEC, :], ident[0:NVEC, 0:NVEC])
            for k in range(KT):
                tr = nc.tensor.transpose(bank[:, 1, k * 2 * NS:(k + 1) * 2 * NS], conv_rows[:, k * P:(k + 1) * P],
                                         ident[0:2 * NS, 0:2 * NS])
            tr.then_inc(cst_t, 1)
            pe.wait_ge(h_lo, NXT)
            forget_code(NT).then_inc(unit_done, 1)

            with pe.Fori(0, H) as i:
                for s, kind in enumerate(STEPS):
                    u, par = i * NSTEP + (U_BODY + s), par_of(s)
                    n = s - STEPS.index(kind)
                    if s >= 2:
                        k2, back = s - 2, 0
                    else:
                        k2, back = s - 2 + NSTEP, 1
                    if LAST_READER[STEPS[k2]] == "act":
                        pe.wait_ge(act_freed, i * ACT_PER + (ACT0 + act_upto[k2] - back * ACT_PER) + START)
                    else:
                        pe.wait_ge(dve_freed, i * DVE_PER + (dve_upto[k2] - back * DVE_PER) + START)
                    channel_unit(pe, u, par, act_y)

                    if s == 1:
                        pe.wait_ge(w2_in, i * 32 + 32)
                        pe.wait_ge(lr_sum, 1)
                        for kk in range(KK):
                            ap = bank[:, 2 * kk:2 * kk + 2, :].rearrange("p b c -> p (b c)")
                            for j in range(2):
                                mm = nc.tensor.matmul(ap[:, A0 + j * HALF:A0 + (j + 1) * HALF],
                                                      w2h[:, kk * P:(kk + 1) * P],
                                                      lr_t[0:LR_LO + RANK, j * HALF:(j + 1) * HALF], start=True, stop=True)
                        mm.then_inc(logits, 1)
                    if 5 <= s <= 8:
                        m = s - 5
                        pe.wait_ge(act_freed, i * ACT_PER + (ACT0 + act_upto[s - 1]) + START)
                        if m == 0:
                            pe.wait_ge(kd_saved, i + 1)
                        if m >= 2:
                            pe.wait_ge(v_saved, i * VV + (m - 1))
                        for c in range(NT + 1):
                            t0 = c * P if c < NT else LAST
                            b, o = 2 * (m % 2) + c // 4, c % 4 * P
                            tr = nc.tensor.transpose(bank[:, b, o:o + P], mix_tile[:, m % 2, t0:t0 + P], ident[:, :])
                        tr.then_inc(v_turned, 1)
                    if s == 4:
                        pe.wait_ge(kd_ready, i + 1)
                        for c in range(NT + 1):
                            t0 = c * P if c < NT else LAST
                            for kk in range(KK):
                                o = (c * KK + kk) * P
                                tr = nc.tensor.transpose(bank[:, o // 512, o % 512:o % 512 + P],
                                                         dec[:, kk, t0:t0 + P], ident[:, :])
                        tr.then_inc(kd_turned, 1)
                    if 9 <= s <= 16:
                        l = j = s - 9
                        if l:
                            pe.wait_ge(lvl_merged, i * NLEVEL + l)
                        if j == 0:
                            pe.wait_ge(qe_ready, i + 1)
                            pe.wait_ge(v2_ready, i + 1)
                        pe.wait_ge(seq_kd, i * NS + (j + 1))
                        if j:
                            pe.wait_ge(seq_upd, i * NS + j)
                        pe.wait_ge(seq_split, i * NS + (j + 1))
                        for kk in range(KK):
                            for n2, st in enumerate((s_hi, s_lo)):
                                nc.tensor.matmul(bank[:, 2, :], q_seq[:, kk, :], st[:, kk, :],
                                                 start=(j == 0 and kk == 0 and n2 == 0),
                                                 stop=(j == NS - 1 and kk == KK - 1 and n2 == 1))
                        for kk in range(KK):
                            mm = nc.tensor.matmul(bank[:, kk, :], kd_seq[:, j % 2, kk * P:(kk + 1) * P],
                                                  v2[:, j // (NS // 2), :], start=True, stop=True)
                        mm.then_inc(seq_mm, 1)
                        if l < len(LEVELS):
                            pe.wait_ge(lvl_ready, i * len(LEVELS) + (l + 1))
                            key = qry = dec
                        else:
                            key, qry = qk[:, 1], qk[:, 0]
                        for c in range(NT):
                            for kk in range(KK):
                                qs = queries(qry[:, kk, c * P:(c + 1) * P], l)
                                w = P if l == len(LEVELS) else P // 2
                                mm = nc.tensor.matmul(bank[0:key_rows(l), 3, c * w:(c + 1) * w],
                                                      key[:, kk, c * P:c * P + key_rows(l)], qs,
                                                      start=(kk == 0), stop=(kk == KK - 1))
                        if l < len(LEVELS) and 2 * LEVELS[l] <= LS:
                            for kk in range(KK):
                                mm = nc.tensor.matmul(bank[:, 3, G_S:G_S + TS // 2], key[:, kk, LAST:T],
                                                      queries(qry[:, kk, TP:T], l),
                                                      start=(kk == 0), stop=(kk == KK - 1))
                        if l == len(LEVELS) - 1:
                            for kk in range(KK):
                                mm = nc.tensor.matmul(bank[:, 3, G_S + TS:G_S + 2 * TS], qk[:, 1, kk, LAST:T],
                                                      qk[:, 0, kk, TP:T], start=(kk == 0), stop=(kk == KK - 1))
                        mm.then_inc(gram_done, 1)
                    if 17 <= s <= 17 + NT:
                        c = s - 17
                        if c == 0:
                            pe.wait_ge(inter_saved, i + 1)
                            pe.wait_ge(lvl_merged, i * NLEVEL + NLEVEL)
                            pe.wait_ge(seq_upd, i * NS + NS)
                        else:
                            pe.wait_ge(chunk_sq, i * NT + c)
                            pe.wait_ge(chunk_state, i * NT + c)
                        if c < NT:
                            for v in range(VV):
                                out = bank[:, 2, v * P:(v + 1) * P]
                                nc.tensor.matmul(out, v_rows[:, c, v * P:(v + 1) * P], scores[:, c * P:(c + 1) * P],
                                                 start=True, stop=(c == 0))
                                for kk in range(KK if c else 0):
                                    nc.tensor.matmul(out, s_prompt[:, kk, v * P:(v + 1) * P],
                                                     qe[:, kk, c * P:(c + 1) * P], start=False, stop=(kk == KK - 1))
                            for kk in range(KK):
                                mm = nc.tensor.matmul(bank[:, kk, :], kd_rows[:, c, kk * P:(kk + 1) * P],
                                                      v_rows[:, c, :], start=True, stop=True)
                        else:
                            for v in range(VV):
                                out = bank[:, 2, v * TS:(v + 1) * TS]
                                nc.tensor.matmul(out, q_state[:, v * P:(v + 1) * P], pair[:, :], start=True, stop=False)
                                mm = nc.tensor.matmul(out, v_rows[S0:P, NT, v * P:(v + 1) * P], scores[S0:P, TP:T],
                                                      start=False, stop=True)
                        mm.then_inc(chunk_mm, 1)
                    if 18 <= s <= 18 + NT:
                        c = s - 18
                        w = P if c < NT else TS
                        pe.wait_ge(ssq_ready, i * (NT + 1) + (c + 1))
                        if c:
                            pe.wait_ge(o_ready, i * (NT + 1) + c)
                        nc.tensor.matmul(bank[:, 3, 0:w], mean_w[:, :], ssq[:, 0:w], start=True, stop=True
                                         ).then_inc(mean_mm, 1)
                    if s == 24:
                        pe.wait_ge(tail_ready, i * CH + CH)
                        for c in range(CH):
                            tr = nc.tensor.transpose(bank[0:2 * NS + 2, 0, c * P:(c + 1) * P],
                                                     conv_tail[:, c, :], ident[:, :])
                        tr.then_inc(tail_turned, 1)

            pe.wait_ge(xa_in, 16 * -(-KT // XA_STEP))
            with pe.Fori(0, KT // 2) as i:
                for n in range(2):
                    pe.wait_ge(act_freed, ACT0 + H * ACT_PER + START)
                    if n == 0:
                        pe.wait_ge(dve_freed, i * 2 + (H * DVE_PER - 1) + START)
                    else:
                        pe.wait_ge(dve_freed, i * 2 + H * DVE_PER + START)
                    channel_unit(pe, i * 2 + (U_A + n), (U_A + n) % 2, act_x)
            pe.wait_ge(yb_in, 16 * (KT // 2))
            with pe.Fori(0, KT // 2) as i:
                for n in range(2):
                    pe.wait_ge(dve_freed, i * 2 + (H * DVE_PER + KT + n - 1) + START)
                    channel_unit(pe, i * 2 + (U_B + n), (U_B + n) % 2, act_y)
            def turn_out(m, n, reused):
                pe.wait_ge(act_freed, m + (ACT0 + H * ACT_PER + 1) + START)
                if reused:
                    pe.wait_ge(out_sum, m - 1 + START)
                for c in range(NT + 1):
                    t0 = c * P if c < NT else LAST
                    b, o = 2 * n + c // 4, c % 4 * P
                    tr = nc.tensor.transpose(bank[:, b, o:o + P], gate_tile[:, n, t0:t0 + P], ident[:, :])
                tr.then_inc(out_turned, 1)

            def out_tiles(i, first):
                for n in range(2):
                    u = i * 2 + (U_O + n)
                    if first:
                        pe.wait_ge(dve_freed, H * DVE_PER + 2 * KT - 1 + n + START)
                        channel_unit(pe, u, (U_O + n) % 2, act_x, (mix_lo, KT))
                    else:
                        pe.wait_ge(act_freed, i * 2 + (ACT0 + H * ACT_PER + n - 1) + START)
                        channel_unit(pe, u, (U_O + n) % 2, act_x)
                    if not (first and n == 0):
                        turn_out(i * 2 + (n - 1), 1 - n, not first)

            out_tiles(0, True)
            with pe.Fori(1, KT // 2) as i:
                out_tiles(i, False)
            turn_out(KT - 1, 1, True)

        @block.vector
        def _(dve):
            V = nc.vector
            for sm in (lo_ready, dve_freed, out_sum):
                dve.sem_inc(sm, START)
            V.memset(eps[:, :], EPS).then_inc(eps_set, 1)
            count = [0]
            base = [0]

            def link(ins):
                count[0] += 1
                ins.then_inc(dve_self, 1)
                dve.wait_ge(dve_self, base[0] + count[0])

            def refined(root, ms, eps_ap, one, two):
                link(V.reciprocal(one, root))
                if eps_ap is None:
                    link(V.tensor_tensor(two, ms, one, ALU.mult))
                else:
                    link(V.scalar_tensor_tensor(out=two, in0=ms, scalar=eps_ap, in1=one, op0=ALU.add, op1=ALU.mult))
                link(V.tensor_tensor(two, two, one, ALU.mult))
                link(V.tensor_scalar(two, two, -0.5, 1.5, ALU.mult, ALU.add))
                link(V.tensor_tensor(one, one, two, ALU.mult))

            dve.wait_ge(ident_in, 16)
            V.tensor_tensor(pair[:, :], ident[:, 0:TS], ident[:, TS:P], ALU.add)
            V.memset(mean_w[:, :], 1.0 / DV)

            def scale_rows(t):
                n = P if t < NT else TS
                dve.wait_ge(rms_in, t + 1)
                link(V.tensor_scalar(stat[0:n, 8 + t:9 + t], stat[0:n, t:t + 1], 1.0 / D, EPS, ALU.mult, ALU.add))
                refined(stat[0:n, 16 + t:17 + t], stat[0:n, 8 + t:9 + t], None, stat[0:n, 24 + t:25 + t],
                        stat[0:n, 32 + t:33 + t])
                if t == 0:
                    dve.wait_ge(g_in, 16)
                V.scalar_tensor_tensor(out=x_rows[0:n, t, :], in0=x_rows[0:n, t, :], scalar=stat[0:n, 24 + t:25 + t],
                                       in1=g_rows[0:n, :], op0=ALU.mult, op1=ALU.mult).then_inc(x_scaled, 1)

            scale_rows(0)
            for t in range(NT + 1):
                if t < NT:
                    scale_rows(t + 1)
                if t == 1:
                    dve.wait_ge(hi_ready, 1)
                    lr_w = w_hi[0][:, :].rearrange("p (k c) -> p k c", k=KT)
                    V.tensor_tensor(lr_w[:, :, LR_LO:LR_LO + RANK],
                                    raw[0][:, :].rearrange("p (k c) -> p k c", k=KT)[:, :, 0:RANK],
                                    lr_w[:, :, 0:RANK].bitcast(F32), ALU.subtract).then_inc(lo_ready, 1)
                n = P if t < NT else TS
                for g in range(KT // G4):
                    dve.wait_ge(h_hi, t * (KT // G4) + g + 1)
                    hk = act_y[:, g * G4:(g + 1) * G4, :, t * P:t * P + n]
                    V.tensor_tensor(hk[:, :, 1, :],
                                    acc[g // 2][:, g % 2 * 512:g % 2 * 512 + G4 * n].rearrange("p (k t) -> p k t", k=G4),
                                    hk[:, :, 0, :].bitcast(F32), ALU.subtract).then_inc(h_lo, 1)
            subtract_lo(dve, 1, 1)
            dve.wait_ge(const_in, 16 * 7)
            V.tensor_copy(masks[:, :, :].rearrange("p l t -> p (l t)"),
                          mix_tile[:, :, :].rearrange("p a t -> p (a t)")[:, 0:NLEVEL * P])
            dve.wait_ge(cst_t, 1)
            V.tensor_copy(cvec[:, 0:NVEC], bank[:, 1, 256:256 + NVEC])
            V.tensor_copy(conv_state[:, :, :].rearrange("p k r -> p (k r)"), bank[:, 1, 0:KT * 2 * NS]
                          ).then_inc(cst_ready, 1)
            SELF0 = count[0]
            dve.wait_ge(act_freed, ACT0 + START)
            lr_p, lr_s = lr_t[:, 0:TP].rearrange("p (c t) -> p c t", c=NT), lr_t[:, TP:T]
            V.tensor_tensor(lr_p, lr_p, lr_parts(1)[0], ALU.add)
            V.tensor_tensor(lr_s, lr_s, lr_parts(1)[1], ALU.add).then_inc(lr_sum, 1)

            SELF_PER = 65

            with dve.Fori(0, H) as i:
                count[0] = 0
                base[0] = i * SELF_PER + SELF0

                def level_diff(l):
                    B = LEVELS[l]
                    ins = None
                    for view, ok in ((prompt_blocks, True), (sample_blocks, 2 * B <= LS)):
                        if ok:
                            c = view(cum, 2 * B)
                            for kk in range(KK):
                                ref = c[:, kk, :, B - 1:B].to_broadcast(list(c[:, kk].shape))
                                ins = V.tensor_tensor(view(dec, 2 * B)[:, kk], c[:, kk], ref, ALU.subtract)
                    ins.then_inc(lvl_diff, 1)

                def level_mult(l):
                    B = LEVELS[l]
                    tt = T if 2 * B <= LS else TP
                    dve.wait_ge(lvl_exp, i * len(LEVELS) + (l + 1))
                    for half, src in ((0, 1), (1, 0)):
                        for kk in range(KK):
                            a = dec[:, kk, 0:tt].rearrange("p (c n) -> p c n", n=2 * B)[:, :, half * B:(half + 1) * B]
                            b = qk[:, src, kk, 0:tt].rearrange("p (c n) -> p c n", n=2 * B)[:, :, half * B:(half + 1) * B]
                            ins = V.tensor_tensor(a, a, b, ALU.mult)
                    ins.then_inc(lvl_ready, 1)

                for s, kind in enumerate(STEPS):
                    n = s - STEPS.index(kind)
                    par = par_of(s)
                    out = acc[par][:, A0:A0 + T]
                    if 9 <= s <= 16:
                        j = s - 9
                        if j:
                            dve.wait_ge(seq_mm, i * NS + j)
                        link(V.memset(q_seq[:, :, :].bitcast(F32), 0.0))
                        q_j = qe[:, :, TP + j * LS:TP + (j + 1) * LS]
                        link(V.tensor_copy(q_seq[:, :, j * LS:(j + 1) * LS], q_j))
                        V.tensor_tensor(q_seq[:, :, TS + j * LS:TS + (j + 1) * LS], q_j,
                                        q_seq[:, :, j * LS:(j + 1) * LS].bitcast(F32), ALU.subtract)
                        dve.wait_ge(state_hi, i * NS + (j + 1))
                        V.tensor_tensor(s_lo[:, :, :], states[:, j % 2, :, :], s_hi[:, :, :].bitcast(F32),
                                        ALU.subtract).then_inc(seq_split, 1)
                    subtract_lo(dve, i * NSTEP + (U_BODY + s + 1), par_of(s + 1))
                    if 5 <= s <= 8:
                        m = s - 5
                        dve.wait_ge(v_turned, i * VV + (m + 1))
                        two = bank[:, 2 * (m % 2):2 * (m % 2) + 2, :].rearrange("p b c -> p (b c)")
                        ins = V.tensor_copy(v_rows[:, :, m * P:(m + 1) * P],
                                            two[:, 0:(NT + 1) * P].rearrange("p (t c) -> p t c", c=P))
                        ins.then_inc(v_saved, 1)
                    if kind == "conv_x":
                        c = n // 4
                        if c == 0:
                            V.memset(u_tile[:, 0:2], 0.0)
                        us = u_tile[:, TP + 2:].rearrange("p (s l) -> p s l", s=NS)
                        V.tensor_copy(us[:, :, 0:2], conv_state[:, bass.ds(i * CH + c, 1), :]
                                      .rearrange("p k (s r) -> p (k s) r", r=2))
                        dve.wait_ge(act_freed, i * ACT_PER + (ACT0 + act_upto[s - 1]) + START)
                        dve.wait_ge(unit_done, i * NSTEP + (U_BODY + s + 1) + START)
                        V.tensor_tensor(u_tile[:, 2:TP + 2], mix_tile[:, 0, 0:TP], out[:, 0:TP], ALU.mult)
                        link(V.tensor_tensor(us[:, :, 2:], mix_tile[:, 0, TP:T].rearrange("p (s l) -> p s l", s=NS),
                                             out[:, TP:T].rearrange("p (s l) -> p s l", s=NS), ALU.mult))
                        V.tensor_copy(conv_tail[:, c, 0:2], u_tile[:, TP:TP + 2])
                        V.tensor_copy(conv_tail[:, c, 2:].rearrange("p (s r) -> p s r", r=2), us[:, :, LS:LS + 2]
                                      ).then_inc(tail_ready, 1)
                        cw = [cvec[:, bass.ds(i * CH + (cconv + j * KT + c), 1)] for j in range(3)]
                        y1 = mix_tile[:, 1, 0:TP]
                        y2 = mix_tile[:, 1, TP:T].rearrange("p (s l) -> p s l", s=NS)
                        V.tensor_scalar(y1, u_tile[:, 0:TP], cw[0], None, ALU.mult)
                        link(V.tensor_scalar(y2, us[:, :, 0:LS], cw[0], None, ALU.mult))
                        for j in (1, 2):
                            V.scalar_tensor_tensor(out=y1, in0=u_tile[:, j:TP + j], scalar=cw[j], in1=y1,
                                                   op0=ALU.mult, op1=ALU.add)
                            ins = V.scalar_tensor_tensor(out=y2, in0=us[:, :, j:LS + j], scalar=cw[j], in1=y2,
                                                         op0=ALU.mult, op1=ALU.add)
                            if j == 1:
                                link(ins)
                        ins.then_inc(dve_freed, 1)
                    if kind == "conv_b":
                        dve.wait_ge(dve_freed, i * DVE_PER + dve_upto[s - 1] + START)
                        dve.wait_ge(unit_done, i * NSTEP + (U_BODY + s + 1) + START)
                        V.tensor_tensor(mix_tile[:, 1, :], mix_tile[:, 1, :], out, ALU.mult).then_inc(dve_freed, 1)
                    if kind == "conv_g":
                        m = n // 4
                        dve.wait_ge(dve_freed, i * DVE_PER + dve_upto[s - 1] + START)
                        dve.wait_ge(cg_sig, i * 8 + (m + 1))
                        link(V.tensor_tensor(mix_tile[:, 0, :], mix_tile[:, 0, :], out, ALU.mult))
                        V.tensor_tensor(mix_tile[:, 1, :], mix_tile[:, 1, :], mix_tile[:, 0, :], ALU.mult
                                        ).then_inc(z_f32, 1)
                    if kind == "gla_gate":
                        m = 4 + n
                        dve.wait_ge(cg_sig, i * 8 + (m + 1))
                        link(V.scalar_tensor_tensor(out=mix_tile[:, 1, :], in0=out,
                                                    scalar=cvec[:, cgla + n:cgla + n + 1],
                                                    in1=mix_tile[:, 1, :], op0=ALU.mult, op1=ALU.mult))
                        V.tensor_tensor(mix_tile[:, 1, :], mix_tile[:, 1, :], o_t[:, n, :], ALU.mult
                                        ).then_inc(z_f32, 1)
                    if kind in ("conv_g", "gla_gate"):
                        dve.wait_ge(z_hi, i * 8 + (m + 1))
                        V.tensor_tensor(z_tile[:, 1, :], mix_tile[:, 1, :], z_tile[:, 0, :].bitcast(F32),
                                        ALU.subtract).then_inc(dve_freed, 1)

                    if s == 1:
                        dve.wait_ge(abs_done, i + 1)
                        for kk in range(KK):
                            ap = bank[:, 2 * kk:2 * kk + 2, :].rearrange("p b c -> p (b c)")[:, A0:A0 + T]
                            ins = V.tensor_scalar(cum[:, kk, :], ap, cvec[:, bass.ds(i * KK + (cbal + kk), 1)], 0.0,
                                                  ALU.add, ALU.min)
                        ins.then_inc(neg_part, 1)
                        dve.wait_ge(neg_part, i + 1)
                        dve.wait_ge(soft_part, i + 1)
                        link(V.tensor_tensor(dec[:, :, :], cum[:, :, :], dec[:, :, :], ALU.subtract))
                        for kk in range(KK):
                            ins = V.tensor_tensor_scan(cum[:, kk, :], reset[:, :], dec[:, kk, :], 0.0, ALU.mult, ALU.add)
                        ins.then_inc(cum_ready, 1)
                    if s == 2:
                        dve.wait_ge(eb_ready, i + 1)
                        V.tensor_tensor(qe[:, :, :], qe[:, :, :], qk[:, 0, :, :], ALU.mult).then_inc(qe_ready, 1)
                    if s == 3:
                        dve.wait_ge(cum_ready, i + 1)
                        for view, w in ((prompt_blocks, P), (sample_blocks, LS)):
                            for kk in range(KK):
                                c = view(cum, w)[:, kk]
                                ins = V.tensor_tensor(view(dec, w)[:, kk], c, c[:, :, w - 1:w].to_broadcast(list(c.shape)),
                                                      ALU.subtract)
                        ins.then_inc(kd_diff, 1)
                        dve.wait_ge(kd_exp, i + 1)
                        dve.wait_ge(act_freed, i * ACT_PER + ACT0 + 4 + START)
                        V.tensor_tensor(dec[:, :, :], dec[:, :, :], qk[:, 1, :, :], ALU.mult).then_inc(kd_ready, 1)
                    if s == 7:
                        V.memset(scores[:, :], 0.0)
                        dve.wait_ge(kd_turned, i + 1)
                        level_diff(0)
                        level_mult(0)
                        dve.wait_ge(kd_saved, i + 1)
                    if s == 8:
                        dve.wait_ge(v2_hi, i + 1)
                        for g in range(2):
                            own, _, by_lo, by_lo2 = row_blocks(g)
                            for rows in (by_lo, by_lo2):
                                ins = V.tensor_tensor(v2[rows, g, :], v_rows[own, NT, :], v2[own, g, :].bitcast(F32),
                                                      ALU.subtract)
                        ins.then_inc(v2_ready, 1)
                    if 9 <= s <= 16:
                        l = s - 9
                        wait_turn(dve, gram_done, i * NLEVEL + (l + 1))
                        w = P if l == len(LEVELS) else P // 2
                        for c in range(NT):
                            r = key_rows(l)
                            dst, m = queries(scores[0:r, c * P:(c + 1) * P], l), queries(masks[0:r, l, :], l)
                            src = bank[0:r, 3, c * w:(c + 1) * w]
                            if w < P:
                                src = src.rearrange("p (c n) -> p c n", n=LEVELS[l])
                            ins = V.copy_predicated(dst, m, src)
                        if l < len(LEVELS) and 2 * LEVELS[l] <= LS:
                            ins = V.copy_predicated(queries(scores[S0:P, TP:T], l), queries(masks[S0:P, l, S0:P], l),
                                                    bank[S0:P, 3, G_S:G_S + TS // 2]
                                                    .rearrange("p (c n) -> p c n", n=LEVELS[l]))
                        if l == len(LEVELS) - 1:
                            count[0] += 1
                            ins.then_inc(dve_self, 1)
                            wait_turn(dve, dve_self, base[0] + count[0])
                            ins = V.copy_predicated(scores[S0:P, TP:T], masks[S0:P, l + 1, S0:P],
                                                    bank[S0:P, 3, G_S + TS:G_S + 2 * TS])
                        ins.then_inc(lvl_merged, 1)
                        if l + 1 < len(LEVELS):
                            level_diff(l + 1)
                            level_mult(l + 1)
                        j = s - 9
                        dve.wait_ge(seq_mm, i * NS + (j + 1))
                        for kk in range(KK):
                            st = states[:, j % 2, kk, :]
                            ins = V.scalar_tensor_tensor(out=st, in0=st, scalar=decay_end[:, kk, NT + j:NT + j + 1],
                                                         in1=bank[:, kk, :], op0=ALU.mult, op1=ALU.add)
                        ins.then_inc(seq_upd, 1)
                    if s in SEQ_STEP:
                        j = SEQ_STEP.index(s)
                        own, under, _, under_lo = row_blocks(j // (NS // 2))
                        dve.wait_ge(kd_hi, i * NS + (j + 1))
                        for rows in (under, under_lo):
                            ins = V.scalar_tensor_tensor(out=kd_seq[rows, j % 2, :], in0=kd_rows[own, NT, :],
                                                         scalar=seq_sel[own, j:j + 1],
                                                         in1=kd_seq[own, j % 2, :].bitcast(F32),
                                                         op0=ALU.mult, op1=ALU.subtract)
                        ins.then_inc(seq_kd, 1)
                    if 17 <= s <= 17 + NT:
                        c = s - 17
                        dve.wait_ge(chunk_mm, i * (NT + 1) + (c + 1))
                        if c < NT:
                            for kk in range(KK):
                                st = s_prompt[:, kk, :]
                                if c == 0:
                                    ins = V.tensor_copy(st, bank[:, kk, :])
                                else:
                                    ins = V.scalar_tensor_tensor(out=st, in0=st, scalar=decay_end[:, kk, c:c + 1],
                                                                 in1=bank[:, kk, :], op0=ALU.mult, op1=ALU.add)
                            ins.then_inc(chunk_state, 1)
                            w = P
                            sq = dec[:, 0, 0:VV * P].rearrange("p (v t) -> p v t", v=VV)
                            dve.wait_ge(chunk_sq, i * NT + (c + 1))
                        else:
                            w = TS
                            o_s = o_t[:, :, TP:T]
                            link(V.tensor_copy(o_s, bank[:, 2, 0:VV * TS].rearrange("p (v t) -> p v t", v=VV)))
                            sq = dec[:, 0, 0:VV * TS].rearrange("p (v t) -> p v t", v=VV)
                            link(V.tensor_tensor(sq, o_s, o_s, ALU.mult))
                        if c:
                            dve.wait_ge(reps_set, i * (NT + 1) + c)
                            norm = c - 1
                            refined(rstd[:, :], bank[:, 3, 0:P], eps[:, :], rstd[:, :], nsq[:, :])
                            for v in range(VV):
                                ov = o_t[:, v, norm * P:(norm + 1) * P]
                                ins = V.tensor_tensor(ov, ov, rstd[:, :], ALU.mult)
                            ins.then_inc(o_ready, 1)
                        V.tensor_reduce(ssq[:, 0:w], sq.rearrange("p v t -> p t v"), AX_X, ALU.add).then_inc(ssq_ready, 1)
                    if s == 18 + NT:
                        dve.wait_ge(reps_set, i * (NT + 1) + (NT + 1))
                        refined(rstd[:, 0:TS], bank[:, 3, 0:TS], eps[:, :], rstd[:, 0:TS], nsq[:, 0:TS])
                        for v in range(VV):
                            ov = o_t[:, v, TP:T]
                            ins = V.tensor_tensor(ov, ov, rstd[:, 0:TS], ALU.mult)
                        ins.then_inc(o_ready, 1)
                        dve.wait_ge(o_ready, i * (NT + 1) + (NT + 1))
                dve.wait_ge(sp_out, i * 16 + 16)
                assert count[0] == SELF_PER, count[0]

            with dve.Fori(0, KT // 2) as i:
                for n in range(2):
                    u1 = U_A + n + 1
                    subtract_lo(dve, i * 2 + u1, u1 % 2)
                    dve.wait_ge(unit_done, i * 2 + u1 + START)
                    dve.wait_ge(gate_in[n], i * 16 + 16)
                    V.tensor_tensor(mix_tile[:, n, :], gate_tile[:, n, :], acc[(U_A + n) % 2][:, A0:A0 + T], ALU.mult
                                    ).then_inc(dve_freed, 1)
            with dve.Fori(0, KT // 2) as i:
                for n in range(2):
                    u1 = U_B + n + 1
                    subtract_lo(dve, i * 2 + u1, u1 % 2)
                    dve.wait_ge(unit_done, i * 2 + u1 + START)
                    dve.wait_ge(gate_in[n], i * 16 + (KT // 2 + 1) * 16)
                    dve.wait_ge(ma_in[n], i * 16 + 16)
                    g = gate_tile[:, n, :]
                    V.tensor_tensor(g, g, acc[(U_B + n) % 2][:, A0:A0 + T], ALU.mult).then_inc(dve_freed, 1)
                    dve.wait_ge(dve_freed, i * 2 + (H * DVE_PER + KT + n + 1) + START)
                    V.tensor_tensor(g, g, mix_tile[:, n, :], ALU.add).then_inc(mix_sum, 1)
                    dve.wait_ge(mix_hi, i * 2 + (n + 1))
                    xk = act_x[:, bass.ds(i * 2 + n, 1), :, :].rearrange("p k h t -> p (k h) t")
                    V.tensor_tensor(xk[:, 1, :], g, xk[:, 0, :].bitcast(F32), ALU.subtract).then_inc(mix_lo, 1)

            def add_turned(m, n):
                dve.wait_ge(out_turned, m + 1)
                two = bank[:, 2 * n:2 * n + 2, :].rearrange("p b c -> p (b c)")
                dst = resid[:, :, bass.ds(m * P, P)]
                V.tensor_tensor(dst, dst, two[:, 0:(NT + 1) * P].rearrange("p (t c) -> p t c", c=P), ALU.add
                                ).then_inc(out_sum, 1)

            def weight(m):
                dve.wait_ge(squared, m + 1)
                dst = resid[:, :, bass.ds(m * P, P)]
                g = gfin[:, bass.ds(m * P, P)].rearrange("p (o c) -> p o c", o=1).to_broadcast([P, NT + 1, P])
                V.tensor_tensor(dst, dst, g, ALU.mult).then_inc(weighted, 1)

            def out_tiles(i, first, last):
                for n in range(2):
                    u1 = U_O + n + 1
                    if not (last and n == 1):
                        subtract_lo(dve, i * 2 + u1, u1 % 2)
                    if first and n == 1:
                        dve.wait_ge(resid_in, 16 * (NT + 3))
                    if not (first and n == 0):
                        add_turned(i * 2 + (n - 1), 1 - n)
                    if not first:
                        weight(i * 2 + (n - 2))

            out_tiles(0, True, False)
            with dve.Fori(1, KT // 2 - 1) as i:
                out_tiles(i, False, False)
            out_tiles(KT // 2 - 1, False, True)
            add_turned(KT - 1, 1)
            weight(KT - 2)
            base[0], count[0] = SELF0 + H * SELF_PER, 0
            dve.wait_ge(squared, KT)
            link(V.tensor_reduce(stat[:, 0:NT + 1], parts[:, :].rearrange("p (m t) -> p t m", t=NT + 1), AX_X, ALU.add))
            V.tensor_scalar(stat[:, 8:8 + NT + 1], stat[:, 0:NT + 1], 1.0 / D, EPS, ALU.mult, ALU.add
                            ).then_inc(mean_sq, 1)
            weight(KT - 1)
            dve.wait_ge(rms_out, 1)
            refined(stat[:, 16:16 + NT + 1], stat[:, 8:8 + NT + 1], None, stat[:, 24:24 + NT + 1],
                    stat[:, 32:32 + NT + 1])
            dve.sem_inc(y_rstd, 1)
            dve.wait_ge(weighted, KT)
            for t in SCALED_BY_DVE:
                V.tensor_scalar(resid[:, t, :], resid[:, t, :], stat[:, 24 + t:25 + t], None, ALU.mult
                                ).then_inc(y_dve, 1)


_INS = ["x_prompt", "x_sample", "state_conv", "state_gla", "norm_g", "w_in", "conv_w", "w_alpha2", "b_alpha",
        "gla_norm_g", "w_branch_a", "w_branch_b", "w_out", "final_norm_g"]


def _constants(tp, ns, ls):
    import numpy as np
    t = np.arange(P)
    tokens = np.arange(tp + ns * ls)
    start = np.where(tokens < tp, tokens % P == 0, (tokens - tp) % ls == 0)
    reset = np.broadcast_to(1.0 - start, (P, tokens.size))
    rows = t - (P - ns * ls)
    sel = (rows[:, None] // ls == np.arange(ns)[None, :]) & (rows[:, None] >= 0)
    m = []
    s, q = t[:, None], t[None, :]
    for b in LEVELS:
        m.append((s // (2 * b) == q // (2 * b)) & (s % (2 * b) < b) & (q % (2 * b) >= b))
    m.append(s == q)
    return np.concatenate([np.eye(P), reset, sel] + m, axis=1).astype(np.float32)


def kernel(**inputs):
    import numpy as _np
    import concourse.bacc as _bacc
    from concourse import mybir as _mybir
    from concourse.bass_utils import run_bass_kernel_spmd as _run

    nc = _bacc.Bacc("TRN2", target_bir_lowering=False, num_devices=1)
    arrays, args = {}, []
    for name in _INS:
        a = _np.ascontiguousarray(inputs[name])
        arrays[f"in_{name}"] = a
        args.append(nc.dram_tensor(f"in_{name}", a.shape, _mybir.dt.from_np(a.dtype), kind="ExternalInput").ap())
    b, tp, d = inputs["x_prompt"].shape
    ns, ls, _ = inputs["x_sample"].shape
    a = _constants(tp, ns, ls)
    arrays["in_const_f32"] = a
    args.append(nc.dram_tensor("in_const_f32", a.shape, _mybir.dt.float32, kind="ExternalInput").ap())
    depth, _, r, _ = inputs["state_conv"].shape
    gla = inputs["state_gla"].shape
    outs = [(b, tp, d), (ns, ls, d), (depth, b, r, d), (depth, b) + tuple(gla[2:]), (depth, ns, r, d), tuple(gla)]
    for n, shape in enumerate(outs):
        args.append(nc.dram_tensor(f"out_{n}", shape, _mybir.dt.float32, kind="ExternalOutput").ap())
    hybrid_kernel(nc, *args)
    res = _run(nc, [arrays], core_ids=[0])
    return tuple(res.results[0][f"out_{n}"] for n in range(len(outs)))
```
